# Optimizing a Trainium2 kernel written in Bass

```python
import math
import jax, jax.numpy as jnp
from jax import lax
import numpy as np

D_MODEL = 1024
BATCH = 1
SEQ = 512
DEPTH = 2
DEC_BATCH = 8
DEC_SEQ = 1
PAST_LEN = 1024
PAGE_SIZE = 128

N_EVEN = (DEPTH + 1) // 2
N_ODD = DEPTH // 2
D_FF = 2816
EPS = 1e-6
CONV_CH = D_MODEL // 2
CONV_W = 31
SB_HEADS = 8
SB_HEAD_DIM = (D_MODEL // 2) // SB_HEADS
SB_QBLOCK = 128
SB_BIAS_INIT = -8.0
M_D_INNER = 2 * D_MODEL
M_HEAD_DIM = 64
M_HEADS = M_D_INNER // M_HEAD_DIM
M_GROUPS = 4
M_HPG = M_HEADS // M_GROUPS
M_D_STATE = 128
M_CONV_W = 4
M_CONV_DIM = M_D_INNER + 2 * M_GROUPS * M_D_STATE
M_CHUNK = 128
M_IN = M_D_INNER + M_CONV_DIM + M_HEADS
AB_IN = 2 * CONV_CH + 3 * SB_HEADS * SB_HEAD_DIM
AB_MIX = CONV_CH + SB_HEADS * SB_HEAD_DIM

kernel_name = 'stickbreak_conformer_mamba2_hybrid_step'

F32 = jnp.float32

def rmsnorm(x, w):
    xf = x.astype(F32)
    y = xf * lax.rsqrt(jnp.mean(xf * xf, axis=-1, keepdims=True) + EPS)
    return (y * w.astype(F32)).astype(x.dtype)

def swiglu_ffn(x, norm_w, w_gate, w_up, w_down):
    h = rmsnorm(x, norm_w)
    return (jax.nn.silu(h @ w_gate) * (h @ w_up)) @ w_down

def causal_dwconv(u, prev, w, b):
    up = jnp.concatenate([prev.astype(u.dtype), u], axis=1)
    out = lax.conv_general_dilated(up, w.astype(u.dtype)[:, None, :], window_strides=(1,), padding='VALID',
                                   dimension_numbers=('NWC', 'WIO', 'NWC'), feature_group_count=u.shape[-1])
    new_state = up[:, up.shape[1] - (w.shape[0] - 1):]
    return out + b.astype(u.dtype), new_state

def sb_block(q, k, v, q_pos, k_pos, bias):
    z = jnp.einsum('bqhd,bkhd->bhqk', q.astype(F32), k.astype(F32)) * (SB_HEAD_DIM ** -0.5)
    z = z + bias.astype(F32)[None, :, None, None]
    mask = k_pos[None, :] < q_pos[:, None]
    lb = jnp.where(mask, jax.nn.log_sigmoid(-z), 0.0)
    rev = lax.cumsum(lb, axis=3, reverse=True)
    after = jnp.concatenate([rev[..., 1:], jnp.zeros_like(rev[..., :1])], axis=-1)
    wgt = jnp.where(mask, jnp.exp(jax.nn.log_sigmoid(z) + after), 0.0)
    return jnp.einsum('bhqk,bkhd->bqhd', wgt, v.astype(F32)).astype(v.dtype)

def sb_attention(q, k, v, q_offset, bias):
    b, tq = q.shape[0], q.shape[1]
    k_pos = jnp.arange(k.shape[1], dtype=jnp.int32)
    if tq % SB_QBLOCK != 0 or tq <= SB_QBLOCK:
        q_pos = q_offset + jnp.arange(tq, dtype=jnp.int32)
        return sb_block(q, k, v, q_pos, k_pos, bias)
    nb = tq // SB_QBLOCK

    def one_block(i):
        start = i * SB_QBLOCK
        qb = lax.dynamic_slice_in_dim(q, start, SB_QBLOCK, axis=1)
        q_pos = q_offset + start + jnp.arange(SB_QBLOCK, dtype=jnp.int32)
        return sb_block(qb, k, v, q_pos, k_pos, bias)

    out = lax.map(one_block, jnp.arange(nb, dtype=jnp.int32))
    return jnp.moveaxis(out, 0, 1).reshape(b, tq, SB_HEADS, SB_HEAD_DIM)

def conv_attn_mixer(h, conv_prev, k_past, v_past, q_offset, w_in, conv_w, conv_b, ln_g, ln_b, sb_bias, w_out):
    b, t, _ = h.shape
    proj = h @ w_in
    hd = SB_HEADS * SB_HEAD_DIM
    glu_a = proj[..., :CONV_CH]
    glu_g = proj[..., CONV_CH:2 * CONV_CH]
    q = proj[..., 2 * CONV_CH:2 * CONV_CH + hd].reshape(b, t, SB_HEADS, SB_HEAD_DIM)
    k = proj[..., 2 * CONV_CH + hd:2 * CONV_CH + 2 * hd].reshape(b, t, SB_HEADS, SB_HEAD_DIM)
    v = proj[..., 2 * CONV_CH + 2 * hd:].reshape(b, t, SB_HEADS, SB_HEAD_DIM)
    u = glu_a * jax.nn.sigmoid(glu_g)
    c, conv_new = causal_dwconv(u, conv_prev, conv_w, conv_b)
    cf = c.astype(F32)
    mu = jnp.mean(cf, axis=-1, keepdims=True)
    var = jnp.mean(jnp.square(cf - mu), axis=-1, keepdims=True)
    cn = (cf - mu) * lax.rsqrt(var + EPS) * ln_g.astype(F32) + ln_b.astype(F32)
    a_out = jax.nn.silu(cn).astype(h.dtype)
    if k_past is None:
        k_all, v_all = k, v
    else:
        k_all = jnp.concatenate([k_past.astype(k.dtype), k], axis=1)
        v_all = jnp.concatenate([v_past.astype(v.dtype), v], axis=1)
    o = sb_attention(q, k_all, v_all, q_offset, sb_bias).reshape(b, t, hd)
    mixed = jnp.concatenate([a_out, o], axis=-1)
    return mixed @ w_out, conv_new, k, v

def ssd_scan(x, dt, a, bmat, cmat, h0, chunk):
    b, t, g, hg, p = x.shape
    n = bmat.shape[-1]
    nc = t // chunk
    xf = x.astype(F32).reshape(b, nc, chunk, g, hg, p)
    dtc = dt.reshape(b, nc, chunk, g, hg)
    bf = bmat.astype(F32).reshape(b, nc, chunk, g, n)
    cf = cmat.astype(F32).reshape(b, nc, chunk, g, n)
    a_cs = jnp.cumsum(dtc * a, axis=2)
    dtx = xf * dtc[..., None]
    cb = jnp.einsum('bclgn,bcsgn->bcgls', cf, bf)
    acs = jnp.moveaxis(a_cs, 2, -1)
    causal = jnp.tril(jnp.ones((chunk, chunk), dtype=bool))
    decay = jnp.exp(jnp.where(causal, acs[..., :, None] - acs[..., None, :], -jnp.inf))
    y_diag = jnp.einsum('bcghls,bcsghp->bclghp', cb[:, :, :, None] * decay, dtx)
    dtx_end = dtx * jnp.exp(a_cs[:, :, -1:] - a_cs)[..., None]
    s_chunk = jnp.einsum('bcsgn,bcsghp->bcghpn', bf, dtx_end)
    a_tot = a_cs[:, :, -1]

    def step(hc, inp):
        at, sc = inp
        return jnp.exp(at)[..., None, None] * hc + sc, hc

    h_last, h_prev = lax.scan(step, h0.astype(F32), (jnp.moveaxis(a_tot, 1, 0), jnp.moveaxis(s_chunk, 1, 0)))
    h_prev = jnp.moveaxis(h_prev, 0, 1)
    y_off = jnp.einsum('bclgn,bcghpn->bclghp', cf, h_prev) * jnp.exp(a_cs)[..., None]
    return (y_diag + y_off).reshape(b, t, g, hg, p), h_last

def mamba2_mixer(h, conv_prev, ssm_prev, w_in, conv_w, conv_b, dt_bias, a_log, d_skip, norm_w, w_out):
    b, t, _ = h.shape
    proj = h @ w_in
    z = proj[..., :M_D_INNER]
    xbc = proj[..., M_D_INNER:M_D_INNER + M_CONV_DIM]
    dt_raw = proj[..., M_D_INNER + M_CONV_DIM:]
    xbc, conv_new = causal_dwconv(xbc, conv_prev, conv_w, conv_b)
    xbc = jax.nn.silu(xbc)
    gn = M_GROUPS * M_D_STATE
    x = xbc[..., :M_D_INNER].reshape(b, t, M_GROUPS, M_HPG, M_HEAD_DIM)
    bmat = xbc[..., M_D_INNER:M_D_INNER + gn].reshape(b, t, M_GROUPS, M_D_STATE)
    cmat = xbc[..., M_D_INNER + gn:].reshape(b, t, M_GROUPS, M_D_STATE)
    dt = jax.nn.softplus(dt_raw.astype(F32) + dt_bias.astype(F32)).reshape(b, t, M_GROUPS, M_HPG)
    a = -jnp.exp(a_log.astype(F32)).reshape(M_GROUPS, M_HPG)
    chunk = M_CHUNK if t % M_CHUNK == 0 else t
    h0 = ssm_prev.astype(F32).reshape(b, M_GROUPS, M_HPG, M_HEAD_DIM, M_D_STATE)
    y, h_last = ssd_scan(x, dt, a, bmat, cmat, h0, chunk)
    y = y + d_skip.astype(F32).reshape(M_GROUPS, M_HPG)[:, :, None] * x.astype(F32)
    y = y.reshape(b, t, M_D_INNER) * jax.nn.silu(z.astype(F32))
    yg = y.reshape(b, t, M_GROUPS, M_D_INNER // M_GROUPS)
    yg = yg * lax.rsqrt(jnp.mean(yg * yg, axis=-1, keepdims=True) + EPS)
    y = yg.reshape(b, t, M_D_INNER) * norm_w.astype(F32)
    out = y.astype(h.dtype) @ w_out
    return out, conv_new, h_last.reshape(b, M_HEADS, M_HEAD_DIM, M_D_STATE)

def setup_inputs(seed: int = 0) -> dict:
    key = jax.random.key(seed)
    ks = iter(jax.random.split(key, 48))

    def nrm(shape, scale):
        return jax.random.normal(next(ks), shape, F32) * scale

    n_pages = PAST_LEN // PAGE_SIZE
    n_used = DEC_BATCH * n_pages
    n_phys = n_used + n_used // 4
    perm = jax.random.permutation(next(ks), n_phys)
    page_table = perm[:n_used].reshape(DEC_BATCH, n_pages).astype(jnp.int32)

    dt0 = jnp.exp(jax.random.uniform(next(ks), (N_ODD, M_HEADS), F32, math.log(1e-3), math.log(1e-1)))
    dt_bias = dt0 + jnp.log(-jnp.expm1(-dt0))
    a_log = jnp.log(jax.random.uniform(next(ks), (N_ODD, M_HEADS), F32, 1.0, 16.0))

    return {
        'x_prompt': nrm((BATCH, SEQ, D_MODEL), 1.0),
        'x_sample': nrm((DEC_BATCH, DEC_SEQ, D_MODEL), 1.0),
        'cache_sb_k': nrm((N_EVEN, n_phys, PAGE_SIZE, SB_HEADS, SB_HEAD_DIM), 1.0),
        'cache_sb_v': nrm((N_EVEN, n_phys, PAGE_SIZE, SB_HEADS, SB_HEAD_DIM), 1.0),
        'state_conv_a': nrm((N_EVEN, DEC_BATCH, CONV_W - 1, CONV_CH), 0.5),
        'state_mamba_conv': nrm((N_ODD, DEC_BATCH, M_CONV_W - 1, M_CONV_DIM), 1.0),
        'state_ssm': nrm((N_ODD, DEC_BATCH, M_HEADS, M_HEAD_DIM, M_D_STATE), 0.1),
        'page_table': page_table,
        'ffn1_norm': 1.0 + nrm((DEPTH, D_MODEL), 0.02),
        'ffn1_gate': nrm((DEPTH, D_MODEL, D_FF), D_MODEL ** -0.5),
        'ffn1_up': nrm((DEPTH, D_MODEL, D_FF), D_MODEL ** -0.5),
        'ffn1_down': nrm((DEPTH, D_FF, D_MODEL), D_FF ** -0.5),
        'mix_norm': 1.0 + nrm((DEPTH, D_MODEL), 0.02),
        'ffn2_norm': 1.0 + nrm((DEPTH, D_MODEL), 0.02),
        'ffn2_gate': nrm((DEPTH, D_MODEL, D_FF), D_MODEL ** -0.5),
        'ffn2_up': nrm((DEPTH, D_MODEL, D_FF), D_MODEL ** -0.5),
        'ffn2_down': nrm((DEPTH, D_FF, D_MODEL), D_FF ** -0.5),
        'final_norm': 1.0 + nrm((D_MODEL,), 0.02),
        'ab_in_proj': nrm((N_EVEN, D_MODEL, AB_IN), D_MODEL ** -0.5),
        'conv_a_w': nrm((N_EVEN, CONV_W, CONV_CH), CONV_W ** -0.5),
        'conv_a_b': nrm((N_EVEN, CONV_CH), 0.02),
        'conv_a_ln_g': 1.0 + nrm((N_EVEN, CONV_CH), 0.02),
        'conv_a_ln_b': nrm((N_EVEN, CONV_CH), 0.02),
        'sb_beta_bias': SB_BIAS_INIT + nrm((N_EVEN, SB_HEADS), 0.5),
        'ab_out_proj': nrm((N_EVEN, AB_MIX, D_MODEL), AB_MIX ** -0.5),
        'm_in_proj': nrm((N_ODD, D_MODEL, M_IN), D_MODEL ** -0.5),
        'm_conv_w': nrm((N_ODD, M_CONV_W, M_CONV_DIM), M_CONV_W ** -0.5),
        'm_conv_b': nrm((N_ODD, M_CONV_DIM), 0.02),
        'm_dt_bias': dt_bias,
        'm_A_log': a_log,
        'm_D': 1.0 + nrm((N_ODD, M_HEADS), 0.1),
        'm_norm': 1.0 + nrm((N_ODD, M_D_INNER), 0.02),
        'm_out_proj': nrm((N_ODD, M_D_INNER, D_MODEL), M_D_INNER ** -0.5),
    }

def reference(x_prompt, x_sample, cache_sb_k, cache_sb_v, state_conv_a, state_mamba_conv, state_ssm, page_table,
              ffn1_norm, ffn1_gate, ffn1_up, ffn1_down, mix_norm, ffn2_norm, ffn2_gate, ffn2_up, ffn2_down,
              final_norm, ab_in_proj, conv_a_w, conv_a_b, conv_a_ln_g, conv_a_ln_b, sb_beta_bias, ab_out_proj,
              m_in_proj, m_conv_w, m_conv_b, m_dt_bias, m_A_log, m_D, m_norm, m_out_proj):
    dec_b, n_pages = page_table.shape
    past_len = n_pages * cache_sb_k.shape[2]
    bp = x_prompt.shape[0]
    xp, xs = x_prompt, x_sample
    kp_l, vp_l, cap_l, mcp_l, ssp_l = [], [], [], [], []
    ks_l, vs_l, cas_l, mcs_l, sss_l = [], [], [], [], []
    for layer in range(DEPTH):
        f1 = (ffn1_norm[layer], ffn1_gate[layer], ffn1_up[layer], ffn1_down[layer])
        xp = xp + 0.5 * swiglu_ffn(xp, *f1)
        xs = xs + 0.5 * swiglu_ffn(xs, *f1)
        hp = rmsnorm(xp, mix_norm[layer])
        hs = rmsnorm(xs, mix_norm[layer])
        if layer % 2 == 0:
            e = layer // 2
            wa = (ab_in_proj[e], conv_a_w[e], conv_a_b[e], conv_a_ln_g[e], conv_a_ln_b[e], sb_beta_bias[e],
                  ab_out_proj[e])
            conv0 = jnp.zeros((bp, CONV_W - 1, CONV_CH), xp.dtype)
            mp, cvp, kp, vp = conv_attn_mixer(hp, conv0, None, None, 0, *wa)
            k_past = cache_sb_k[e][page_table].reshape(dec_b, past_len, SB_HEADS, SB_HEAD_DIM)
            v_past = cache_sb_v[e][page_table].reshape(dec_b, past_len, SB_HEADS, SB_HEAD_DIM)
            ms, cvs, ks_new, vs_new = conv_attn_mixer(hs, state_conv_a[e], k_past, v_past, past_len, *wa)
            kp_l.append(kp); vp_l.append(vp); cap_l.append(cvp)
            ks_l.append(ks_new); vs_l.append(vs_new); cas_l.append(cvs)
        else:
            o = layer // 2
            wm = (m_in_proj[o], m_conv_w[o], m_conv_b[o], m_dt_bias[o], m_A_log[o], m_D[o], m_norm[o], m_out_proj[o])
            mconv0 = jnp.zeros((bp, M_CONV_W - 1, M_CONV_DIM), xp.dtype)
            ssm0 = jnp.zeros((bp, M_HEADS, M_HEAD_DIM, M_D_STATE), F32)
            mp, mcp, ssp = mamba2_mixer(hp, mconv0, ssm0, *wm)
            ms, mcs, sss = mamba2_mixer(hs, state_mamba_conv[o], state_ssm[o], *wm)
            mcp_l.append(mcp); ssp_l.append(ssp)
            mcs_l.append(mcs); sss_l.append(sss)
        xp = xp + mp
        xs = xs + ms
        f2 = (ffn2_norm[layer], ffn2_gate[layer], ffn2_up[layer], ffn2_down[layer])
        xp = xp + 0.5 * swiglu_ffn(xp, *f2)
        xs = xs + 0.5 * swiglu_ffn(xs, *f2)
    y_prompt = rmsnorm(xp, final_norm)
    y_sample = rmsnorm(xs, final_norm)
    return (y_prompt, y_sample,
            jnp.stack(kp_l), jnp.stack(vp_l), jnp.stack(cap_l), jnp.stack(mcp_l), jnp.stack(ssp_l),
            jnp.stack(ks_l), jnp.stack(vs_l), jnp.stack(cas_l), jnp.stack(mcs_l), jnp.stack(sss_l))


_drawn_inputs = setup_inputs


def setup_inputs(seed=0):
    import zlib

    import numpy as np

    out = dict(_drawn_inputs(seed))
    spreads = {}
    factors = {'cache_sb_k': 29.008,
     'cache_sb_v': 23.456,
     'ffn1_norm': 3.174,
     'ffn2_norm': 4.107,
     'final_norm': 8.009,
     'conv_a_ln_g': 3.659,
     'conv_a_ln_b': 4.076,
     'sb_beta_bias': 24.416,
     'm_norm': 22.207}
    for name, (base, spread) in spreads.items():
        noise = np.random.default_rng([zlib.crc32(name.encode()), seed]).standard_normal(out[name].shape)
        drawn = base * np.exp(spread * noise) if base else spread * noise
        out[name] = __import__('jax').numpy.asarray(drawn.astype(out[name].dtype))
    for name, factor in factors.items():
        out[name] = (out[name] * factor).astype(out[name].dtype)
    return out
```

```python
from contextlib import ExitStack

import concourse.bass as bass
from concourse import mybir

F32 = mybir.dt.float32
F32R = mybir.dt.float32r
I32 = mybir.dt.int32
ALU = mybir.AluOpType
ACT = mybir.ActivationFunctionType
AX = mybir.AxisListType

P = 128


class Chain:

    def __init__(self, eng, sem):
        self.eng, self.sem, self.n = eng, sem, 0

    def __call__(self, ins):
        ins.then_inc(self.sem, 1)
        self.n += 1
        self.eng.wait_ge(self.sem, self.n)


def bass_trunk(nc, d, o):
    _, T, DM = d["x_prompt"].shape
    B = d["x_sample"].shape[0]
    NT = T + B
    H2 = NT // 2
    KB = DM // P
    DFF = d["ffn1_gate"].shape[2]
    NF = DFF // P
    FA = (NF // 2 + 1) // 2 * 2
    FPARTS = [(0, FA), (FA, NF - FA)]
    NTT = T // P
    CCH = d["conv_a_w"].shape[2]
    CW = d["conv_a_w"].shape[1]
    CB = CCH // P
    _, NPHYS, PAGE, NH, DH = d["cache_sb_k"].shape
    HD = NH * DH
    NPG = d["page_table"].shape[1]
    MH = d["m_A_log"].shape[1]
    MDI = d["m_norm"].shape[1]
    MP, MN = d["state_ssm"].shape[3:]
    MCW, MCD = d["m_conv_w"].shape[1:]
    MG = (MCD - MDI) // (2 * MN)
    HPG = MH // MG
    GB = MDI // MG // P
    EPS = 1e-6
    assert PAGE == P and MN == P and HD == CCH == 4 * P and GB == 4 and MP == DH == 64 and KB == 8 and H2 % 2 == 0

    NS_FFN = NF + 2 * KB
    NS_A = 10 + 4
    NS_M = 1 + MG * 7
    N_F = [2 * 0, NS_FFN + NS_A, 2 * NS_FFN + NS_A, 3 * NS_FFN + NS_A + NS_M]
    N_A = NS_FFN
    N_M = 3 * NS_FFN + NS_A
    N_END = 4 * NS_FFN + NS_A + NS_M
    FFN_W = [("ffn1", 0), ("ffn2", 0), ("ffn1", 1), ("ffn2", 1)]

    with ExitStack() as top:
        def sb_in(stack, name, shape, dt=F32):
            return stack.enter_context(nc.sbuf_tensor(name, shape, dt))

        def sb(name, shape, dt=F32):
            return sb_in(top, name, shape, dt)

        def sem(name):
            return top.enter_context(nc.semaphore(name))

        xT = sb("xT", [P, KB, NT])
        hh = sb("hh", [P, KB, NT], F32R)
        hl = sb("hl", [P, KB, NT], F32R)
        raw = sb("raw", [P, 2, 2048])
        wh = sb("wh", [P, 2, 2048], F32R)
        wl = sb("wl", [P, 2, 2048], F32R)
        ident = sb("ident", [P, P])
        ones = sb("ones", [P, P])
        mean_d = sb("mean_d", [P, P])
        mean_c = sb("mean_c", [P, P])
        epst = sb("epst", [P, 1])
        NV1 = 7 * KB + 3 * CB + MCD // P + MDI // P
        vec = sb("vec", [P, NV1])
        cwv = sb("cwv", [P, CW * CB])
        mwv = sb("mwv", [P, MCW * MCD // P])
        V_NORM = {("ffn1", 0): 0, ("ffn1", 1): KB, ("mix", 0): 2 * KB, ("mix", 1): 3 * KB,
                  ("ffn2", 0): 4 * KB, ("ffn2", 1): 5 * KB, ("final", 0): 6 * KB}
        V_CB, V_LG, V_LB = 7 * KB, 7 * KB + CB, 7 * KB + 2 * CB
        V_MB = 7 * KB + 3 * CB
        V_MN = V_MB + MCD // P
        PS = top.enter_context(nc.psum_tensor("PS", [P, 8, 512], F32))

        landed = [sem("landed0"), sem("landed1")]
        w_hi = sem("w_hi")
        w_ready = sem("w_ready")
        w_used = sem("w_used")
        stored = sem("stored")
        n_stores = [0]

        def raw_view(p, nk, cols, off=0):
            return raw[:, p, off:off + nk * cols].rearrange("p (k c) -> p k c", k=nk)

        def kview(ap):
            return ap.rearrange("(k p) c -> p k c", p=P)

        def slot_parts(n):
            p = n % 2
            for f in range(4):
                if N_F[f] <= n < N_F[f] + NS_FFN:
                    return ffn_parts(f, n - N_F[f], p)
            if N_A <= n < N_A + NS_A:
                i = n - N_A
                W = d["ab_in_proj"][0]
                if i < 4:
                    cols = [CCH + i * P, i * P]
                elif i < 10:
                    cols = [2 * CCH + (i - 4) * 2 * P, 2 * CCH + (i - 4) * 2 * P + P]
                else:
                    W = d["ab_out_proj"][0]
                    cols = [(i - 10) * 2 * P, (i - 10) * 2 * P + P]
                return [(raw_view(p, KB, P, j * KB * P), kview(W[:, c:c + P])) for j, c in enumerate(cols)]
            i = n - N_M
            W = d["m_in_proj"][0]
            if i == 0:
                c, hk = MDI + MCD, KB // 2
                return [(raw_view(p, hk, MH, j * hk * MH), kview(W[j * hk * P:(j + 1) * hk * P, c:c + MH]))
                        for j in range(2)]
            g, i = divmod(i - 1, 7)
            if i < 5:
                cols = [blk_col(g, 2 * i), blk_col(g, 2 * i + 1)]
                return [(raw_view(p, KB, P, j * KB * P), kview(W[:, c:c + P])) for j, c in enumerate(cols)]
            W = d["m_out_proj"][0][g * GB * P:(g + 1) * GB * P, (i - 5) * 4 * P:(i - 4) * 4 * P]
            return [(raw_view(p, 2, 4 * P, j * 2 * 4 * P), kview(W[j * 2 * P:(j + 1) * 2 * P, :])) for j in range(2)]

        def blk_col(g, i):
            if i < 4:
                return (g * GB + i) * P
            if i < 8:
                return MDI + (g * GB + i - 4) * P
            return MDI + MDI + (g + (i - 8) * MG) * P

        def ffn_parts(f, i, p):
            if i < FA:
                return ffn_f(f, i, p)
            if i < FA + KB:
                return ffn_d(f, 0, i - FA, p)
            if i < NF + KB:
                return ffn_f(f, i - KB, p)
            return ffn_d(f, 1, i - NF - KB, p)

        def ffn_f(f, F, p):
            w, l = FFN_W[f]
            return [(raw_view(p, KB, P), kview(d[w + "_gate"][l])[:, :, bass.ds(F * P, P)]),
                    (raw_view(p, KB, P, KB * P), kview(d[w + "_up"][l])[:, :, bass.ds(F * P, P)])]

        def ffn_d(f, part, j, p):
            w, l = FFN_W[f]
            f0, nf = FPARTS[part]
            src = kview(d[w + "_down"][l])
            hk = nf // 2
            return [(raw_view(p, hk, P, q * hk * P), src[:, f0 + q * hk:f0 + (q + 1) * hk, bass.ds(j * P, P)])
                    for q in range(2)]

        def load(sp, n, parts, p):
            sp.wait_ge(w_ready, n + 1)
            for dst, src in parts:
                sp.dma_start(dst, src).then_inc(landed[p], 16)

        def load_static(sp, n):
            if n < N_END:
                load(sp, n, slot_parts(n), n % 2)

        def split_hi(act, n, p, half, cols=2048):
            act.wait_ge(landed[p], 32 * half + 32)
            act.wait_ge(w_used, n + 1)
            act.activation(wh[:, p, 0:cols], raw[:, p, 0:cols], ACT.Copy).then_inc(w_hi, 1)

        def split_lo(dve, n, p, cols=2048):
            dve.wait_ge(w_hi, n + 1)
            dve.tensor_tensor(wl[:, p, 0:cols], raw[:, p, 0:cols], wh[:, p, 0:cols].bitcast(F32),
                              ALU.subtract).then_inc(w_ready, 1)

        def hi_static(act, n):
            if n < N_END:
                split_hi(act, n, n % 2, n // 2, slot_cols(n))

        def lo_static(dve, n):
            if n < N_END:
                split_lo(dve, n, n % 2, slot_cols(n))

        def slot_cols(n):
            return sum(a.shape[1] * a.shape[2] for a, _ in slot_parts(n))

        def mm3(pe, outs, w, k0, nk, rh, rl, first=True, last=True, step=P, m=P):
            ins = None
            for k in range(nk):
                c = w(k)
                for a, (x, y) in enumerate(((wh, rh), (wh, rl), (wl, rh))):
                    for half, out in enumerate(outs):
                        ins = pe.matmul(out, x[:, k0, c:c + m], y[:, k, half * H2:(half + 1) * H2],
                                        start=first and k == 0 and a == 0, stop=last and k == nk - 1 and a == 2)
            return ins

        def halves(ap):
            return ap.rearrange("p (h c) -> p h c", h=2)

        norm_sq = sem("norm_sq")
        norm_ms = sem("norm_ms")
        norm_sd = sem("norm_sd")
        norm_rs = sem("norm_rs")
        norm_hf = sem("norm_hf")
        norm_hi = sem("norm_hi")
        norm_lo = sem("norm_lo")

        class Norm:

            def __init__(self, i, stack):
                self.i = i
                self.hf = sb_in(stack, f"norm{i}_buf", [P, KB, NT])
                self.sd = sb_in(stack, f"norm{i}_sdev", [P, NT])
                self.rstd = sb_in(stack, f"norm{i}_rstd", [P, NT])

            def wait_split(self, eng):
                eng.wait_ge(norm_lo, (self.i + 1) * KB)

            def wait_normed(self, eng):
                eng.wait_ge(norm_hf, (self.i + 1) * KB)

            def act_squares(self, act):
                for k in range(KB):
                    act.activation(self.hf[:, k, :], xT[:, k, :], ACT.Square).then_inc(norm_sq, 1)

            def act_sd(self, act):
                act.wait_ge(norm_ms, self.i + 1)
                act.activation(halves(self.sd[:, :]), PS[:, 4:6, 0:H2], ACT.Sqrt, bias=epst[:, 0:1])\
                    .then_inc(norm_sd, 1)

            def act_hi(self, act):
                for k in range(KB):
                    act.wait_ge(norm_hf, self.i * KB + k + 1)
                    act.activation(hh[:, k, :], self.hf[:, k, :], ACT.Copy).then_inc(norm_hi, 1)

            def pe_mean(self, pe):
                for k in range(KB):
                    pe.wait_ge(norm_sq, self.i * KB + k + 1)
                    for half in range(2):
                        ins = pe.matmul(PS[:, 4 + half, 0:H2], mean_d[:, :],
                                        self.hf[:, k, half * H2:(half + 1) * H2], start=k == 0, stop=k == KB - 1)
                ins.then_inc(norm_ms, 1)

            def dve_scale(self, dve, col, split=True):
                dve.wait_ge(norm_sd, self.i + 1)
                dve.reciprocal(self.rstd[:, :], self.sd[:, :]).then_inc(norm_rs, 1)
                dve.wait_ge(norm_rs, self.i + 1)

                def lo(k):
                    dve.wait_ge(norm_hi, self.i * KB + k + 1)
                    dve.tensor_tensor(hl[:, k, :], self.hf[:, k, :], hh[:, k, :].bitcast(F32),
                                      ALU.subtract).then_inc(norm_lo, 1)
                for k in range(KB):
                    dve.scalar_tensor_tensor(out=self.hf[:, k, :], in0=xT[:, k, :], scalar=vec[:, col + k:col + k + 1],
                                             in1=self.rstd[:, :], op0=ALU.mult, op1=ALU.mult)\
                        .then_inc(norm_hf, 1)
                    if split and k >= 1:
                        lo(k - 1)
                if split:
                    lo(KB - 1)

        def stage_setup():
            with ExitStack() as st:
                xin = sb_in(st, "xin", [P, NTT + 1, DM])
                rows = sb_in(st, "rows", [P, 3, P])
                x_in = sem("x_in")
                vec_in = sem("vec_in")
                zeroed = sem("zeroed")
                consts = sem("consts")
                setup_tr = sem("setup_tr")
                setup_out = sem("setup_out")
                block = st.enter_context(nc.Block())
                vs = []
                r0 = 0
                for name in ("ffn1_norm", "mix_norm", "ffn2_norm"):
                    vs.append((0, r0, 2 * KB, d[name].rearrange("l (k p) -> (l k) p", p=P)))
                    r0 += 2 * KB
                vs.append((0, r0, KB, d["final_norm"].rearrange("(k p) -> k p", p=P)))
                r0 += KB
                for name in ("conv_a_b", "conv_a_ln_g", "conv_a_ln_b", "m_conv_b", "m_norm"):
                    k = d[name].shape[1] // P
                    vs.append((0, r0, k, d[name].rearrange("l (k p) -> (l k) p", p=P)))
                    r0 += k
                vs.append((1, 0, CW * CB, d["conv_a_w"].rearrange("l w (k p) -> (l w k) p", p=P)))
                vs.append((2, 0, MCW * MCD // P, d["m_conv_w"].rearrange("l w (k p) -> (l w k) p", p=P)))

                @block.sync
                def _(sp):
                    for t in range(NTT):
                        sp.dma_start(xin[:, t, :], d["x_prompt"][0, t * P:(t + 1) * P, :]).then_inc(x_in, 16)
                    sp.dma_start(xin[0:B, NTT, :], d["x_sample"].rearrange("b t c -> (b t) c")).then_inc(x_in, 16)
                    for c, r, k, src in vs:
                        sp.dma_start(rows[r:r + k, c, :], src).then_inc(vec_in, 16)
                    load_static(sp, 0)
                    load_static(sp, 1)

                @block.gpsimd
                def _(pool):
                    pool.memset(ident[:, :], 0.0).then_inc(zeroed, 1)
                    pool.memset(ones[:, :], 1.0)
                    pool.memset(mean_d[:, :], 1.0 / DM)
                    pool.memset(mean_c[:, :], 1.0 / CCH)
                    pool.memset(epst[:, :], EPS)
                    pool.wait_ge(zeroed, 1)
                    pool.affine_select(out=ident[:, :], in_=ident[:, :], compare_op=ALU.not_equal, fill=1.0, base=0,
                                       pattern=[[-1, P]], channel_multiplier=1).then_inc(consts, 1)

                @block.tensor
                def _(pe):
                    pe.sem_inc(w_used, 2)
                    pe.wait_ge(consts, 1)
                    pe.wait_ge(x_in, 16 * (NTT + 1))
                    for k in range(KB):
                        if k >= 6:
                            pe.wait_ge(setup_out, k - 5)
                        for t in range(NTT):
                            ins = pe.transpose(PS[:, k % 6, t * P:(t + 1) * P], xin[:, t, k * P:(k + 1) * P],
                                               ident[:, :])
                        ins.then_inc(setup_tr, 1)
                    for k in range(KB):
                        ins = pe.transpose(PS[:, 6, k * B:(k + 1) * B], xin[0:B, NTT, k * P:(k + 1) * P],
                                           ident[0:B, 0:B])
                    ins.then_inc(setup_tr, 1)
                    pe.wait_ge(vec_in, 16 * len(vs))
                    for c, n in enumerate((NV1, CW * CB, MCW * MCD // P)):
                        ins = pe.transpose(PS[:, 7, c * P:c * P + n], rows[0:n, c, :], ident[0:n, 0:n])
                    ins.then_inc(setup_tr, 1)

                @block.vector
                def _(dve):
                    dve.sem_inc(w_ready, 2)
                    for k in range(KB):
                        dve.wait_ge(setup_tr, k + 1)
                        dve.tensor_copy(xT[:, k, 0:T], PS[:, k % 6, :]).then_inc(setup_out, 1)
                    dve.wait_ge(setup_tr, KB + 1)
                    dve.tensor_copy(xT[:, :, T:NT], PS[:, 6, 0:KB * B].rearrange("p (k b) -> p k b", k=KB))
                    dve.wait_ge(setup_tr, KB + 2)
                    dve.tensor_copy(vec[:, :], PS[:, 7, 0:NV1])
                    dve.tensor_copy(cwv[:, :], PS[:, 7, P:P + CW * CB])
                    dve.tensor_copy(mwv[:, :], PS[:, 7, 2 * P:2 * P + MCW * MCD // P])
                    lo_static(dve, 0)

                @block.scalar
                def _(act):
                    hi_static(act, 0)

        silu_done = sem("silu_done")
        hid_done = sem("hid_done")
        hid_hi = sem("hid_hi")
        slot_out = sem("slot_out")

        def stage_ffn(f):
            w, l = FFN_W[f]
            N0 = N_F[f]
            with ExitStack() as st:
                nm = Norm((0, 2, 3, 5)[f], st)
                hid_h = sb_in(st, f"hid_h{f}", [P, FA, NT], F32R)
                hid_l = sb_in(st, f"hid_l{f}", [P, FA, NT], F32R)
                gact = sb_in(st, f"gact{f}", [P, 2, NT])
                hidf = sb_in(st, f"hidf{f}", [P, 2, NT])
                F0 = f * NF
                S0 = f * NS_FFN
                block = st.enter_context(nc.Block())
                phases = []
                s = 0
                for part, (f0, nf) in enumerate(FPARTS):
                    phases.append(("f", part, s, nf // 2))
                    s += nf
                    phases.append(("d", part, s, KB // 2))
                    s += KB

                @block.sync
                def _(sp):
                    for kind, part, s0, iters in phases:
                        f0, nf = FPARTS[part]
                        skip = 1 if s0 == 0 else 0
                        with sp.Fori(skip, iters) as t:
                            for u in range(2):
                                p = (N0 + s0 + u) % 2
                                parts = ffn_f(f, f0 + u + 2 * t, p) if kind == "f" else ffn_d(f, part, u + 2 * t, p)
                                load(sp, N0 + s0 + u + 2 * t, parts, p)
                    load_static(sp, N0 + NS_FFN)
                    load_static(sp, N0 + NS_FFN + 1)

                def ahead(kind, part, u):
                    return FPARTS[part][1] * P if kind == "d" and u == 0 else 2048

                def ends_program(f, kind, part):
                    return int(N_F[f] + NS_FFN == N_END and kind == "d" and part == 1)

                @block.scalar
                def _(act):
                    nm.act_squares(act)
                    nm.act_sd(act)
                    nm.act_hi(act)
                    for kind, part, s0, iters in phases:
                        f0, nf = FPARTS[part]

                        def slot(t, u, last=False):
                            n = N0 + s0 + u
                            if not last:
                                split_hi(act, n + 1 + 2 * t, (n + 1) % 2, (n + 1) // 2 + t, ahead(kind, part, u))
                            if kind == "f":
                                act.wait_ge(w_used, n + 3 + 2 * t)
                                b = 4 * (n % 2)
                                act.activation(halves(gact[:, u, :]), PS[:, b:b + 2, 0:H2], ACT.Silu)\
                                    .then_inc(silu_done, 1)
                                act.wait_ge(hid_done, F0 + f0 + u + 1 + 2 * t)
                                act.activation(hid_h[:, u + 2 * t, :], hidf[:, u, :], ACT.Copy)\
                                    .then_inc(hid_hi, 1)
                        peel = ends_program(f, kind, part)
                        with act.Fori(0, iters - peel) as t:
                            slot(t, 0)
                            slot(t, 1)
                        if peel:
                            slot(iters - 1, 0)
                            slot(iters - 1, 1, last=True)

                @block.tensor
                def _(pe):
                    nm.pe_mean(pe)
                    nm.wait_split(pe)
                    for kind, part, s0, iters in phases:
                        f0, nf = FPARTS[part]
                        if kind == "d":
                            pe.wait_ge(slot_out, S0 + s0 + 2)
                        with pe.Fori(0, iters) as t:
                            for u in range(2):
                                n = N0 + s0 + u
                                p = n % 2
                                pe.wait_ge(w_ready, n + 3 + 2 * t)
                                pe.wait_ge(slot_out, S0 + s0 + u + 1 + 2 * t)
                                b = 4 * p
                                if kind == "f":
                                    for q in range(2):
                                        ins = mm3(pe, [PS[:, b + 2 * q + i, 0:H2] for i in range(2)],
                                                  lambda k: (q * KB + k) * P, p, KB, hh, hl)
                                else:
                                    ins = mm3(pe, [PS[:, b + i, 0:H2] for i in range(2)], lambda k: k * P, p, nf,
                                              hid_h, hid_l)
                                ins.then_inc(w_used, 1)

                @block.vector
                def _(dve):
                    if f == 0:
                        dve.sem_inc(slot_out, 2)
                    nm.dve_scale(dve, V_NORM[(w, l)])
                    for kind, part, s0, iters in phases:
                        f0, nf = FPARTS[part]

                        def slot(t, u, last=False):
                            n = N0 + s0 + u
                            if not last:
                                split_lo(dve, n + 1 + 2 * t, (n + 1) % 2, ahead(kind, part, u))
                            b = 4 * (n % 2)
                            if kind == "f":
                                dve.wait_ge(silu_done, F0 + f0 + u + 1 + 2 * t)
                                dve.tensor_tensor(halves(hidf[:, u, :]), halves(gact[:, u, :]),
                                                  PS[:, b + 2:b + 4, 0:H2], ALU.mult).then_inc(hid_done, 1)
                                dve.wait_ge(hid_hi, F0 + f0 + u + 1 + 2 * t)
                                dve.tensor_tensor(hid_l[:, u + 2 * t, :], hidf[:, u, :],
                                                  hid_h[:, u + 2 * t, :].bitcast(F32),
                                                  ALU.subtract).then_inc(slot_out, 1)
                            else:
                                dve.wait_ge(w_used, n + 3 + 2 * t)
                                dve.scalar_tensor_tensor(
                                    out=halves(xT[:, u + 2 * t, :]), in0=PS[:, b:b + 2, 0:H2], scalar=0.5,
                                    in1=halves(xT[:, u + 2 * t, :]), op0=ALU.mult, op1=ALU.add)\
                                    .then_inc(slot_out, 1)
                        peel = ends_program(f, kind, part)
                        with dve.Fori(0, iters - peel) as t:
                            slot(t, 0)
                            slot(t, 1)
                        if peel:
                            slot(iters - 1, 0)
                            slot(iters - 1, 1, last=True)

        def stage_a():
            N0 = N_A
            PADW = CW - 1
            UW = PADW + NT
            KW = [T - kb * P for kb in range(NTT)]
            KO = {0: 0, 1: KW[0], 3: KW[0] + KW[1], 2: KW[0] + KW[1] + KW[3]}
            W = sum(KW)
            assert KO[2] == 2 * 512 and W <= 3 * 512
            NPH = NPG * NH
            SCALE = float(DH) ** -0.5
            NK = 4
            with ExitStack() as st:
                nm = Norm(1, st)
                cbuf = nm.hf[:, 0:CB, :]
                ktok = nm.hf[:, CB:CB + 4, 0:HD]
                uA = sb_in(st, "uA", [P, CB, UW])
                uS = sb_in(st, "uS", [P, CB, B, CW])
                qT = sb_in(st, "qT", [P, HD // P, NT])
                kT = sb_in(st, "kT", [P, HD // P, NT])
                vtok = sb_in(st, "vtok", [P, NTT, HD])
                zc = sb_in(st, "zc", [P, 2, W])
                sp_ = sb_in(st, "spl", [P, 2, W])
                vT = sp_[:, :, :].rearrange("p a c -> p (a c)")[:, 0:4 * NT].rearrange("p (k c) -> p k c", k=4)
                lnsq = zc[:, :, :].rearrange("p a c -> p (a c)")[:, 0:4 * NT].rearrange("p (k c) -> p k c", k=4)
                page = sb_in(st, "page", [P, NK, HD])
                prod = sb_in(st, "prod", [P, 2, HD])
                qb = sb_in(st, "qb", [P, 2, HD])
                srow = sb_in(st, "srow", [B, 3, HD])
                dz = sb_in(st, "dz", [P, B, NPG, NH])
                dsp = sb_in(st, "dsp", [P, B, NPG, NH])
                dsf = qb[:, 0, :].rearrange("p (b n h) -> p b n h", b=B, n=NPG)
                oS = sb_in(st, "oS", [P, HD // P, B])
                sig = nm.rstd
                biasb = sb_in(st, "biasb", [P, NH])
                ptab = sb_in(st, "ptab", [1, B * NPG], I32)
                tri = sb_in(st, "tri", [P, P])
                qmask = sb_in(st, "qmask", [P, P])
                tl = sb_in(st, "tl", [PADW + B, CCH])

                names = ("conv_in small_in masks tr_done cp_done u_done conv_done u0_mm u0_free u1_free a_chain d_chain "
                         "ln_cc ln_sq ln_ms ln_var ln_sd ln_cn ln_hi "
                         "tail_tr tail_cp kv_tr kv_cp srow_tr srow_cp qb_mm qb_cp page0 page1 page2 page3 "
                         "prod_done prod_free z_mm z_cp nabs_done lnp_done sp_done sum_mm t_done w_exp w_mask pv_mm pv_hi "
                         "pv_lo dnabs dlnp dsf_done dsum_mm dt_done dw_exp dpv_mm os_done os_hi mix_lo").split()
                S = {n: sem("a_" + n) for n in names}
                page_in = [S[f"page{i}"] for i in range(NK)]
                block = st.enter_context(nc.Block())
                cst_rows = B * PADW // 2

                @block.sync
                def _(sp):
                    sc = d["state_conv_a"][0].rearrange("b w c -> (b w) c")
                    for i in range(2):
                        sp.dma_start(zc[0:cst_rows, i, 0:CCH], sc[i * cst_rows:(i + 1) * cst_rows, :])\
                            .then_inc(S["conv_in"], 16)
                    sp.dma_start(biasb[:, :], d["sb_beta_bias"].to_broadcast([P, NH])).then_inc(S["small_in"], 16)
                    sp.dma_start(ptab[:, :], d["page_table"].rearrange("b n -> (b n)").rearrange("(a n) -> a n", a=1))\
                        .then_inc(S["small_in"], 16)
                    sp.dma_start(o[9][0, :, 0:PADW - 1, :], d["state_conv_a"][0][:, 1:PADW, :]).then_inc(stored, 16)
                    n_stores[0] += 1
                    for n in range(2, 12):
                        load_static(sp, N0 + n)
                    sp.wait_ge(S["tail_cp"], 1)
                    sp.dma_start(o[4][0, 0], tl[0:PADW, :]).then_inc(stored, 16)
                    sp.dma_start(o[9][0, :, PADW - 1, :], tl[PADW:PADW + B, :]).then_inc(stored, 16)
                    sp.wait_ge(S["kv_cp"], 2 * NTT)
                    sp.dma_start(o[2][0, 0].rearrange("(t p) h e -> p t (h e)", p=P), ktok).then_inc(stored, 16)
                    sp.dma_start(o[3][0, 0].rearrange("(t p) h e -> p t (h e)", p=P), vtok[:, :, :])\
                        .then_inc(stored, 16)
                    sp.wait_ge(S["srow_cp"], 3)
                    sp.dma_start(o[7][0, :, 0].rearrange("b h e -> b (h e)"), srow[:, 1, :]).then_inc(stored, 16)
                    sp.dma_start(o[8][0, :, 0].rearrange("b h e -> b (h e)"), srow[:, 2, :]).then_inc(stored, 16)
                    n_stores[0] += 6
                    sp.wait_ge(S["small_in"], 32)
                    i = 0
                    for cache in ("cache_sb_k", "cache_sb_v"):
                        for j in range(B * NPG):
                            pid = sp.value_load(ptab[0:1, j:j + 1], min_val=0, max_val=NPHYS - 1)
                            used = i - NK + 1
                            if 1 <= used <= B * NPG:
                                sp.wait_ge(S["prod_done"], used)
                            elif used > B * NPG:
                                sp.wait_ge(S["dpv_mm"], used - B * NPG)
                            src = d[cache][0].rearrange("n t h e -> n t (h e)")[bass.ds(pid, 1), :, :]
                            sp.dma_start(page[:, i % NK, :], src.rearrange("a t c -> t (a c)"))\
                                .then_inc(page_in[i % NK], 16)
                            i += 1
                    for n in range(12, NS_A + 2):
                        load_static(sp, N0 + n)
                    sp.wait_ge(stored, 16 * n_stores[0])

                @block.gpsimd
                def _(pool):
                    pool.memset(tri[:, :], 1.0).then_inc(S["masks"], 1)
                    pool.memset(qmask[:, :], 1.0).then_inc(S["masks"], 1)
                    pool.memset(uA[:, :, 0:PADW], 0.0).then_inc(S["masks"], 1)
                    pool.wait_ge(S["masks"], 2)
                    pool.affine_select(out=tri[:, :], in_=tri[:, :], compare_op=ALU.is_ge, fill=0.0, base=0,
                                       pattern=[[-1, P]], channel_multiplier=1).then_inc(S["masks"], 1)
                    pool.affine_select(out=qmask[:, :], in_=qmask[:, :], compare_op=ALU.is_ge, fill=0.0, base=-1,
                                       pattern=[[1, P]], channel_multiplier=-1).then_inc(S["masks"], 1)
                    for i in range(B * NPG):
                        b = i // NPG
                        pool.wait_ge(S["qb_cp"], b + 1)
                        pool.wait_ge(page_in[i % NK], 16 * (i // NK + 1))
                        if i >= 2:
                            pool.wait_ge(S["prod_free"], i - 1)
                        pool.tensor_tensor(prod[:, i % 2, :], page[:, i % NK, :], qb[:, b % 2, :], ALU.mult)\
                            .then_inc(S["prod_done"], 1)

                @block.tensor
                def _(pe):
                    nm.pe_mean(pe)
                    pe.wait_ge(S["conv_in"], 32)
                    for i in range(2):
                        for c in range(CB):
                            ins = pe.transpose(PS[:, 6 + i, c * P:c * P + cst_rows],
                                               zc[0:cst_rows, i, c * P:(c + 1) * P], ident[0:cst_rows, 0:cst_rows])
                    ins.then_inc(S["tr_done"], 1)
                    nm.wait_split(pe)

                    def project(i, rh, rl):
                        n = N0 + i
                        pe.wait_ge(w_ready, n + 3)
                        for j, free in enumerate(("u0_free", "u1_free")):
                            if i >= 1:
                                pe.wait_ge(S[free], i)
                            ins = mm3(pe, [PS[:, 2 * j + h, 0:H2] for h in range(2)], lambda k: (j * KB + k) * P,
                                      n % 2, KB, rh, rl)
                            if j == 0:
                                ins.then_inc(S["u0_mm"], 1)
                        ins.then_inc(w_used, 1)

                    for i in range(10):
                        project(i, hh, hl)
                    pe.wait_ge(S["u_done"], CB)
                    pe.wait_ge(S["cp_done"], 1)
                    for c in range(CB):
                        ins = pe.transpose(PS[0:PADW + B, 6, c * P:(c + 1) * P], uA[:, c, T:T + PADW + B], ident[:, :])
                    ins.then_inc(S["tail_tr"], 1)
                    pe.wait_ge(S["u0_free"], 10)
                    pe.wait_ge(S["u1_free"], 10)
                    for i, src in enumerate([kT] * NTT + [vT] * NTT):
                        t = i % NTT
                        if i >= 2:
                            pe.wait_ge(S["kv_cp"], i - 1)
                        for c in range(HD // P):
                            ins = pe.transpose(PS[:, 4 + i % 2, c * P:(c + 1) * P], src[:, c, t * P:(t + 1) * P],
                                               ident[:, :])
                        ins.then_inc(S["kv_tr"], 1)
                    for i, src in enumerate((qT, kT, vT)):
                        if i >= 1:
                            pe.wait_ge(S["srow_cp"], i)
                        for c in range(HD // P):
                            ins = pe.transpose(PS[0:B, 7, c * P:(c + 1) * P], src[:, c, T:NT], ident[:, :])
                        ins.then_inc(S["srow_tr"], 1)
                    pe.wait_ge(S["conv_done"], 1)
                    pe.wait_ge(S["kv_cp"], 2 * NTT)
                    for k in range(CB):
                        for half in range(2):
                            ins = pe.matmul(PS[:, 4 + half, 0:H2], mean_c[:, :], cbuf[:, k, half * H2:(half + 1) * H2],
                                            start=k == 0, stop=k == CB - 1)
                    ins.then_inc(S["ln_ms"], 1)
                    for k in range(CB):
                        pe.wait_ge(S["ln_sq"], k + 1)
                        for half in range(2):
                            ins = pe.matmul(PS[:, half, 0:H2], mean_c[:, :], lnsq[:, k, half * H2:(half + 1) * H2],
                                            start=k == 0, stop=k == CB - 1)
                    ins.then_inc(S["ln_var"], 1)
                    pe.wait_ge(S["ln_sd"], 1)
                    pe.wait_ge(S["masks"], 5)
                    pe.wait_ge(S["srow_cp"], 3)
                    pe.wait_ge(S["tail_cp"], 1)
                    z_ps = PS[:, 0:3, :].rearrange("p b c -> p (b c)")
                    s_ps = PS[:, 3:6, :].rearrange("p b c -> p (b c)")

                    for i in range(NH + 2):
                        if i < B:
                            if i >= 1:
                                pe.wait_ge(S["qb_cp"], i)
                            pe.matmul(PS[:, 7, :], ident[0:B, i:i + 1].to_broadcast([B, P]), srow[:, 0, :],
                                      start=True, stop=True).then_inc(S["qb_mm"], 1)
                        if i < NH:
                            if i >= 1:
                                pe.wait_ge(S["z_cp"], i)
                            r = DH * (i % 2)
                            for kb in range(NTT):
                                ins = pe.matmul(z_ps[:, KO[kb]:KO[kb] + KW[kb]],
                                                kT[r:r + DH, i // 2, kb * P:(kb + 1) * P],
                                                qT[r:r + DH, i // 2, kb * P:T], start=True, stop=True)
                            ins.then_inc(S["z_mm"], 1)
                        if 1 <= i <= NH:
                            h = i - 1
                            pe.wait_ge(S["sp_done"], h + 1)
                            if h >= 1:
                                pe.wait_ge(S["t_done"], h)
                            for kb in (0, 1, 3, 2):
                                for kk in range(kb, NTT):
                                    lo = KO[kb] + (kk - kb) * P
                                    ins = pe.matmul(s_ps[:, lo:lo + KW[kk]], (tri if kk == kb else ones)[:, :],
                                                    sp_[:, h % 2, KO[kk]:KO[kk] + KW[kk]],
                                                    start=kk == kb, stop=kk == NTT - 1)
                            ins.then_inc(S["sum_mm"], 1)
                        if i >= 2:
                            h = i - 2
                            r = DH * (h % 2)
                            pe.wait_ge(S["w_mask"], h + 1)
                            if h >= 2 and h % 2 == 0:
                                pe.wait_ge(S["pv_lo"], h // 2)
                            for kb in range(NTT):
                                ins = pe.matmul(PS[r:r + DH, 6, kb * P:T],
                                                vtok[:, kb, h * DH:(h + 1) * DH],
                                                zc[:, h % 2, KO[kb]:KO[kb] + KW[kb]], start=kb == 0, stop=kb == NTT - 1)
                            ins.then_inc(S["pv_mm"], 1)
                    pe.wait_ge(S["dsf_done"], 1)
                    pe.wait_ge(S["t_done"], NH)
                    fl = lambda a: a[:, :, :, :].rearrange("p b n h -> p (b n h)")
                    pe.matmul(PS[:, 5, 0:B * NPH], tri[:, :], fl(dsp), start=True, stop=False)
                    pe.matmul(PS[:, 5, 0:B * NPH], ones[:, :], fl(dsf), start=False, stop=True)\
                        .then_inc(S["dsum_mm"], 1)
                    pe.wait_ge(S["dw_exp"], 1)
                    for b in range(B):
                        for pg in range(NPG):
                            i = B * NPG + b * NPG + pg
                            pe.wait_ge(page_in[i % NK], 16 * (i // NK + 1))
                            for j in range(HD // P):
                                ins = pe.matmul(PS[:, j, 2 * b:2 * b + 2], page[:, i % NK, j * P:(j + 1) * P],
                                                dz[:, b, pg, 2 * j:2 * j + 2], start=pg == 0, stop=pg == NPG - 1)
                            ins.then_inc(S["dpv_mm"], 1)
                    pe.wait_ge(S["mix_lo"], 1)
                    pe.wait_ge(S["os_done"], 1)
                    for i in range(10, 14):
                        project(i, hh, hl)

                @block.scalar
                def _(act):
                    ch = Chain(act, S["a_chain"])
                    nm.act_squares(act)
                    nm.act_sd(act)
                    nm.act_hi(act)
                    for i in range(10):
                        hi_static(act, N0 + i + 1)
                        act.wait_ge(S["u0_mm"], i + 1)
                        ps = PS[:, 0:2, 0:H2]
                        if i < 4:
                            if i >= 1:
                                act.wait_ge(S["u_done"], i)
                            act.activation(halves(sig[:, :]), ps, ACT.Sigmoid).then_inc(S["u0_free"], 1)
                        else:
                            dst, name = ((qT, "q"), (kT, "k"), (vT, "v"))[(i - 4) // 2]
                            act.activation(halves(dst[:, 2 * (i % 2), :]), ps, ACT.Copy).then_inc(S["u0_free"], 1)
                    hi_static(act, N0 + 11)
                    act.wait_ge(S["ln_cc"], CB)
                    for k in range(CB):
                        act.activation(lnsq[:, k, :], cbuf[:, k, :], ACT.Square).then_inc(S["ln_sq"], 1)
                    act.wait_ge(S["ln_var"], 1)
                    act.activation(halves(nm.sd[:, :]), PS[:, 0:2, 0:H2], ACT.Sqrt, bias=epst[:, 0:1])\
                        .then_inc(S["ln_sd"], 1)
                    for k in range(CB):
                        act.wait_ge(S["ln_cn"], k + 1)
                        ch(act.activation(cbuf[:, k, :], cbuf[:, k, :], ACT.Silu, bias=vec[:, V_LB + k:V_LB + k + 1]))
                        act.activation(hh[:, k, :], cbuf[:, k, :], ACT.Copy).then_inc(S["ln_hi"], 1)
                    act.wait_ge(S["small_in"], 32)

                    z_ps = PS[:, 0:3, :].rearrange("p b c -> p (b c)")

                    for i in range(NH + 2):
                        if i < B:
                            act.wait_ge(S["qb_mm"], i + 1)
                            if i >= 2:
                                act.wait_ge(S["prod_done"], (i - 1) * NPG)
                            act.activation(qb[:, i % 2, :], PS[:, 7, :], ACT.Copy).then_inc(S["qb_cp"], 1)
                        if i < NH:
                            act.wait_ge(S["z_mm"], i + 1)
                            if i >= 2:
                                act.wait_ge(S["pv_mm"], i - 1)
                            act.activation(zc[:, i % 2, :], z_ps[:, 0:W], ACT.Identity, scale=SCALE,
                                           bias=biasb[:, i:i + 1]).then_inc(S["z_cp"], 1)
                            act.wait_ge(S["nabs_done"], i + 1)
                            ch(act.activation(sp_[:, i % 2, :], sp_[:, i % 2, :], ACT.Exp))
                            act.activation(sp_[:, i % 2, :], sp_[:, i % 2, :], ACT.Ln, bias=1.0)\
                                .then_inc(S["lnp_done"], 1)
                        if 1 <= i <= NH:
                            act.wait_ge(S["t_done"], i)
                            act.activation(zc[:, (i - 1) % 2, :], zc[:, (i - 1) % 2, :], ACT.Exp)\
                                .then_inc(S["w_exp"], 1)
                        if i >= 3 and i % 2 == 1:
                            pair = (i - 3) // 2
                            act.wait_ge(S["pv_mm"], 2 * pair + 2)
                            act.activation(hh[:, CB + pair, 0:T], PS[:, 6, :], ACT.Copy)\
                                .then_inc(S["pv_hi"], 1)
                    fl = lambda a: a[:, :, :, :].rearrange("p b n h -> p (b n h)")
                    act.wait_ge(S["dnabs"], 1)
                    ch(act.activation(fl(dsp), fl(dsp), ACT.Exp))
                    act.activation(fl(dsp), fl(dsp), ACT.Ln, bias=1.0).then_inc(S["dlnp"], 1)
                    act.wait_ge(S["dt_done"], 1)
                    act.activation(fl(dz), fl(dz), ACT.Exp).then_inc(S["dw_exp"], 1)
                    act.wait_ge(S["os_done"], 1)
                    act.activation(hh[:, CB:CB + HD // P, T:NT], oS[:, :, :], ACT.Copy).then_inc(S["os_hi"], 1)
                    for i in range(10, 14):
                        if i >= 11:
                            hi_static(act, N0 + i + 1)
                @block.vector
                def _(dve):
                    ch = Chain(dve, S["d_chain"])
                    nm.dve_scale(dve, V_NORM[("mix", 0)])
                    dve.wait_ge(S["tr_done"], 1)
                    hb = B // 2
                    for i in range(2):
                        for c in range(CB):
                            ins = dve.tensor_copy(uS[:, c, i * hb:(i + 1) * hb, 0:PADW],
                                                  PS[:, 6 + i, c * P:c * P + cst_rows]
                                                  .rearrange("p (b w) -> p b w", b=hb))
                    ins.then_inc(S["cp_done"], 1)
                    dve.wait_ge(S["cp_done"], 1)
                    dve.wait_ge(S["masks"], 5)

                    def conv(piece):
                        c, second = divmod(piece, 2)
                        out = cbuf[:, c, 0:T]
                        for w in (range(CW // 2 + 1, CW) if second else range(CW // 2 + 1)):
                            tap = cwv[:, w * CB + c:w * CB + c + 1]
                            if w == 0:
                                ch(dve.tensor_scalar(out, uA[:, c, w:w + T], tap, vec[:, V_CB + c:V_CB + c + 1],
                                                     ALU.mult, ALU.add))
                            else:
                                ch(dve.scalar_tensor_tensor(out=out, in0=uA[:, c, w:w + T], scalar=tap, in1=out,
                                                            op0=ALU.mult, op1=ALU.add))

                    def conv_sample(c):
                        taps = cwv[:, c:CW * CB:CB].rearrange("p (a w) -> p a w", a=1).to_broadcast([P, B, CW])
                        tmp = prod[:, 0, 0:B * CW].rearrange("p (b w) -> p b w", b=B)
                        ch(dve.tensor_tensor(tmp, uS[:, c, :, :], taps, ALU.mult))
                        ch(dve.tensor_reduce(oS[:, c, :], tmp, AX.X, ALU.add))
                        ch(dve.tensor_scalar(cbuf[:, c, T:NT], oS[:, c, :], vec[:, V_CB + c:V_CB + c + 1], None,
                                             ALU.add))

                    for i in range(10):
                        lo_static(dve, N0 + i + 1)
                        dve.wait_ge(w_used, N0 + i + 3)
                        ps = PS[:, 2:4, 0:H2]
                        if i < 4:
                            dve.wait_ge(S["u0_free"], i + 1)
                            dve.tensor_tensor(halves(uA[:, i, PADW:UW]), ps, halves(sig[:, :]), ALU.mult)\
                                .then_inc(S["u1_free"], 1)
                            dve.wait_ge(S["u1_free"], i + 1)
                            dve.tensor_copy(uS[:, i, :, PADW], uA[:, i, PADW + T:UW]).then_inc(S["u_done"], 1)
                        else:
                            dst, name = ((qT, "q"), (kT, "k"), (vT, "v"))[(i - 4) // 2]
                            dve.tensor_copy(halves(dst[:, 2 * (i % 2) + 1, :]), ps).then_inc(S["u1_free"], 1)
                        if i >= 2:
                            conv(i - 2)
                            if i % 2 == 1:
                                dve.wait_ge(S["u_done"], (i - 3) // 2 + 1)
                                conv_sample((i - 3) // 2)
                    dve.sem_inc(S["conv_done"], 1)
                    dve.wait_ge(S["tail_tr"], 1)
                    dve.tensor_copy(tl[:, :], PS[0:PADW + B, 6, :]).then_inc(S["tail_cp"], 1)
                    for i in range(2 * NTT):
                        dve.wait_ge(S["kv_tr"], i + 1)
                        dst = ktok[:, i, :] if i < NTT else vtok[:, i - NTT, :]
                        dve.tensor_copy(dst, PS[:, 4 + i % 2, :]).then_inc(S["kv_cp"], 1)
                    for i in range(3):
                        dve.wait_ge(S["srow_tr"], i + 1)
                        dve.tensor_copy(srow[:, i, :], PS[0:B, 7, :]).then_inc(S["srow_cp"], 1)
                    lo_static(dve, N0 + 11)
                    dve.wait_ge(S["ln_ms"], 1)
                    for k in range(CB):
                        dve.tensor_tensor(halves(cbuf[:, k, :]), halves(cbuf[:, k, :]), PS[:, 4:6, 0:H2],
                                          ALU.subtract).then_inc(S["ln_cc"], 1)
                    dve.wait_ge(S["ln_sd"], 1)
                    ch(dve.reciprocal(nm.rstd[:, :], nm.sd[:, :]))
                    for k in range(CB):
                        dve.scalar_tensor_tensor(out=cbuf[:, k, :], in0=cbuf[:, k, :],
                                                 scalar=vec[:, V_LG + k:V_LG + k + 1], in1=nm.rstd[:, :],
                                                 op0=ALU.mult, op1=ALU.mult).then_inc(S["ln_cn"], 1)
                    for k in range(CB):
                        dve.wait_ge(S["ln_hi"], k + 1)
                        dve.tensor_tensor(hl[:, k, :], cbuf[:, k, :], hh[:, k, :].bitcast(F32), ALU.subtract)

                    def nabs(out, in_):
                        return dve.scalar_tensor_tensor(out=out, in0=in_, scalar=-1.0, in1=in_, op0=ALU.mult,
                                                        op1=ALU.min)

                    for i in range(NH + 2):
                        if i < NH:
                            s, z = sp_[:, i % 2, :], zc[:, i % 2, :]
                            dve.wait_ge(S["z_cp"], i + 1)
                            if i >= 2:
                                dve.wait_ge(S["sum_mm"], i - 1)
                            nabs(s, z).then_inc(S["nabs_done"], 1)
                            dve.wait_ge(S["lnp_done"], i + 1)
                            ch(dve.scalar_tensor_tensor(out=s, in0=z, scalar=0.0, in1=s, op0=ALU.max, op1=ALU.add))
                            for kb in range(NTT):
                                ins = dve.tensor_tensor(s[:, KO[kb]:KO[kb] + P], s[:, KO[kb]:KO[kb] + P],
                                                        qmask[:, :], ALU.mult)
                            ins.then_inc(S["sp_done"], 1)
                        if 1 <= i <= B:
                            for pg in range(NPG):
                                j = (i - 1) * NPG + pg
                                dve.wait_ge(S["prod_done"], j + 1)
                                dve.tensor_reduce(dz[:, i - 1, pg, :],
                                                  prod[:, j % 2, :].rearrange("p (h e) -> p h e", h=NH), AX.X, ALU.add)\
                                    .then_inc(S["prod_free"], 1)
                        if 1 <= i <= NH:
                            z = zc[:, (i - 1) % 2, :]
                            dve.wait_ge(S["sum_mm"], i)
                            dve.tensor_tensor(z, z, PS[:, 3:6, :].rearrange("p b c -> p (b c)")[:, 0:W],
                                              ALU.subtract).then_inc(S["t_done"], 1)
                            dve.wait_ge(S["w_exp"], i)
                            for kb in range(NTT):
                                ins = dve.tensor_tensor(z[:, KO[kb]:KO[kb] + P], z[:, KO[kb]:KO[kb] + P],
                                                        qmask[:, :], ALU.mult)
                            ins.then_inc(S["w_mask"], 1)
                        if i >= 3 and i % 2 == 1:
                            pair = (i - 3) // 2
                            dve.wait_ge(S["pv_hi"], pair + 1)
                            dve.tensor_tensor(hl[:, CB + pair, 0:T], PS[:, 6, :],
                                              hh[:, CB + pair, 0:T].bitcast(F32), ALU.subtract)\
                                .then_inc(S["pv_lo"], 1)
                    fl3 = lambda a: a[:, :, :, :].rearrange("p b n h -> p (b n) h")
                    fl = lambda a: a[:, :, :, :].rearrange("p b n h -> p (b n h)")
                    bb = biasb[:, :].rearrange("p (a h) -> p a h", a=1).to_broadcast([P, B * NPG, NH])
                    dve.wait_ge(S["prod_free"], B * NPG)
                    ch(dve.scalar_tensor_tensor(out=fl3(dz), in0=fl3(dz), scalar=SCALE, in1=bb, op0=ALU.mult,
                                                op1=ALU.add))
                    nabs(fl(dsp), fl(dz)).then_inc(S["dnabs"], 1)
                    dve.wait_ge(S["dlnp"], 1)
                    ch(dve.scalar_tensor_tensor(out=fl(dsp), in0=fl(dz), scalar=0.0, in1=fl(dsp), op0=ALU.max,
                                                op1=ALU.add))
                    ch(dve.memset(dsf[:, :, NPG - 1, :], 0.0))
                    for pg in range(NPG - 2, -1, -1):
                        ch(dve.tensor_tensor(dsf[:, :, pg, :], dsf[:, :, pg + 1, :], dsp[:, :, pg + 1, :], ALU.add))
                    dve.sem_inc(S["dsf_done"], 1)
                    dve.wait_ge(S["dsum_mm"], 1)
                    dve.tensor_tensor(fl(dz), fl(dz), PS[:, 5, 0:B * NPH], ALU.subtract).then_inc(S["dt_done"], 1)
                    dve.wait_ge(S["dpv_mm"], B * NPG)
                    for r in range(2):
                        ch(dve.tensor_copy(oS[r * DH:(r + 1) * DH, :, :],
                                           PS[r * DH:(r + 1) * DH, 0:HD // P, r:2 * B:2]))
                    dve.sem_inc(S["os_done"], 1)
                    dve.wait_ge(S["os_hi"], 1)
                    dve.tensor_tensor(hl[:, CB:CB + HD // P, T:NT], oS[:, :, :],
                                      hh[:, CB:CB + HD // P, T:NT].bitcast(F32), ALU.subtract)\
                        .then_inc(S["mix_lo"], 1)
                    for i in range(10, 14):
                        if i >= 11:
                            lo_static(dve, N0 + i + 1)
                        for j, done in enumerate(("u0_mm", None)):
                            dve.wait_ge(*((S["u0_mm"], i + 1) if j == 0 else (w_used, N0 + i + 3)))
                            k = 2 * (i - 10) + j
                            dve.tensor_tensor(halves(xT[:, k, :]), halves(xT[:, k, :]), PS[:, 2 * j:2 * j + 2, 0:H2],
                                              ALU.add).then_inc(S[f"u{j}_free"], 1)

        def stage_m():
            N0 = N_M
            MT = MCW - 1
            NBX = MCD // P
            GC = GB * P
            TAIL = MT + B
            with ExitStack() as st:
                nm = Norm(4, st)
                yT = nm.hf[:, 0:GB, :]
                ysq = nm.hf[:, GB:2 * GB, :]
                zs = sb_in(st, "zs", [P, GB, NT])
                xraw = sb_in(st, "xraw", [P, 2, MT + NT])
                xwin = sb_in(st, "xwin", [P, 2, B, MCW])
                xc = sb_in(st, "xc", [P, GB + 2, NT])
                dtx = sb_in(st, "dtx", [P, NTT, GC])
                dtxe = ysq[:, 0:2, 0:GC]
                btok = sb_in(st, "btok", [P, NTT, MN])
                cbT = sb_in(st, "cbT", [P, NTT, P])
                hT = sb_in(st, "hT", [P, NTT, GC])
                dec = sb_in(st, "dec", [P, 2, T])
                cdec = sb_in(st, "cdec", [P, 2, T - P])
                yh = sb_in(st, "yh", [P, GB, NT], F32R)
                yl = sb_in(st, "yl", [P, GB, NT], F32R)
                mst = sb_in(st, "mst", [P, NBX, B * MT])
                tails = sb_in(st, "tails", [P, NBX, TAIL])
                ms_b = sb_in(st, "ms_b", [P, 2, GB, MN])
                ms_t = sb_in(st, "ms_t", [P, 2, GB, MN])
                bcs = sb_in(st, "bcs", [P, 2, 2 * MN])
                bsr = sb_in(st, "bsr", [B, 2 * MN])
                xdt = sb_in(st, "xdt", [P, GB, B])
                ysm = sb_in(st, "ysm", [P, GB, B])
                exs = sb_in(st, "exs", [P, GB, 2 * B])
                dtT = dec[:, :, :].rearrange("p a c -> p (a c)")[0:MH, 0:NT]
                daT = cdec[:, :, :].rearrange("p a c -> p (a c)")[0:MH, 0:NT]
                acsT = sb_in(st, "acsT", [MH, T])
                smp = sb_in(st, "smp", [MH, 2 * B])
                hvec = sb_in(st, "hvec", [MH, 4])
                dcol = sb_in(st, "dcol", [P, MH // 2])
                ttok = sb_in(st, "ttok", [P, 2, NTT, MH])
                etot = sb_in(st, "etot", [P, NTT, MH])
                wend = sb_in(st, "wend", [P, NTT, MH])
                causal = sb_in(st, "causal", [P, P])
                ttail = xc[:, :, :].rearrange("p a c -> p (a c)")[0:TAIL, 0:MCD]
                strows = xc[:, :, :].rearrange("p a c -> p (a c)")[0:B * MT, 0:MCD]
                hout = btok

                names = ("st_in vec3_in masks st_tr st_cp dt_mm u0_mm u0_free u1_free a_chain d_chain g_chain dt_x dt_nabs dt_lnp "
                         "dt_done exa acs_done smp_exp tk_tr tk_cp tot_mm tot_e wend_e wend_done dcol_mm dcol_cp raw_done "
                         "win_done conv_done silu_done xt_tr dtx_done bt_tr bt_cp cb_mm cb_done s_mm s_done head_bc "
                         "dec_arg dec_exp dec_cb cdec_e cdec_c y_mm y_done exs_mm exs_cp bs_cp bcs_mm bcs_cp "
                         "xdt_done ms0 ms1 ms_new ms_y ms_stored0 ms_stored1 ysq_done yms_done ysd_done yn_done yh_done yl_done ho_tr ho_cp "
                         "ho_st t_tr t_cp uo_mm gated h_scaled").split()
                S = {n: sem("m_" + n) for n in names}
                block = st.enter_context(nc.Block())
                flat_xin = "b w c -> (b w) c"

                def expand(pe, out, h, rows):
                    for r in range(2):
                        ins = pe.matmul(out[r * MP:(r + 1) * MP, :], ident[0:MH, h + r:h + r + 1].to_broadcast([MH, MP]),
                                        rows, start=True, stop=True)
                    return ins

                def group_block(g, i, j):
                    k = 2 * i + j - 4
                    return k, (g * GB + k if k < GB else MDI // P + g + (k - GB) * MG)

                def state(dve, g, t, hs):
                    i = g * NTT + t
                    dve.wait_ge(S["s_mm"], i + 1)
                    byh = lambda a: a.rearrange("p (h q) -> p h q", h=HPG)
                    if t == 0:
                        dve.tensor_copy(hT[:, 0, :], PS[:, 0, 0:GC]).then_inc(S["s_done"], 1)
                        return
                    dve.wait_ge(S["s_done"], i)
                    e = etot[:, t, hs].rearrange("p (h a) -> p h a", a=1).to_broadcast([P, HPG, MP])
                    dve.tensor_tensor(byh(hT[:, t, :]), byh(hT[:, t - 1, :]), e, ALU.mult).then_inc(S["h_scaled"], 1)
                    dve.wait_ge(S["h_scaled"], g * (NTT - 1) + t)
                    dve.tensor_tensor(hT[:, t, :], hT[:, t, :], PS[:, t, 0:GC], ALU.add)\
                        .then_inc(S["s_done"], 1)

                @block.sync
                def _(sp):
                    sp.dma_start(strows, d["state_mamba_conv"][0].rearrange(flat_xin)).then_inc(S["st_in"], 16)
                    for i, name in enumerate(("m_dt_bias", "m_A_log", "m_D")):
                        sp.dma_start(hvec[:, i:i + 1], d[name].rearrange("l h -> h l")).then_inc(S["vec3_in"], 16)
                    sp.dma_start(o[10][0, :, 0:MT - 1, :], d["state_mamba_conv"][0][:, 1:MT, :]).then_inc(stored, 16)
                    n_stores[0] += 1
                    for n in range(2, NS_M + 2):
                        load_static(sp, N0 + n)
                    sp.wait_ge(S["t_cp"], NBX // 4)
                    sp.dma_start(o[5][0, 0], ttail[0:MT, :]).then_inc(stored, 16)
                    sp.dma_start(o[10][0, :, MT - 1, :], ttail[MT:TAIL, :]).then_inc(stored, 16)
                    n_stores[0] += 2
                    sp.wait_ge(stored, 16 * n_stores[0])

                @block.gpsimd
                def _(pool):
                    pool.memset(causal[:, :], 1.0).then_inc(S["masks"], 1)
                    pool.memset(xraw[:, :, 0:MT], 0.0).then_inc(S["masks"], 1)
                    pool.wait_ge(S["masks"], 1)
                    pool.affine_select(out=causal[:, :], in_=causal[:, :], compare_op=ALU.is_ge, fill=0.0, base=0,
                                       pattern=[[1, P]], channel_multiplier=-1).then_inc(S["masks"], 1)
                    def load_state(i):
                        g, b = divmod(i, B)
                        if i >= 2:
                            pool.wait_ge(S[f"ms_stored{i % 2}"], 16 * (i // 2))
                            pool.wait_ge(S["ms_y"], i - 1)
                        pool.dma_start(ms_b[:, i % 2, :, :],
                                       d["state_ssm"][0, b, g * HPG:(g + 1) * HPG].rearrange("h q n -> (h q) n")
                                       .rearrange("(j p) n -> p j n", p=P)).then_inc(S[f"ms{i % 2}"], 16)

                    load_state(0)
                    for g in range(MG):
                        for b in range(B):
                            i = g * B + b
                            if i + 1 < MG * B:
                                load_state(i + 1)
                            s, t = ms_b[:, i % 2, :, :], ms_t[:, i % 2, :, :]
                            bc = bcs[:, i % 2, 0:MN].rearrange("p (a n) -> p a n", a=1).to_broadcast([P, GB, MN])
                            col = lambda a, c: a[:, :, c:c + 1].to_broadcast([P, GB, MN])
                            pool.wait_ge(S["xdt_done"], g + 1)
                            pool.wait_ge(S["bcs_cp"], i + 1)
                            if i >= 2:
                                pool.wait_ge(S["ms_y"], i - 1)
                            pool.tensor_tensor(t, col(xdt, b), bc, ALU.mult).then_inc(S["g_chain"], 1)
                            pool.wait_ge(S[f"ms{i % 2}"], 16 * (i // 2 + 1))
                            pool.tensor_tensor(s, s, col(exs, B + b), ALU.mult).then_inc(S["g_chain"], 1)
                            pool.wait_ge(S["g_chain"], 2 * i + 2)
                            pool.tensor_tensor(s, s, t, ALU.add).then_inc(S["ms_new"], 1)
                            pool.wait_ge(S["ms_new"], i + 1)
                            pool.dma_start(o[11][0, b, g * HPG:(g + 1) * HPG].rearrange("h q n -> (h q) n")
                                           .rearrange("(j p) n -> p j n", p=P), s).then_inc(S[f"ms_stored{i % 2}"], 16)
                        pool.wait_ge(S["ho_cp"], g + 1)
                        pool.dma_start(o[6][0, 0, g * HPG:(g + 1) * HPG].rearrange("h q n -> (h q) n")
                                       .rearrange("(j p) n -> p j n", p=P), hout[:, :, :]).then_inc(S["ho_st"], 16)
                    pool.wait_ge(S["ho_st"], 16 * MG)
                    pool.wait_ge(S["ms_stored0"], 16 * MG * B // 2)
                    pool.wait_ge(S["ms_stored1"], 16 * MG * B // 2)

                @block.tensor
                def _(pe):
                    nm.pe_mean(pe)
                    pe.wait_ge(S["st_in"], 16)
                    r = B * MT
                    for c in range(NBX):
                        ins = pe.transpose(PS[:, 6 + c // 12, (c % 12) * r:(c % 12 + 1) * r],
                                           strows[:, c * P:(c + 1) * P], ident[0:r, 0:r])
                    ins.then_inc(S["st_tr"], 1)
                    nm.wait_split(pe)
                    pe.wait_ge(w_ready, N0 + 3)
                    mm3(pe, [PS[0:MH, h, 0:H2] for h in range(2)], lambda k: k * MH, N0 % 2, KB, hh, hl, m=MH)\
                        .then_inc(w_used, 1)
                    pe.wait_ge(S["acs_done"], NTT)
                    pe.wait_ge(S["st_cp"], 2)
                    for j, src in enumerate((dtT, acsT)):
                        for t in range(NTT):
                            ins = pe.transpose(PS[:, 4, (j * NTT + t) * MH:(j * NTT + t + 1) * MH],
                                               src[:, t * P:(t + 1) * P], ident[0:MH, 0:MH])
                    ins.then_inc(S["tk_tr"], 1)
                    pe.wait_ge(S["tk_cp"], 1)
                    pe.matmul(PS[:, 5, 0:NTT * MH], ident[:, P - 1:P].to_broadcast([P, P]),
                              ttok[:, 1, :, :].rearrange("p t h -> p (t h)"), start=True, stop=True)\
                        .then_inc(S["tot_mm"], 1)
                    pe.wait_ge(S["vec3_in"], 48)
                    for j in range(MH // 2):
                        ins = expand(pe, PS[:, 6, j:j + 1], 2 * j, hvec[:, 2:3])
                    ins.then_inc(S["dcol_mm"], 1)

                    units = [1, 0]

                    def unit(j):
                        if units[j] >= 1:
                            pe.wait_ge(S[f"u{j}_free"], units[j])
                        units[j] += 1

                    for g in range(MG):
                        for i in range(5):
                            n = N0 + 1 + 7 * g + i
                            pe.wait_ge(w_ready, n + 3)
                            for j in range(2):
                                unit(j)
                                ins = mm3(pe, [PS[:, 2 * j + h, 0:H2] for h in range(2)], lambda k: (j * KB + k) * P,
                                          n % 2, KB, hh, hl)
                                if j == 0:
                                    ins.then_inc(S["u0_mm"], 1)
                            ins.then_inc(w_used, 1)
                        pe.wait_ge(S["silu_done"], 6 * (g + 1))
                        if g >= 1:
                            pe.wait_ge(S["y_done"], 4 * g)
                            pe.wait_ge(S["ho_cp"], g)
                        else:
                            pe.wait_ge(S["wend_done"], 1)
                            pe.wait_ge(S["dcol_cp"], 1)
                        for t in range(NTT):
                            i = g * NTT + t
                            if t >= 2:
                                pe.wait_ge(S["dtx_done"], i - 1)
                            for c in range(GB):
                                ins = pe.transpose(PS[:, 4 + t % 2, c * P:(c + 1) * P], xc[:, c, t * P:(t + 1) * P],
                                                   ident[:, :])
                            ins.then_inc(S["xt_tr"], 1)
                        for t in range(NTT):
                            ins = pe.transpose(PS[:, 6, t * P:(t + 1) * P], xc[:, GB, t * P:(t + 1) * P], ident[:, :])
                        ins.then_inc(S["bt_tr"], 1)
                        for t in range(NTT):
                            ins = pe.matmul(PS[:, 7, t * P:(t + 1) * P], xc[:, GB, t * P:(t + 1) * P],
                                            xc[:, GB + 1, t * P:(t + 1) * P], start=True, stop=True)
                        ins.then_inc(S["cb_mm"], 1)
                        pe.wait_ge(S["bt_cp"], g + 1)
                        for t in range(NTT):
                            i = g * NTT + t
                            pe.wait_ge(S["dtx_done"], i + 1)
                            pe.matmul(PS[:, t, 0:GC], btok[:, t, :], dtxe[:, t % 2, :], start=True,
                                      stop=True).then_inc(S["s_mm"], 1)
                        for j in range(2):
                            ins = pe.transpose(PS[0:B, 6, j * MN:(j + 1) * MN], xc[:, GB + j, T:NT], ident[:, :])
                        pe.wait_ge(S["smp_exp"], 1)
                        for j in range(GB):
                            ins = expand(pe, PS[:, 6, 2 * MN + j * 2 * B:2 * MN + (j + 1) * 2 * B],
                                         g * HPG + 2 * j, smp[:, :])
                        ins.then_inc(S["exs_mm"], 1)
                        pe.wait_ge(S["bs_cp"], g + 1)
                        pe.wait_ge(S["exs_cp"], g + 1)
                        pe.wait_ge(S["cb_done"], g + 1)
                        pe.wait_ge(S["s_done"], (g + 1) * NTT)

                        def head_bc(hd):
                            i = g * HPG + hd
                            if hd >= 2:
                                pe.wait_ge(S["dec_arg"], i - 1)
                                pe.wait_ge(S["cdec_e"], i - 1)
                            pe.matmul(PS[:, 4 + hd % 2, :], ident[0:MH, i:i + 1].to_broadcast([MH, P]), acsT[:, :],
                                      start=True, stop=True).then_inc(S["head_bc"], 1)

                        head_bc(0)
                        for hd in range(HPG):
                            i = g * HPG + hd
                            if hd + 1 < HPG:
                                head_bc(hd + 1)
                            k = g * B + hd
                            if k >= 1:
                                pe.wait_ge(S["bcs_cp"], k)
                            pe.matmul(PS[:, 6, 0:2 * MN], ident[0:B, hd:hd + 1].to_broadcast([B, P]), bsr[:, :],
                                      start=True, stop=True).then_inc(S["bcs_mm"], 1)
                            if hd % 2 == 0 and hd >= 2:
                                pe.wait_ge(S["y_done"], 4 * g + hd // 2)
                            pe.wait_ge(S["dec_cb"], i + 1)
                            pe.wait_ge(S["cdec_c"], i + 1)
                            r = MP * (hd % 2)
                            for t in range(NTT):
                                out = PS[r:r + MP, 7, t * P:(t + 1) * P]
                                ins = pe.matmul(out, dtx[:, t, hd * MP:(hd + 1) * MP], dec[:, i % 2, t * P:(t + 1) * P],
                                                start=True, stop=t == 0)
                                if t >= 1:
                                    ins = pe.matmul(out, hT[:, t - 1, hd * MP:(hd + 1) * MP],
                                                    cdec[:, i % 2, (t - 1) * P:t * P], start=False, stop=True)
                            ins.then_inc(S["y_mm"], 1)
                        pe.wait_ge(S["dec_arg"], (g + 1) * HPG)
                        pe.wait_ge(S["cdec_e"], (g + 1) * HPG)
                        for j in range(GB):
                            ins = pe.transpose(PS[:, 5, j * P:(j + 1) * P], hT[:, NTT - 1, j * P:(j + 1) * P],
                                               ident[:, :])
                        ins.then_inc(S["ho_tr"], 1)
                        pe.wait_ge(S["bcs_cp"], (g + 1) * B)
                        pe.wait_ge(S["y_done"], 4 * (g + 1))
                        for k in range(GB):
                            pe.wait_ge(S["ysq_done"], g * GB + k + 1)
                            for half in range(2):
                                ins = pe.matmul(PS[:, 6 + half, 0:H2], mean_c[:, :],
                                                ysq[:, k, half * H2:(half + 1) * H2], start=k == 0, stop=k == GB - 1)
                        ins.then_inc(S["yms_done"], 1)
                        pe.wait_ge(S["yl_done"], (g + 1) * GB)
                        for i in range(2):
                            n = N0 + 1 + 7 * g + 5 + i
                            pe.wait_ge(w_ready, n + 3)
                            for j in range(4):
                                unit(j % 2)
                                b = 2 * (j % 2)
                                ins = mm3(pe, [PS[:, b + h, 0:H2] for h in range(2)],
                                          lambda k: (k * 4 + j) * P, n % 2, GB, yh, yl)
                                if j < 3:
                                    ins.then_inc(S["uo_mm"], 1)
                            ins.then_inc(w_used, 1)
                    for q in range(NBX // 4):
                        if q >= 2:
                            pe.wait_ge(S["t_cp"], q - 1)
                        for c in range(4):
                            ins = pe.transpose(PS[0:TAIL, 4 + q % 2, c * P:(c + 1) * P], tails[:, 4 * q + c, :],
                                               ident[:, :])
                        ins.then_inc(S["t_tr"], 1)

                @block.scalar
                def _(act):
                    ch = Chain(act, S["a_chain"])
                    nm.act_squares(act)
                    nm.act_sd(act)
                    nm.act_hi(act)
                    hi_static(act, N0 + 1)
                    act.wait_ge(S["vec3_in"], 48)
                    act.activation(hvec[:, 3:4], hvec[:, 1:2], ACT.Exp).then_inc(S["exa"], 1)
                    act.wait_ge(w_used, N0 + 3)
                    act.activation(halves(daT[:, :]), PS[0:MH, 0:2, 0:H2], ACT.Identity, bias=hvec[:, 0:1])\
                        .then_inc(S["u0_free"], 1)
                    act.wait_ge(S["dt_nabs"], 1)
                    ch(act.activation(dtT[:, :], dtT[:, :], ACT.Exp))
                    act.activation(dtT[:, :], dtT[:, :], ACT.Ln, bias=1.0).then_inc(S["dt_lnp"], 1)
                    act.wait_ge(S["dt_done"], 2)
                    act.activation(smp[:, B:2 * B], daT[:, T:NT], ACT.Exp).then_inc(S["smp_exp"], 1)
                    act.wait_ge(S["tot_mm"], 1)
                    act.activation(etot[:, :, :].rearrange("p t h -> p (t h)"), PS[:, 5, 0:NTT * MH], ACT.Exp)\
                        .then_inc(S["tot_e"], 1)
                    act.wait_ge(S["wend_e"], 1)
                    act.activation(wend[:, :, :], wend[:, :, :], ACT.Exp).then_inc(S["tot_e"], 1)
                    for g in range(MG):
                        for i in range(5):
                            n = N0 + 1 + 7 * g + i
                            hi_static(act, n + 1)
                            for j in range(2):
                                if j == 0:
                                    act.wait_ge(S["u0_mm"], 5 * g + i + 1)
                                else:
                                    act.wait_ge(w_used, n + 3)
                                ps = PS[:, 2 * j:2 * j + 2, 0:H2]
                                if i < 2:
                                    if g >= 1:
                                        act.wait_ge(S["yn_done"], g * GB)
                                    act.activation(halves(zs[:, 2 * i + j, :]), ps, ACT.Silu)\
                                        .then_inc(S[f"u{j}_free"], 1)
                                else:
                                    k = 6 * g + 2 * (i - 2) + j
                                    if k >= 2:
                                        act.wait_ge(S["conv_done"], k - 1)
                                    act.activation(halves(xraw[:, j, MT:MT + NT]), ps, ACT.Copy)\
                                        .then_inc(S[f"u{j}_free"], 1)
                            if i >= 2:
                                for j in range(2):
                                    k = 6 * g + 2 * (i - 2) + j
                                    act.wait_ge(S["conv_done"], k + 1)
                                    c = 2 * (i - 2) + j
                                    act.activation(xc[:, c, :], xc[:, c, :], ACT.Silu).then_inc(S["silu_done"], 1)
                        act.wait_ge(S["bt_tr"], g + 1)
                        if g >= 1:
                            act.wait_ge(S["ho_st"], 16 * g)
                        act.activation(btok[:, :, :], PS[:, 6, :].rearrange("p (t n) -> p t n", t=NTT), ACT.Copy)\
                            .then_inc(S["bt_cp"], 1)
                        act.wait_ge(S["exs_mm"], g + 1)
                        act.activation(bsr[:, :], PS[0:B, 6, 0:2 * MN], ACT.Copy).then_inc(S["bs_cp"], 1)
                        act.activation(exs[:, :, :], PS[:, 6, 2 * MN:2 * MN + GB * 2 * B]
                                       .rearrange("p (j c) -> p j c", j=GB), ACT.Copy).then_inc(S["exs_cp"], 1)
                        for hd in range(HPG):
                            i = g * HPG + hd
                            act.wait_ge(S["dec_arg"], i + 1)
                            act.activation(dec[:, i % 2, :], dec[:, i % 2, :], ACT.Exp).then_inc(S["dec_exp"], 1)
                            act.wait_ge(S["head_bc"], i + 1)
                            if i >= 2:
                                act.wait_ge(S["y_mm"], i - 1)
                            act.activation(cdec[:, i % 2, :], PS[:, 4 + hd % 2, P:T], ACT.Exp).then_inc(S["cdec_e"], 1)
                            k = g * B + hd
                            act.wait_ge(S["bcs_mm"], k + 1)
                            if k >= 2:
                                act.wait_ge(S["ms_y"], k - 1)
                            act.activation(bcs[:, k % 2, :], PS[:, 6, 0:2 * MN], ACT.Copy).then_inc(S["bcs_cp"], 1)
                        act.wait_ge(S["ho_tr"], g + 1)
                        act.activation(hout[:, :, :], PS[:, 5, :].rearrange("p (j n) -> p j n", j=GB), ACT.Copy)\
                            .then_inc(S["ho_cp"], 1)
                        for k in range(GB):
                            act.wait_ge(S["gated"], g * GB + k + 1)
                            act.activation(ysq[:, k, :], yT[:, k, :], ACT.Square).then_inc(S["ysq_done"], 1)
                        hi_static(act, N0 + 1 + 7 * g + 6)
                        act.wait_ge(S["yms_done"], g + 1)
                        act.activation(halves(nm.sd[:, :]), PS[:, 6:8, 0:H2], ACT.Sqrt, bias=epst[:, 0:1])\
                            .then_inc(S["ysd_done"], 1)
                        for k in range(GB):
                            act.wait_ge(S["yn_done"], g * GB + k + 1)
                            act.activation(yh[:, k, :], yT[:, k, :], ACT.Copy).then_inc(S["yh_done"], 1)
                        hi_static(act, N0 + 1 + 7 * g + 7)

                @block.vector
                def _(dve):
                    ch = Chain(dve, S["d_chain"])
                    nm.dve_scale(dve, V_NORM[("mix", 1)])
                    r = B * MT
                    for i in range(2):
                        dve.wait_ge(S["st_tr"], 1)
                        dve.tensor_copy(mst[:, i * 12:(i + 1) * 12, :],
                                        PS[:, 6 + i, 0:12 * r].rearrange("p (c r) -> p c r", c=12))\
                            .then_inc(S["st_cp"], 1)
                    lo_static(dve, N0 + 1)
                    dve.wait_ge(S["u0_free"], 1)
                    dve.scalar_tensor_tensor(out=dtT[:, :], in0=daT[:, :], scalar=-1.0, in1=daT[:, :], op0=ALU.mult,
                                             op1=ALU.min).then_inc(S["dt_nabs"], 1)
                    dve.wait_ge(S["dt_lnp"], 1)
                    dve.scalar_tensor_tensor(out=dtT[:, :], in0=daT[:, :], scalar=0.0, in1=dtT[:, :], op0=ALU.max,
                                             op1=ALU.add).then_inc(S["dt_done"], 1)
                    dve.wait_ge(S["exa"], 1)
                    dve.wait_ge(S["dt_done"], 1)
                    dve.tensor_scalar(daT[:, :], dtT[:, :], hvec[:, 3:4], -1.0, ALU.mult, ALU.mult)\
                        .then_inc(S["dt_done"], 1)
                    dve.wait_ge(S["dt_done"], 2)
                    for t in range(NTT):
                        c = slice(t * P, (t + 1) * P)
                        dve.tensor_tensor_scan(acsT[:, c], ones[0:MH, 0:P], daT[:, c], 0.0, ALU.mult, ALU.add)\
                            .then_inc(S["acs_done"], 1)
                    ch(dve.tensor_copy(smp[:, 0:B], dtT[:, T:NT]))
                    dve.wait_ge(S["tk_tr"], 1)
                    dve.tensor_copy(ttok[:, :, :, :].rearrange("p a t h -> p (a t h)"), PS[:, 4, 0:2 * NTT * MH])\
                        .then_inc(S["tk_cp"], 1)
                    dve.wait_ge(S["tk_cp"], 1)
                    dve.wait_ge(S["tot_mm"], 1)
                    dve.wait_ge(S["tot_e"], 1)
                    dve.tensor_tensor(wend[:, :, :], PS[:, 5, 0:NTT * MH].rearrange("p (t h) -> p t h", t=NTT),
                                      ttok[:, 1, :, :], ALU.subtract).then_inc(S["wend_e"], 1)
                    dve.wait_ge(S["tot_e"], 2)
                    dve.tensor_tensor(wend[:, :, :], wend[:, :, :], ttok[:, 0, :, :], ALU.mult)\
                        .then_inc(S["wend_done"], 1)
                    dve.wait_ge(S["dcol_mm"], 1)
                    dve.tensor_copy(dcol[:, :], PS[:, 6, 0:MH // 2]).then_inc(S["dcol_cp"], 1)
                    dve.wait_ge(S["masks"], 3)
                    dve.wait_ge(S["dcol_cp"], 1)
                    dve.wait_ge(S["wend_done"], 1)
                    dve.wait_ge(S["st_cp"], 2)
                    for g in range(MG):
                        for i in range(5):
                            n = N0 + 1 + 7 * g + i
                            lo_static(dve, n + 1)
                            if i < 2:
                                continue
                            for j in range(2):
                                k, cb = group_block(g, i, j)
                                x = xraw[:, j, :]
                                out = xc[:, k, :]
                                dve.wait_ge(S[f"u{j}_free"], (1 - j) + 9 * g + i + 1)
                                dve.tensor_copy(xwin[:, j, :, 0:MT],
                                                mst[:, cb, :].rearrange("p (b w) -> p b w", b=B))
                                ch(dve.tensor_copy(xwin[:, j, :, MT], x[:, MT + T:MT + NT]))
                                dve.tensor_copy(tails[:, cb, :], x[:, T:T + TAIL])
                                for w in range(MCW):
                                    tap = mwv[:, w * NBX + cb:w * NBX + cb + 1]
                                    for dst, src in ((out[:, 0:T], x[:, w:w + T]), (out[:, T:NT], xwin[:, j, :, w])):
                                        if w == 0:
                                            ins = dve.tensor_scalar(dst, src, tap, vec[:, V_MB + cb:V_MB + cb + 1],
                                                                    ALU.mult, ALU.add)
                                        else:
                                            ins = dve.scalar_tensor_tensor(out=dst, in0=src, scalar=tap, in1=dst,
                                                                           op0=ALU.mult, op1=ALU.add)
                                    if w < MCW - 1:
                                        ch(ins)
                                ins.then_inc(S["conv_done"], 1)
                        hs = slice(g * HPG, (g + 1) * HPG)
                        for t in range(NTT):
                            i = g * NTT + t
                            dve.wait_ge(S["xt_tr"], i + 1)
                            ps = PS[:, 4 + t % 2, :].rearrange("p (h q) -> p h q", h=HPG)
                            byh = lambda a: a.rearrange("p (h a) -> p h a", a=1).to_broadcast([P, HPG, MP])
                            dve.tensor_tensor(dtx[:, t, :].rearrange("p (h q) -> p h q", h=HPG), ps,
                                              byh(ttok[:, 0, t, hs]), ALU.mult)
                            if t >= 2:
                                dve.wait_ge(S["s_mm"], i - 1)
                            dve.tensor_tensor(dtxe[:, t % 2, :].rearrange("p (h q) -> p h q", h=HPG), ps,
                                              byh(wend[:, t, hs]), ALU.mult).then_inc(S["dtx_done"], 1)
                            if t >= 2:
                                state(dve, g, t - 2, hs)
                        state(dve, g, 2, hs)
                        state(dve, g, 3, hs)
                        dve.wait_ge(S["cb_mm"], g + 1)
                        dve.tensor_tensor(cbT[:, :, :], PS[:, 7, :].rearrange("p (t c) -> p t c", t=NTT),
                                          causal[:, :].rearrange("p (a c) -> p a c", a=1).to_broadcast([P, NTT, P]),
                                          ALU.mult).then_inc(S["cb_done"], 1)
                        dve.wait_ge(S["exs_cp"], g + 1)
                        dve.tensor_tensor(xdt[:, :, :], xc[:, 0:GB, T:NT], exs[:, :, 0:B], ALU.mult)\
                            .then_inc(S["xdt_done"], 1)
                        dve.wait_ge(S["cb_done"], g + 1)
                        for hd in range(HPG + 1):
                            if hd < HPG:
                                i = g * HPG + hd
                                dve.wait_ge(S["head_bc"], i + 1)
                                if i >= 2:
                                    dve.wait_ge(S["y_mm"], i - 1)
                                for t in range(NTT):
                                    ins = dve.tensor_scalar(dec[:, i % 2, t * P:(t + 1) * P],
                                                            PS[:, 4 + hd % 2, t * P:(t + 1) * P],
                                                            ttok[:, 1, t, i:i + 1], 0.0, ALU.subtract, ALU.min)
                                ins.then_inc(S["dec_arg"], 1)
                            if hd >= 1:
                                k = g * B + hd - 1
                                dve.wait_ge(S["ms_new"], k + 1)
                                cc = bcs[:, k % 2, MN:2 * MN].rearrange("p (a n) -> p a n", a=1)\
                                    .to_broadcast([P, GB, MN])
                                ch(dve.tensor_tensor(ms_t[:, k % 2, :, :], ms_b[:, k % 2, :, :], cc, ALU.mult))
                                dve.tensor_reduce(ysm[:, :, hd - 1], ms_t[:, k % 2, :, :], AX.X, ALU.add)\
                                    .then_inc(S["ms_y"], 1)
                            if hd < HPG:
                                dve.wait_ge(S["dec_exp"], i + 1)
                                dve.tensor_tensor(dec[:, i % 2, :], dec[:, i % 2, :],
                                                  cbT[:, :, :].rearrange("p t c -> p (t c)"), ALU.mult)\
                                    .then_inc(S["dec_cb"], 1)
                                dve.wait_ge(S["cdec_e"], i + 1)
                                dve.tensor_tensor(cdec[:, i % 2, :], cdec[:, i % 2, :], xc[:, GB + 1, P:T],
                                                  ALU.mult).then_inc(S["cdec_c"], 1)
                            if hd >= 2 and hd % 2 == 0:
                                pair = hd // 2 - 1
                                dve.wait_ge(S["y_mm"], g * HPG + hd)
                                dve.scalar_tensor_tensor(out=yT[:, pair, 0:T], in0=xc[:, pair, 0:T],
                                                         scalar=dcol[:, g * GB + pair:g * GB + pair + 1],
                                                         in1=PS[:, 7, :], op0=ALU.mult, op1=ALU.add)\
                                    .then_inc(S["y_done"], 1)
                        dcb = dcol[:, g * GB:(g + 1) * GB].rearrange("p (j a) -> p j a", a=1).to_broadcast([P, GB, B])
                        ch(dve.tensor_tensor(yT[:, :, T:NT], xc[:, 0:GB, T:NT], dcb, ALU.mult))
                        dve.wait_ge(S["ms_y"], (g + 1) * B)
                        ch(dve.tensor_tensor(yT[:, :, T:NT], yT[:, :, T:NT], ysm[:, :, :], ALU.add))
                        dve.wait_ge(S["y_done"], 4 * (g + 1))
                        for k in range(GB):
                            dve.tensor_tensor(yT[:, k, :], yT[:, k, :], zs[:, k, :], ALU.mult)\
                                .then_inc(S["gated"], 1)
                        lo_static(dve, N0 + 1 + 7 * g + 6)
                        dve.wait_ge(S["ysd_done"], g + 1)
                        ch(dve.reciprocal(nm.rstd[:, :], nm.sd[:, :]))
                        for k in range(GB):
                            c = V_MN + g * GB + k
                            dve.scalar_tensor_tensor(out=yT[:, k, :], in0=yT[:, k, :], scalar=vec[:, c:c + 1],
                                                     in1=nm.rstd[:, :], op0=ALU.mult, op1=ALU.mult)\
                                .then_inc(S["yn_done"], 1)
                        for k in range(GB):
                            dve.wait_ge(S["yh_done"], g * GB + k + 1)
                            dve.tensor_tensor(yl[:, k, :], yT[:, k, :], yh[:, k, :].bitcast(F32), ALU.subtract)\
                                .then_inc(S["yl_done"], 1)
                        for i in range(2):
                            n = N0 + 1 + 7 * g + 5 + i
                            if i == 1:
                                lo_static(dve, n + 1)
                            for j in range(4):
                                if j < 3:
                                    dve.wait_ge(S["uo_mm"], 6 * g + 3 * i + j + 1)
                                else:
                                    dve.wait_ge(w_used, n + 3)
                                k = 4 * i + j
                                b = 2 * (j % 2)
                                dve.tensor_tensor(halves(xT[:, k, :]), halves(xT[:, k, :]), PS[:, b:b + 2, 0:H2],
                                                  ALU.add).then_inc(S[f"u{j % 2}_free"], 1)
                    for q in range(NBX // 4):
                        dve.wait_ge(S["t_tr"], q + 1)
                        dve.tensor_copy(ttail[:, 4 * q * P:4 * (q + 1) * P], PS[0:TAIL, 4 + q % 2, :])\
                            .then_inc(S["t_cp"], 1)

        def stage_final():
            with ExitStack() as st:
                nm = Norm(6, st)
                yout = sb_in(st, "yout", [P, NTT + 1, DM])
                out_tr = sem("out_tr")
                out_cp = sem("out_cp")
                block = st.enter_context(nc.Block())

                @block.scalar
                def _(act):
                    nm.act_squares(act)
                    nm.act_sd(act)

                @block.tensor
                def _(pe):
                    nm.pe_mean(pe)
                    nm.wait_normed(pe)
                    for t in range(NTT + 1):
                        if t >= 2:
                            pe.wait_ge(out_cp, t - 1)
                        b = 2 * (t % 2)
                        m = P if t < NTT else B
                        for k in range(KB):
                            ins = pe.transpose(PS[0:m, b + k // 4, (k % 4) * P:(k % 4 + 1) * P],
                                               nm.hf[:, k, t * P:t * P + m], ident[:, :])
                        ins.then_inc(out_tr, 1)

                @block.vector
                def _(dve):
                    nm.dve_scale(dve, V_NORM[("final", 0)], split=False)
                    for t in range(NTT + 1):
                        m = P if t < NTT else B
                        dve.wait_ge(out_tr, t + 1)
                        b = 2 * (t % 2)
                        dve.tensor_copy(yout[0:m, t, :].rearrange("p (b c) -> p b c", b=2), PS[0:m, b:b + 2, :])\
                            .then_inc(out_cp, 1)

                @block.sync
                def _(sp):
                    for t in range(NTT + 1):
                        sp.wait_ge(out_cp, t + 1)
                        if t < NTT:
                            sp.dma_start(o[0][0, t * P:(t + 1) * P, :], yout[:, t, :]).then_inc(stored, 16)
                        else:
                            sp.dma_start(o[1].rearrange("b t c -> (b t) c"), yout[0:B, t, :]).then_inc(stored, 16)
                        n_stores[0] += 1
                    sp.wait_ge(stored, 16 * n_stores[0])

        stage_setup()
        stage_ffn(0)
        stage_a()
        stage_ffn(1)
        stage_ffn(2)
        stage_m()
        stage_ffn(3)
        stage_final()


def kernel(**inputs):
    import numpy as _np
    import concourse.bacc as _bacc
    from concourse import mybir as _mybir
    from concourse.bass_utils import run_bass_kernel_spmd as _run

    nc = _bacc.Bacc("TRN2", target_bir_lowering=False, num_devices=1)
    arrays, d = {}, {}
    for name in inputs:
        a = _np.ascontiguousarray(inputs[name])
        arrays[f"in_{name}_dram"] = a
        d[name] = nc.dram_tensor(f"in_{name}_dram", a.shape, _mybir.dt.from_np(a.dtype), kind="ExternalInput").ap()
    s = {k: v.shape for k, v in d.items()}
    nb, t, dm = s["x_prompt"]
    b, ts, _ = s["x_sample"]
    ne, _, _, nh, dh = s["cache_sb_k"]
    no, _, mh, mp, mn = s["state_ssm"]
    cw1, cch = s["state_conv_a"][2:]
    mw1, mcd = s["state_mamba_conv"][2:]
    shapes = [(nb, t, dm), (b, ts, dm), (ne, nb, t, nh, dh), (ne, nb, t, nh, dh), (ne, nb, cw1, cch),
              (no, nb, mw1, mcd), (no, nb, mh, mp, mn), (ne, b, ts, nh, dh), (ne, b, ts, nh, dh), (ne, b, cw1, cch),
              (no, b, mw1, mcd), (no, b, mh, mp, mn)]
    outs = [nc.dram_tensor(f"out_{i}_dram", sh, _mybir.dt.float32, kind="ExternalOutput").ap()
            for i, sh in enumerate(shapes)]
    bass_trunk(nc, d, outs)
    r = _run(nc, [arrays], core_ids=[0])
    return tuple(r.results[0][f"out_{i}_dram"] for i in range(len(shapes)))
```

```python
from contextlib import ExitStack

import concourse.bass as bass
from concourse import mybir

F32 = mybir.dt.float32
F32R = mybir.dt.float32r
I32 = mybir.dt.int32
ALU = mybir.AluOpType
ACT = mybir.ActivationFunctionType
AX = mybir.AxisListType

P = 128


class Chain:

    def __init__(self, eng, sem):
        self.eng, self.sem, self.n = eng, sem, 0

    def __call__(self, ins):
        ins.then_inc(self.sem, 1)
        self.n += 1
        self.eng.wait_ge(self.sem, self.n)


def bass_trunk(nc, d, o):
    _, T, DM = d["x_prompt"].shape
    B = d["x_sample"].shape[0]
    NT = T + B
    H2 = NT // 2
    KB = DM // P
    DFF = d["ffn1_gate"].shape[2]
    NF = DFF // P
    FA = (NF // 2 + 1) // 2 * 2
    FPARTS = [(0, FA), (FA, NF - FA)]
    NTT = T // P
    CCH = d["conv_a_w"].shape[2]
    CW = d["conv_a_w"].shape[1]
    CB = CCH // P
    _, NPHYS, PAGE, NH, DH = d["cache_sb_k"].shape
    HD = NH * DH
    NPG = d["page_table"].shape[1]
    MH = d["m_A_log"].shape[1]
    MDI = d["m_norm"].shape[1]
    MP, MN = d["state_ssm"].shape[3:]
    MCW, MCD = d["m_conv_w"].shape[1:]
    MG = (MCD - MDI) // (2 * MN)
    HPG = MH // MG
    GB = MDI // MG // P
    EPS = 1e-6
    assert PAGE == P and MN == P and HD == CCH == 4 * P and GB == 4 and MP == DH == 64 and KB == 8 and H2 % 2 == 0

    NS_FFN = NF + 2 * KB
    NS_A = 10 + 4
    NS_M = 1 + MG * 7
    N_F = [2 * 0, NS_FFN + NS_A, 2 * NS_FFN + NS_A, 3 * NS_FFN + NS_A + NS_M]
    N_A = NS_FFN
    N_M = 3 * NS_FFN + NS_A
    N_END = 4 * NS_FFN + NS_A + NS_M
    FFN_W = [("ffn1", 0), ("ffn2", 0), ("ffn1", 1), ("ffn2", 1)]

    with ExitStack() as top:
        def sb_in(stack, name, shape, dt=F32):
            return stack.enter_context(nc.sbuf_tensor(name, shape, dt))

        def sb(name, shape, dt=F32):
            return sb_in(top, name, shape, dt)

        def sem(name):
            return top.enter_context(nc.semaphore(name))

        xT = sb("xT", [P, KB, NT])
        hh = sb("hh", [P, KB, NT], F32R)
        hl = sb("hl", [P, KB, NT], F32R)
        raw = sb("raw", [P, 2, 2048])
        wh = sb("wh", [P, 2, 2048], F32R)
        wl = sb("wl", [P, 2, 2048], F32R)
        ident = sb("ident", [P, P])
        ones = sb("ones", [P, P])
        mean_d = sb("mean_d", [P, P])
        mean_c = sb("mean_c", [P, P])
        epst = sb("epst", [P, 1])
        NV1 = 7 * KB + 3 * CB + MCD // P + MDI // P
        vec = sb("vec", [P, NV1])
        cwv = sb("cwv", [P, CW * CB])
        mwv = sb("mwv", [P, MCW * MCD // P])
        V_NORM = {("ffn1", 0): 0, ("ffn1", 1): KB, ("mix", 0): 2 * KB, ("mix", 1): 3 * KB,
                  ("ffn2", 0): 4 * KB, ("ffn2", 1): 5 * KB, ("final", 0): 6 * KB}
        V_CB, V_LG, V_LB = 7 * KB, 7 * KB + CB, 7 * KB + 2 * CB
        V_MB = 7 * KB + 3 * CB
        V_MN = V_MB + MCD // P
        PS = top.enter_context(nc.psum_tensor("PS", [P, 8, 512], F32))

        landed = [sem("landed0"), sem("landed1")]
        w_hi = sem("w_hi")
        w_ready = sem("w_ready")
        w_used = sem("w_used")
        stored = sem("stored")
        n_stores = [0]

        def raw_view(p, nk, cols, off=0):
            return raw[:, p, off:off + nk * cols].rearrange("p (k c) -> p k c", k=nk)

        def kview(ap):
            return ap.rearrange("(k p) c -> p k c", p=P)

        def slot_parts(n):
            p = n % 2
            for f in range(4):
                if N_F[f] <= n < N_F[f] + NS_FFN:
                    return ffn_parts(f, n - N_F[f], p)
            if N_A <= n < N_A + NS_A:
                i = n - N_A
                W = d["ab_in_proj"][0]
                if i < 2:
                    cols = [2 * CCH + i * 2 * P, 2 * CCH + i * 2 * P + P]
                elif i < 6:
                    cols = [CCH + (i - 2) * P, (i - 2) * P]
                elif i < 10:
                    cols = [2 * CCH + HD + (i - 6) * 2 * P, 2 * CCH + HD + (i - 6) * 2 * P + P]
                else:
                    W = d["ab_out_proj"][0]
                    cols = [(i - 10) * 2 * P, (i - 10) * 2 * P + P]
                return [(raw_view(p, KB, P, j * KB * P), kview(W[:, c:c + P])) for j, c in enumerate(cols)]
            i = n - N_M
            W = d["m_in_proj"][0]
            if i == 0:
                c, hk = MDI + MCD, KB // 2
                return [(raw_view(p, hk, MH, j * hk * MH), kview(W[j * hk * P:(j + 1) * hk * P, c:c + MH]))
                        for j in range(2)]
            if i < 4:
                kind, g, i = "x", 0, i - 1
            else:
                g, i = divmod(i - 4, 7)
                if i < 2:
                    kind = "z"
                elif g + 1 < MG and i < 5:
                    kind, g, i = "x", g + 1, i - 2
                else:
                    kind, i = "out", i - (5 if g + 1 < MG else 2)
            if kind != "out":
                b = 2 * i + (4 if kind == "x" else 0)
                return [(raw_view(p, KB, P, j * KB * P), kview(W[:, c:c + P]))
                        for j, c in enumerate((blk_col(g, b), blk_col(g, b + 1)))]
            W = d["m_out_proj"][0][g * GB * P:(g + 1) * GB * P, i * 4 * P:(i + 1) * 4 * P]
            return [(raw_view(p, 2, 4 * P, j * 2 * 4 * P), kview(W[j * 2 * P:(j + 1) * 2 * P, :])) for j in range(2)]

        def blk_col(g, i):
            if i < 4:
                return (g * GB + i) * P
            if i < 8:
                return MDI + (g * GB + i - 4) * P
            return MDI + MDI + (g + (i - 8) * MG) * P

        def ffn_parts(f, i, p):
            if i < FA:
                return ffn_f(f, i, p)
            if i < FA + KB:
                return ffn_d(f, 0, i - FA, p)
            if i < NF + KB:
                return ffn_f(f, i - KB, p)
            return ffn_d(f, 1, i - NF - KB, p)

        def ffn_f(f, F, p):
            w, l = FFN_W[f]
            return [(raw_view(p, KB, P), kview(d[w + "_gate"][l])[:, :, bass.ds(F * P, P)]),
                    (raw_view(p, KB, P, KB * P), kview(d[w + "_up"][l])[:, :, bass.ds(F * P, P)])]

        def ffn_d(f, part, j, p):
            w, l = FFN_W[f]
            f0, nf = FPARTS[part]
            src = kview(d[w + "_down"][l])
            hk = nf // 2
            return [(raw_view(p, hk, P, q * hk * P), src[:, f0 + q * hk:f0 + (q + 1) * hk, bass.ds(j * P, P)])
                    for q in range(2)]

        def load(sp, n, parts, p):
            sp.wait_ge(w_ready, n + 1)
            for dst, src in parts:
                sp.dma_start(dst, src).then_inc(landed[p], 16)

        def load_static(sp, n):
            if n < N_END:
                load(sp, n, slot_parts(n), n % 2)

        def split_hi(act, n, p, half, cols=2048):
            act.wait_ge(landed[p], 32 * half + 32)
            act.wait_ge(w_used, n + 1)
            act.activation(wh[:, p, 0:cols], raw[:, p, 0:cols], ACT.Copy).then_inc(w_hi, 1)

        def split_lo(dve, n, p, cols=2048):
            dve.wait_ge(w_hi, n + 1)
            dve.tensor_tensor(wl[:, p, 0:cols], raw[:, p, 0:cols], wh[:, p, 0:cols].bitcast(F32),
                              ALU.subtract).then_inc(w_ready, 1)

        def hi_static(act, n):
            if n < N_END:
                split_hi(act, n, n % 2, n // 2, slot_cols(n))

        def lo_static(dve, n):
            if n < N_END:
                split_lo(dve, n, n % 2, slot_cols(n))

        def slot_cols(n):
            return sum(a.shape[1] * a.shape[2] for a, _ in slot_parts(n))

        def mm3(pe, outs, w, k0, nk, rh, rl, m=P, before=None):
            ins = None
            for k in range(nk):
                if before:
                    before(k)
                c = w(k)
                for a, (x, y) in enumerate(((wh, rh), (wh, rl), (wl, rh))):
                    for half, out in enumerate(outs):
                        ins = pe.matmul(out, x[:, k0, c:c + m], y[:, k, half * H2:(half + 1) * H2],
                                        start=k == 0 and a == 0, stop=k == nk - 1 and a == 2)
            return ins

        def halves(ap):
            return ap.rearrange("p (h c) -> p h c", h=2)

        ssum = sb("ssum", [P, NT])
        sqr = sb("sqr", [P, NT])
        sdev = sb("sdev", [P, NT])
        rstd = sb("rstd", [P, NT])
        norm_sq = sem("norm_sq")
        norm_acc = sem("norm_acc")
        norm_ms = sem("norm_ms")
        norm_sd = sem("norm_sd")
        norm_rs = sem("norm_rs")
        norm_hi = sem("norm_hi")
        norm_lo = sem("norm_lo")

        def norm_zero(pool, i):
            if i >= 1:
                pool.wait_ge(norm_ms, i)
            pool.memset(ssum[:, :], 0.0).then_inc(norm_acc, 1)

        def norm_sum(pool, i, j):
            pool.wait_ge(norm_acc, i * (KB + 1) + 1 + j)
            pool.tensor_tensor(sqr[:, :], xT[:, j, :], xT[:, j, :], ALU.mult).then_inc(norm_sq, 1)
            pool.wait_ge(norm_sq, i * KB + 1 + j)
            pool.tensor_tensor(ssum[:, :], ssum[:, :], sqr[:, :], ALU.add).then_inc(norm_acc, 1)

        def norm_split_hi(act, col, j):
            act.activation(hh[:, j, :], xT[:, j, :], ACT.Copy, scale=vec[:, bass.ds(col + j, 1)]).then_inc(norm_hi, 1)

        def norm_split_lo(dve, i, col, j):
            dve.wait_ge(norm_hi, i * KB + 1 + j)
            dve.scalar_tensor_tensor(out=hl[:, j, :], in0=xT[:, j, :], scalar=vec[:, bass.ds(col + j, 1)],
                                     in1=hh[:, j, :].bitcast(F32), op0=ALU.mult, op1=ALU.subtract)\
                .then_inc(norm_lo, 1)

        def norm_mean(pe, i, b):
            pe.wait_ge(norm_acc, (i + 1) * (KB + 1))
            for half in range(2):
                ins = pe.matmul(PS[:, b + half, 0:H2], mean_d[:, :], ssum[:, half * H2:(half + 1) * H2],
                                start=True, stop=True)
            ins.then_inc(norm_ms, 1)

        def norm_root(act, i, b):
            act.wait_ge(norm_ms, i + 1)
            act.activation(halves(sdev[:, :]), PS[:, b:b + 2, 0:H2], ACT.Sqrt, bias=epst[:, 0:1]).then_inc(norm_sd, 1)

        def norm_rstd(dve, i):
            dve.wait_ge(norm_sd, i + 1)
            dve.reciprocal(rstd[:, :], sdev[:, :]).then_inc(norm_rs, 1)
            dve.wait_ge(norm_rs, i + 1)

        def wait_h(pe, i):
            return lambda k: pe.wait_ge(norm_lo, i * KB + k + 1)

        def stage_setup():
            with ExitStack() as st:
                xin = sb_in(st, "xin", [P, NTT + 1, DM])
                rows = sb_in(st, "rows", [P, 3, P])
                x_in = sem("x_in")
                vec_in = sem("vec_in")
                zeroed = sem("zeroed")
                consts = sem("consts")
                setup_tr = sem("setup_tr")
                setup_out = sem("setup_out")
                block = st.enter_context(nc.Block())
                vs = []
                r0 = 0
                for name in ("ffn1_norm", "mix_norm", "ffn2_norm"):
                    vs.append((0, r0, 2 * KB, d[name].rearrange("l (k p) -> (l k) p", p=P)))
                    r0 += 2 * KB
                vs.append((0, r0, KB, d["final_norm"].rearrange("(k p) -> k p", p=P)))
                r0 += KB
                for name in ("conv_a_b", "conv_a_ln_g", "conv_a_ln_b", "m_conv_b", "m_norm"):
                    k = d[name].shape[1] // P
                    vs.append((0, r0, k, d[name].rearrange("l (k p) -> (l k) p", p=P)))
                    r0 += k
                vs.append((1, 0, CW * CB, d["conv_a_w"].rearrange("l w (k p) -> (l w k) p", p=P)))
                vs.append((2, 0, MCW * MCD // P, d["m_conv_w"].rearrange("l w (k p) -> (l w k) p", p=P)))

                @block.sync
                def _(sp):
                    for t in range(NTT):
                        sp.dma_start(xin[:, t, :], d["x_prompt"][0, t * P:(t + 1) * P, :]).then_inc(x_in, 16)
                    sp.dma_start(xin[0:B, NTT, :], d["x_sample"].rearrange("b t c -> (b t) c")).then_inc(x_in, 16)
                    for c, r, k, src in vs:
                        sp.dma_start(rows[r:r + k, c, :], src).then_inc(vec_in, 16)
                    load_static(sp, 0)
                    load_static(sp, 1)

                @block.gpsimd
                def _(pool):
                    pool.memset(ident[:, :], 0.0).then_inc(zeroed, 1)
                    pool.memset(ones[:, :], 1.0)
                    pool.memset(mean_d[:, :], 1.0 / DM)
                    pool.memset(mean_c[:, :], 1.0 / CCH)
                    pool.memset(epst[:, :], EPS)
                    pool.wait_ge(zeroed, 1)
                    pool.affine_select(out=ident[:, :], in_=ident[:, :], compare_op=ALU.not_equal, fill=1.0, base=0,
                                       pattern=[[-1, P]], channel_multiplier=1).then_inc(consts, 1)
                    norm_zero(pool, 0)
                    pool.wait_ge(setup_out, KB + 1)
                    for k in range(KB):
                        norm_sum(pool, 0, k)

                @block.tensor
                def _(pe):
                    pe.sem_inc(w_used, 2)
                    pe.wait_ge(consts, 1)
                    pe.wait_ge(x_in, 16 * (NTT + 1))
                    for k in range(KB):
                        if k >= 6:
                            pe.wait_ge(setup_out, k - 5)
                        for t in range(NTT):
                            ins = pe.transpose(PS[:, k % 6, t * P:(t + 1) * P], xin[:, t, k * P:(k + 1) * P],
                                               ident[:, :])
                        ins.then_inc(setup_tr, 1)
                    for k in range(KB):
                        ins = pe.transpose(PS[:, 6, k * B:(k + 1) * B], xin[0:B, NTT, k * P:(k + 1) * P],
                                           ident[0:B, 0:B])
                    ins.then_inc(setup_tr, 1)
                    pe.wait_ge(vec_in, 16 * len(vs))
                    for c, n in enumerate((NV1, CW * CB, MCW * MCD // P)):
                        ins = pe.transpose(PS[:, 7, c * P:c * P + n], rows[0:n, c, :], ident[0:n, 0:n])
                    ins.then_inc(setup_tr, 1)

                @block.vector
                def _(dve):
                    dve.sem_inc(w_ready, 2)
                    for k in range(KB):
                        dve.wait_ge(setup_tr, k + 1)
                        dve.tensor_copy(xT[:, k, 0:T], PS[:, k % 6, :]).then_inc(setup_out, 1)
                    dve.wait_ge(setup_tr, KB + 1)
                    dve.tensor_copy(xT[:, :, T:NT], PS[:, 6, 0:KB * B].rearrange("p (k b) -> p k b", k=KB))
                    dve.wait_ge(setup_tr, KB + 2)
                    dve.tensor_copy(vec[:, :], PS[:, 7, 0:NV1])
                    dve.tensor_copy(cwv[:, :], PS[:, 7, P:P + CW * CB])
                    dve.tensor_copy(mwv[:, :], PS[:, 7, 2 * P:2 * P + MCW * MCD // P]).then_inc(setup_out, 1)
                    lo_static(dve, 0)
                    dve.wait_ge(setup_out, KB + 1)
                    for k in range(KB):
                        norm_split_lo(dve, 0, V_NORM[FFN_W[0]], k)

                @block.scalar
                def _(act):
                    hi_static(act, 0)
                    act.wait_ge(setup_out, KB + 1)
                    for k in range(KB):
                        norm_split_hi(act, V_NORM[FFN_W[0]], k)

        g_scaled = sem("g_scaled")
        up_scaled = sem("up_scaled")
        silu_done = sem("silu_done")
        hid_done = sem("hid_done")
        hid_hi = sem("hid_hi")
        slot_out = sem("slot_out")

        def stage_ffn(f):
            N0 = N_F[f]
            ni = (0, 2, 3, 5)[f]
            next_col = (V_NORM[("mix", 0)], V_NORM[FFN_W[2]], V_NORM[("mix", 1)], None)[f]
            with ExitStack() as st:
                hid_h = sb_in(st, f"hid_h{f}", [P, FA, NT], F32R)
                hid_l = sb_in(st, f"hid_l{f}", [P, FA, NT], F32R)
                gact = sb_in(st, f"gact{f}", [P, 2, NT])
                hidf = sb_in(st, f"hidf{f}", [P, 2, NT])
                H0 = f * NF
                S0 = f * NS_FFN
                block = st.enter_context(nc.Block())
                phases = []
                s = 0
                for part, (f0, nf) in enumerate(FPARTS):
                    phases.append(("f", part, s, nf // 2))
                    s += nf
                    phases.append(("d", part, s, KB // 2))
                    s += KB
                mean_bank = 4 * ((N0 + 1) % 2)

                def run(eng, phase, slot):
                    kind, part, s0, iters = phase
                    head = int(s0 == 0)
                    tail = int(N0 + NS_FFN == N_END and kind == "d" and part == 1)
                    if head:
                        slot(0, 0)
                        slot(0, 1)
                    with eng.Fori(head, iters - tail) as t:
                        slot(t, 0)
                        slot(t, 1)
                    if tail:
                        slot(iters - 1, 0)
                        slot(iters - 1, 1)

                def ahead(kind, part, u):
                    return FPARTS[part][1] * P if kind == "d" and u == 0 else 2048

                def is_last(kind, part, t, u):
                    return N0 + NS_FFN == N_END and kind == "d" and part == 1 and isinstance(t, int) and u == 1

                @block.sync
                def _(sp):
                    for kind, part, s0, iters in phases:
                        f0, nf = FPARTS[part]
                        with sp.Fori(int(s0 == 0), iters) as t:
                            for u in range(2):
                                p = (N0 + s0 + u) % 2
                                parts = ffn_f(f, f0 + u + 2 * t, p) if kind == "f" else ffn_d(f, part, u + 2 * t, p)
                                load(sp, N0 + s0 + u + 2 * t, parts, p)
                    load_static(sp, N0 + NS_FFN)
                    load_static(sp, N0 + NS_FFN + 1)

                @block.gpsimd
                def _(pool):
                    s0 = NF + KB
                    norm_zero(pool, ni + 1)
                    with pool.Fori(0, KB) as j:
                        pool.wait_ge(slot_out, S0 + s0 + 3 + j)
                        norm_sum(pool, ni + 1, j)

                @block.scalar
                def _(act):
                    for phase in phases:
                        kind, part, s0, iters = phase
                        f0, nf = FPARTS[part]

                        def slot(t, u):
                            n = N0 + s0 + u
                            if not is_last(kind, part, t, u):
                                split_hi(act, n + 1 + 2 * t, (n + 1) % 2, (n + 1) // 2 + t, ahead(kind, part, u))
                            if n == N0 and isinstance(t, int):
                                norm_root(act, ni, mean_bank)
                            if kind == "f":
                                act.wait_ge(g_scaled, H0 + f0 + u + 1 + 2 * t)
                                act.activation(gact[:, u, :], gact[:, u, :], ACT.Silu).then_inc(silu_done, 1)
                                act.wait_ge(hid_done, H0 + f0 + u + 1 + 2 * t)
                                act.activation(hid_h[:, u + 2 * t, :], hidf[:, u, :], ACT.Copy)\
                                    .then_inc(hid_hi, 1)
                            elif part == 1 and next_col is not None:
                                act.wait_ge(slot_out, S0 + s0 + u + 3 + 2 * t)
                                norm_split_hi(act, next_col, u + 2 * t)
                        run(act, phase, slot)

                @block.tensor
                def _(pe):
                    for phase in phases:
                        kind, part, s0, iters = phase
                        f0, nf = FPARTS[part]
                        if kind == "d":
                            pe.wait_ge(slot_out, S0 + s0 + 2)

                        def slot(t, u):
                            n = N0 + s0 + u
                            p = n % 2
                            b = 4 * p
                            first = s0 == 0 and isinstance(t, int)
                            if kind == "f" and first and u == 1:
                                pe.wait_ge(norm_sd, ni + 1)
                            pe.wait_ge(w_ready, n + 3 + 2 * t)
                            pe.wait_ge(slot_out, S0 + s0 + u + 1 + 2 * t)
                            if kind == "f":
                                for q in range(2):
                                    ins = mm3(pe, [PS[:, b + 2 * q + i, 0:H2] for i in range(2)],
                                              lambda k: (q * KB + k) * P, p, KB, hh, hl,
                                              before=wait_h(pe, ni) if first and u == 0 and q == 0 else None)
                                    if first and u == 0 and q == 0:
                                        norm_mean(pe, ni, mean_bank)
                            else:
                                ins = mm3(pe, [PS[:, b + i, 0:H2] for i in range(2)], lambda k: k * P, p, nf,
                                          hid_h, hid_l)
                            ins.then_inc(w_used, 1)
                        run(pe, phase, slot)

                @block.vector
                def _(dve):
                    if f == 0:
                        dve.sem_inc(slot_out, 2)
                    for phase in phases:
                        kind, part, s0, iters = phase
                        f0, nf = FPARTS[part]

                        def slot(t, u):
                            n = N0 + s0 + u
                            if not is_last(kind, part, t, u):
                                split_lo(dve, n + 1 + 2 * t, (n + 1) % 2, ahead(kind, part, u))
                            if n == N0 and isinstance(t, int):
                                norm_rstd(dve, ni)
                            b = 4 * (n % 2)
                            dve.wait_ge(w_used, n + 3 + 2 * t)
                            if kind == "f":
                                i = H0 + f0 + u + 1 + 2 * t
                                r = halves(rstd[:, :])
                                dve.tensor_tensor(halves(gact[:, u, :]), PS[:, b:b + 2, 0:H2], r, ALU.mult)\
                                    .then_inc(g_scaled, 1)
                                dve.tensor_tensor(halves(hidf[:, u, :]), PS[:, b + 2:b + 4, 0:H2], r, ALU.mult)\
                                    .then_inc(up_scaled, 1)
                                dve.wait_ge(up_scaled, i)
                                dve.wait_ge(silu_done, i)
                                dve.tensor_tensor(hidf[:, u, :], hidf[:, u, :], gact[:, u, :], ALU.mult)\
                                    .then_inc(hid_done, 1)
                                dve.wait_ge(hid_hi, i)
                                dve.tensor_tensor(hid_l[:, u + 2 * t, :], hidf[:, u, :],
                                                  hid_h[:, u + 2 * t, :].bitcast(F32),
                                                  ALU.subtract).then_inc(slot_out, 1)
                            else:
                                dve.scalar_tensor_tensor(
                                    out=halves(xT[:, u + 2 * t, :]), in0=PS[:, b:b + 2, 0:H2], scalar=0.5,
                                    in1=halves(xT[:, u + 2 * t, :]), op0=ALU.mult, op1=ALU.add)\
                                    .then_inc(slot_out, 1)
                                if part == 1 and next_col is not None:
                                    norm_split_lo(dve, ni + 1, next_col, u + 2 * t)
                        run(dve, phase, slot)

        def stage_a():
            N0 = N_A
            PADW = CW - 1
            UW = PADW + NT
            KW = [T - kb * P for kb in range(NTT)]
            KO = {0: 0, 1: KW[0], 3: KW[0] + KW[1], 2: KW[0] + KW[1] + KW[3]}
            W = sum(KW)
            assert KO[2] == 2 * 512 and W <= 3 * 512 and KO[3] + P == KO[2] and NTT == 4
            NPH = NPG * NH
            NB = HD // P
            SCALE = float(DH) ** -0.5
            NK, NV = 6, 8
            NSP = 3
            QS, ES, KS = 2, 3, 10
            with ExitStack() as st:
                cbuf = sb_in(st, "cbuf", [P, CB, NT])
                uA = sb_in(st, "uA", [P, CB, UW])
                ubuf = sb_in(st, "ubuf", [P, 2 * HD])
                uS = ubuf[:, 0:CB * B * CW].rearrange("p (c b w) -> p c b w", c=CB, b=B)
                qT = sb_in(st, "qT", [P, NB, NT])
                kT = sb_in(st, "kT", [P, NB, NT])
                vtok = sb_in(st, "vtok", [P, NTT, HD])
                zc = sb_in(st, "zc", [P, W])
                sp_ = sb_in(st, "spl", [P, NSP, W])
                page = sb_in(st, "page", [P, NK, HD])
                prod = sb_in(st, "prod", [P, 2, HD])
                qb = sb_in(st, "qb", [P, 2, HD])
                qrow = sb_in(st, "qrow", [B, HD])
                vbuf = sb_in(st, "vbuf", [P, 2, NT])
                dz = sb_in(st, "dz", [P, B, NPG, NH])
                dsp = sb_in(st, "dsp", [P, B, NPG, NH])
                orow = [qb[:, 0, :], qb[:, 1, :], dsp[:, :, :, :].rearrange("p b n h -> p (b n h)")]
                dsf = qb[:, 0, :].rearrange("p (b n h) -> p b n h", b=B, n=NPG)
                csum = sb_in(st, "csum", [P, CB, B])
                biasb = sb_in(st, "biasb", [P, NH])
                ptab = sb_in(st, "ptab", [1, B * NPG], I32)
                tri = sb_in(st, "tri", [P, P])
                qmask = sb_in(st, "qmask", [P, P])
                flat = lambda a: a.rearrange("p k c -> p (k c)")
                ktok, tl, krow, vrow = page[:, 0:NTT, :], page[0:PADW + B, NTT, :], page[0:B, NTT + 1, :], qrow[:, :]
                cst = zc[:, 0:2 * HD].rearrange("p (a c) -> p a c", a=2)

                def lnsq(k):
                    return (zc[:, :] if k < 2 else sp_[:, NSP - 1, :])[:, k % 2 * NT:(k % 2 + 1) * NT]

                kplace = [page[:, i, :] for i in range(NK)] \
                    + [flat(sp_[:, :, :])[:, i * HD:(i + 1) * HD] for i in range(NSP * W // HD)] \
                    + [zc[:, i * HD:(i + 1) * HD] for i in range(W // HD)] \
                    + [dsp[:, :, :, :].rearrange("p b n h -> p (b n h)")]
                vplace = [page[:, i, :] for i in range(NK)] + [ubuf[:, i * HD:(i + 1) * HD] for i in range(NV - NK)]
                assert len(kplace) == 2 * NPG and CB == 4 and NH == 8

                names = ("conv_in small_in masks tr_done cp_done u_done u0_mm u0_free u1_free gate_sig d_chain "
                         "ln_cc ln_sq ln_ms ln_var ln_sd ln_cn ln_act ln_hi conv_done tap_done tap_add "
                         "qrow_tr qrow_cp qb_mm qb_cp key_in0 key_in1 v_tr v_cp misc_tr misc_cp row_cp kv_out "
                         "val0 val1 val2 val3 val4 val5 val6 val7 prod_done prod_free z_mm abs_done e_done lnp_done z_cp "
                         "sp_max sp_done sum_mm t_done w_exp w_mask pv_mm pv_hi pv_lo dscore dabs de dlnp dsf_done dsum_mm "
                         "dt_done dw_exp dpv_mm orow_cp orow_in os_tr os_hi mix_lo").split()
                S = {n: nc.alloc_semaphore("a_" + n) for n in names}
                key_in = [S["key_in0"], S["key_in1"]]
                val_in = [S[f"val{i}"] for i in range(NV)]
                block = st.enter_context(nc.Block())
                cst_rows = B * PADW // 2
                fl = lambda a: a[:, :, :, :].rearrange("p b n h -> p (b n h)")
                fl3 = lambda a: a[:, :, :, :].rearrange("p b n h -> p (b n) h")
                LC = CB - 1

                MISC = [("k", t) for t in range(NTT)] + [("tail", 0), ("krow", 0)]
                NR = 9
                VROUNDS = [0] * 3 * NR + ([1] * (NR - 1) + [2]) * 6 + [1, 1, 0, 0, 0, 0, 0, 1, 1]
                assert sum(VROUNDS) == B * NPG and len(VROUNDS) == NR * (NH + 2)

                def between(i):
                    return [1] if i == QS + 1 else []

                def after(i):
                    return [0] if i == QS else [i - 1] if QS < i < B + 1 else []

                REDUCES = [9] * (KS - ES - 1)
                REDUCES.append(B * NPG - sum(REDUCES))

                def vstart(i, part=0):
                    return sum(VROUNDS[:NR * i + part])

                sample_out = PS[:, 5, 0:NB * B].rearrange("p (j b) -> p j b", j=NB)

                @block.sync
                def _(sp):
                    sc = d["state_conv_a"][0].rearrange("b w c -> (b w) c")
                    for i in range(2):
                        sp.dma_start(cst[0:cst_rows, i, :], sc[i * cst_rows:(i + 1) * cst_rows, :])\
                            .then_inc(S["conv_in"], 16)
                    sp.dma_start(biasb[:, :], d["sb_beta_bias"].to_broadcast([P, NH])).then_inc(S["small_in"], 16)
                    sp.dma_start(ptab[:, :], d["page_table"].rearrange("b n -> (b n)").rearrange("(a n) -> a n", a=1))\
                        .then_inc(S["small_in"], 16)
                    sp.dma_start(o[9][0, :, 0:PADW - 1, :], d["state_conv_a"][0][:, 1:PADW, :]).then_inc(stored, 16)
                    n_stores[0] += 1

                    def load_page(cache, j, dst, done):
                        pid = sp.value_load(ptab[0:1, j:j + 1], min_val=0, max_val=NPHYS - 1)
                        src = d[cache][0].rearrange("n t h e -> n t (h e)")[bass.ds(pid, 1), :, :]
                        sp.dma_start(dst, src.rearrange("a t c -> t (a c)")).then_inc(done, 16)

                    for i in range(KS):
                        load_static(sp, N0 + i + 2)
                        if i == 0:
                            sp.wait_ge(S["small_in"], 32)
                        for b in ([i] if i < 2 else [i - 1] if 3 <= i <= B else []):
                            if b == 1:
                                sp.wait_ge(S["tr_done"], 1)
                            if b >= 2:
                                sp.wait_ge(S["prod_done"], (b - 1) * NPG)
                            for pg in range(NPG):
                                load_page("cache_sb_k", b * NPG + pg, kplace[(b % 2) * NPG + pg], key_in[b % 2])
                    load_static(sp, N0 + KS + 2)
                    sp.wait_ge(S["v_cp"], NB)
                    sp.dma_start(o[3][0, 0].rearrange("(t p) h e -> p t (h e)", p=P), vtok[:, :, :])\
                        .then_inc(stored, 16)
                    n_stores[0] += 1
                    sp.wait_ge(S["misc_cp"], len(MISC))
                    sp.wait_ge(S["row_cp"], 1)
                    for dst, src in ((o[2][0, 0].rearrange("(t p) h e -> p t (h e)", p=P), ktok),
                                     (o[4][0, 0], tl[0:PADW, :]),
                                     (o[9][0, :, PADW - 1, :], tl[PADW:PADW + B, :]),
                                     (o[7][0, :, 0].rearrange("b h e -> b (h e)"), krow),
                                     (o[8][0, :, 0].rearrange("b h e -> b (h e)"), vrow)):
                        sp.dma_start(dst, src).then_inc(S["kv_out"], 16)
                    sp.wait_ge(S["kv_out"], 80)
                    for i in range(B * NPG):
                        if i >= NV:
                            sp.wait_ge(S["dpv_mm"], i - NV + 1)
                        load_page("cache_sb_v", i, vplace[i % NV], val_in[i % NV])
                        if i == vstart(5) + NV:
                            load_static(sp, N0 + KS + 3)
                    for b in range(B):
                        q = 32 * (b % 3)
                        sp.wait_ge(S["orow_cp"], b + 1)
                        sp.dma_start(qrow[b:b + 1, :], orow[b // 3][q:q + 1, :]).then_inc(S["orow_in"], 16)
                    for n in range(KS + 4, NS_A + 2):
                        load_static(sp, N0 + n)
                    sp.wait_ge(stored, 16 * n_stores[0])

                @block.gpsimd
                def _(pool):
                    pool.memset(tri[:, :], 1.0).then_inc(S["masks"], 1)
                    pool.memset(qmask[:, :], 1.0).then_inc(S["masks"], 1)
                    pool.memset(uA[:, :, 0:PADW], 0.0).then_inc(S["masks"], 1)
                    pool.wait_ge(S["masks"], 2)
                    pool.affine_select(out=tri[:, :], in_=tri[:, :], compare_op=ALU.is_ge, fill=0.0, base=0,
                                       pattern=[[-1, P]], channel_multiplier=1).then_inc(S["masks"], 1)
                    pool.affine_select(out=qmask[:, :], in_=qmask[:, :], compare_op=ALU.is_ge, fill=0.0, base=-1,
                                       pattern=[[1, P]], channel_multiplier=-1).then_inc(S["masks"], 1)
                    for i in range(B * NPG):
                        b, pg = divmod(i, NPG)
                        if pg == 0:
                            pool.wait_ge(S["qb_cp"], b + 1)
                            pool.wait_ge(key_in[b % 2], 16 * NPG * (b // 2 + 1))
                        if i >= 2:
                            pool.wait_ge(S["prod_free"], i - 1)
                        pool.tensor_tensor(prod[:, i % 2, :], kplace[(b % 2) * NPG + pg], qb[:, b % 2, :], ALU.mult)\
                            .then_inc(S["prod_done"], 1)
                    acc = cbuf[:, LC, 0:T]
                    for w in range(1, CW):
                        pool.wait_ge(S["tap_done"], w + 1)
                        if w >= 2:
                            pool.wait_ge(S["tap_add"], w - 1)
                        pool.tensor_tensor(acc, acc, prod[:, w % 2, :], ALU.add).then_inc(S["tap_add"], 1)
                    norm_zero(pool, 2)
                    for j in range(KB):
                        pool.wait_ge(S[f"u{j % 2}_free"], KS + j // 2 + 1)
                        norm_sum(pool, 2, j)

                @block.tensor
                def _(pe):
                    def project(i, j, before=None):
                        n = N0 + i
                        if j == 0:
                            pe.wait_ge(w_ready, n + 3)
                        if i >= 1:
                            pe.wait_ge(S[f"u{j}_free"], i)
                        ins = mm3(pe, [PS[:, 2 * j + h, 0:H2] for h in range(2)], lambda k: (j * KB + k) * P,
                                  n % 2, KB, hh, hl, before=before)
                        ins.then_inc(S["u0_mm"] if j == 0 else w_used, 1)

                    def v_tokens(k):
                        i = 8 + k // 2
                        pe.wait_ge(S[f"u{k % 2}_free"], i + 1)
                        if k >= 2:
                            pe.wait_ge(S["v_cp"], k - 1)
                        pe.transpose(PS[0:B, 6, k * P:(k + 1) * P], vbuf[:, k % 2, T:NT], ident[:, :])
                        for t in range(NTT):
                            ins = pe.transpose(PS[:, 4 + k % 2, t * P:(t + 1) * P],
                                               vbuf[:, k % 2, t * P:(t + 1) * P], ident[:, :])
                        ins.then_inc(S["v_tr"], 1)

                    def q_everywhere(samples):
                        for b in samples:
                            if b == 0:
                                pe.wait_ge(S["qrow_cp"], 1)
                            else:
                                pe.wait_ge(S["qb_cp"], b)
                            pe.matmul(PS[:, 7, :], ident[0:B, b:b + 1].to_broadcast([B, P]), qrow[:, :],
                                      start=True, stop=True).then_inc(S["qb_mm"], 1)

                    for i in range(KS):
                        project(i, 0, wait_h(pe, 1) if i == 0 else None)
                        if i == 0:
                            norm_mean(pe, 1, 4)
                            pe.wait_ge(S["conv_in"], 32)
                            for r in range(2):
                                for c in range(CB):
                                    ins = pe.transpose(PS[:, 6 + r, c * P:c * P + cst_rows],
                                                       cst[0:cst_rows, r, c * P:(c + 1) * P],
                                                       ident[0:cst_rows, 0:cst_rows])
                            ins.then_inc(S["tr_done"], 1)
                        if i == QS:
                            pe.wait_ge(S["u1_free"], QS)
                            pe.wait_ge(S["cp_done"], 1)
                            for c in range(NB):
                                ins = pe.transpose(PS[0:B, 6, c * P:(c + 1) * P], qT[:, c, T:NT], ident[:, :])
                            ins.then_inc(S["qrow_tr"], 1)
                        if i == 9:
                            v_tokens(0)
                            v_tokens(1)
                        q_everywhere(between(i))
                        project(i, 1)
                        q_everywhere(after(i))

                    z_ps = PS[:, 0:3, :].rearrange("p b c -> p (b c)")
                    s_ps = PS[:, 3:6, :].rearrange("p b c -> p (b c)")

                    def values(i, part):
                        if vstart(i, part) == 0 and vstart(i, part + 1):
                            pe.wait_ge(S["dw_exp"], 1)
                        for v in range(vstart(i, part), vstart(i, part + 1)):
                            b, pg = divmod(v, NPG)
                            q = 32 * (b % 3)
                            pe.wait_ge(val_in[v % NV], 16 * (v // NV + 1))
                            if pg == 0 and b >= 3:
                                pe.wait_ge(S["orow_cp"], b - 2)
                            for h in range(NH):
                                ins = pe.matmul(PS[q:q + 1, 7, h * DH:(h + 1) * DH], dz[:, b, pg, h:h + 1],
                                                vplace[v % NV][:, h * DH:(h + 1) * DH], start=pg == 0 and h == 0,
                                                stop=pg == NPG - 1 and h == NH - 1)
                            ins.then_inc(S["dpv_mm"], 1)

                    def scores(h):
                        if h >= 1:
                            pe.wait_ge(S["z_cp"], h)
                        r = DH * (h % 2)
                        for kb in range(NTT):
                            ins = pe.matmul(z_ps[:, KO[kb]:KO[kb] + KW[kb]],
                                            kT[r:r + DH, h // 2, kb * P:(kb + 1) * P],
                                            qT[r:r + DH, h // 2, kb * P:T], start=True, stop=True)
                        ins.then_inc(S["z_mm"], 1)

                    def misc(m):
                        kind, t = MISC[m]
                        if m >= 2:
                            pe.wait_ge(S["misc_cp"], m - 1)
                        for c in range(NB):
                            cs = slice(c * P, (c + 1) * P)
                            if kind == "k":
                                ins = pe.transpose(PS[:, 6 + m % 2, cs], kT[:, c, t * P:(t + 1) * P], ident[:, :])
                            elif kind == "tail":
                                ins = pe.transpose(PS[0:PADW + B, 6 + m % 2, cs], uA[:, c, T:T + PADW + B],
                                                   ident[:, :])
                            else:
                                ins = pe.transpose(PS[0:B, 6 + m % 2, cs], kT[:, c, T:NT], ident[:, :])
                        ins.then_inc(S["misc_tr"], 1)

                    def stats(i, block, done):
                        for k in range(CB):
                            for half in range(2):
                                ins = pe.matmul(PS[:, half, 0:H2], mean_c[:, :],
                                                block(k)[:, half * H2:(half + 1) * H2], start=k == 0, stop=k == CB - 1)
                            if k == CB - 1:
                                ins.then_inc(done, 1)
                            if k % 2:
                                values(i, 7 + k // 2)

                    pe.wait_ge(S["u0_free"], KS)
                    pe.wait_ge(S["u1_free"], KS)
                    scores(0)
                    v_tokens(2)
                    v_tokens(3)
                    pe.wait_ge(S["masks"], 5)
                    pe.wait_ge(S["qb_cp"], B)
                    pe.wait_ge(S["row_cp"], 1)
                    pe.wait_ge(S["v_cp"], NB)
                    for i in range(NH + 2):
                        if i >= 2:
                            h = i - 2
                            r = DH * (h % 2)
                            pe.wait_ge(S["w_mask"], h + 1)
                            if h == 0:
                                pe.wait_ge(S["misc_cp"], len(MISC))
                            if h >= 2 and h % 2 == 0:
                                pe.wait_ge(S["pv_lo"], h // 2)
                            for kb in range(NTT):
                                ins = pe.matmul(PS[r:r + DH, 6, kb * P:T],
                                                vtok[:, kb, h * DH:(h + 1) * DH],
                                                sp_[:, h % NSP, KO[kb]:KO[kb] + KW[kb]], start=kb == 0, stop=kb == NTT - 1)
                                if kb == NTT - 1:
                                    ins.then_inc(S["pv_mm"], 1)
                                if kb % 2:
                                    values(i, kb // 2)
                        if i <= 1:
                            for m in range(i * len(MISC) // 2, (i + 1) * len(MISC) // 2):
                                misc(m)
                        if 1 <= i <= NH:
                            h = i - 1
                            pe.wait_ge(S["sp_done"], h + 1)
                            if h >= 1:
                                pe.wait_ge(S["t_done"], h)
                            pieces = [(kb, kk) for kb in (0, 1, 3, 2) for kk in range(kb, NTT)]
                            for n, (kb, kk) in enumerate(pieces):
                                lo = KO[kb] + (kk - kb) * P
                                ins = pe.matmul(s_ps[:, lo:lo + KW[kk]], (tri if kk == kb else ones)[:, :],
                                                sp_[:, h % NSP, KO[kk]:KO[kk] + KW[kk]],
                                                start=kk == kb, stop=kk == NTT - 1)
                                if n == len(pieces) - 1:
                                    ins.then_inc(S["sum_mm"], 1)
                                if n % 2:
                                    values(i, 2 + n // 2)
                        if i < NH:
                            values(i, 7)
                            values(i, 8)
                        if i + 1 < NH:
                            scores(i + 1)
                        if i == NH:
                            pe.wait_ge(S["z_cp"], NH)
                            pe.wait_ge(S["conv_done"], 1)
                            pe.wait_ge(S["tap_add"], CW - 1)
                            stats(i, lambda k: cbuf[:, k, :], S["ln_ms"])
                        if i == NH + 1:
                            pe.wait_ge(S["ln_sq"], CB)
                            stats(i, lnsq, S["ln_var"])
                        if i == 2:
                            pe.wait_ge(S["dsf_done"], 1)
                            pe.matmul(PS[:, 7, 0:B * NPH], tri[:, :], fl(dsp), start=True, stop=False)
                            pe.matmul(PS[:, 7, 0:B * NPH], ones[:, :], fl(dsf), start=False, stop=True)\
                                .then_inc(S["dsum_mm"], 1)
                    def out_part(i, j, ks, first, last):
                        n = N0 + KS + i
                        if first:
                            pe.wait_ge(w_ready, n + 3)
                        if i >= 1 and first:
                            pe.wait_ge(S[f"u{j}_free"], KS + i)
                        for k in ks:
                            for a, (x, y) in enumerate(((wh, hh), (wh, hl), (wl, hh))):
                                for h in range(2):
                                    ins = pe.matmul(PS[:, 2 * j + h, 0:H2],
                                                    x[:, n % 2, (j * KB + k) * P:(j * KB + k + 1) * P],
                                                    y[:, k, h * H2:(h + 1) * H2], start=first and k == ks[0] and a == 0,
                                                    stop=last and k == ks[-1] and a == 2)
                        if last:
                            ins.then_inc(S["u0_mm"] if j == 0 else w_used, 1)

                    pe.wait_ge(S["t_done"], NH)
                    pe.wait_ge(S["orow_in"], 16 * B)
                    for j in range(NB):
                        ins = pe.transpose(PS[:, 5, j * B:(j + 1) * B], qrow[:, j * P:(j + 1) * P], ident[0:B, 0:B])
                    ins.then_inc(S["os_tr"], 1)

                    pe.wait_ge(S["pv_lo"], NH // 2)
                    pe.wait_ge(S["mix_lo"], 1)
                    out_part(0, 1, range(CB, KB), True, False)
                    pe.wait_ge(S["ln_sd"], 1)
                    out_part(0, 0, range(CB, KB), True, False)
                    pe.wait_ge(S["mix_lo"], 1 + CB)
                    out_part(0, 0, range(CB), False, True)
                    out_part(0, 1, range(CB), False, True)
                    for i in range(1, 4):
                        for j in range(2):
                            out_part(i, j, range(KB), True, True)

                @block.scalar
                def _(act):
                    z_ps = PS[:, 0:3, :].rearrange("p b c -> p (b c)")[:, 0:W]
                    norm_root(act, 1, 4)
                    for i in range(KS):
                        hi_static(act, N0 + i + 1)
                        if i == QS:
                            act.wait_ge(S["qrow_tr"], 1)
                            act.activation(qrow[:, :], PS[0:B, 6, :], ACT.Copy).then_inc(S["qrow_cp"], 1)
                        if QS <= i < QS + CB:
                            act.wait_ge(S["u0_free"], i + 1)
                            act.activation(vbuf[:, 0, :], vbuf[:, 0, :], ACT.Sigmoid).then_inc(S["gate_sig"], 1)
                        if i == 9:
                            for k in range(2):
                                act.wait_ge(S["v_tr"], k + 1)
                                act.activation(vtok[:, :, k * P:(k + 1) * P],
                                               PS[:, 4 + k % 2, :].rearrange("p (t c) -> p t c", t=NTT), ACT.Copy)\
                                    .then_inc(S["v_cp"], 1)
                        for b in between(i) + after(i):
                            act.wait_ge(S["qb_mm"], b + 1)
                            if b >= 2:
                                act.wait_ge(S["prod_done"], (b - 1) * NPG)
                            act.activation(qb[:, b % 2, :], PS[:, 7, :], ACT.Copy).then_inc(S["qb_cp"], 1)
                    for k in range(2, NB):
                        act.wait_ge(S["v_tr"], k + 1)
                        act.activation(vtok[:, :, k * P:(k + 1) * P],
                                       PS[:, 4 + k % 2, :].rearrange("p (t c) -> p t c", t=NTT), ACT.Copy)\
                            .then_inc(S["v_cp"], 1)
                    act.activation(vrow, PS[0:B, 6, :], ACT.Copy).then_inc(S["row_cp"], 1)
                    act.preload_act_table_set("natural_log_exp_and_others")
                    act.wait_ge(S["small_in"], 32)
                    act.wait_ge(S["prod_done"], B * NPG)

                    taps = [0]

                    def tap(n):
                        for _ in range(n):
                            w = taps[0]
                            if w == CW:
                                return
                            taps[0] += 1
                            src, col = uA[:, LC, w:w + T], w * CB + LC
                            if w == 0:
                                act.activation(cbuf[:, LC, 0:T], src, ACT.Identity, scale=cwv[:, col:col + 1],
                                               bias=vec[:, V_CB + LC:V_CB + LC + 1]).then_inc(S["tap_done"], 1)
                                continue
                            if w == 1:
                                act.wait_ge(S["prod_free"], B * NPG)
                            if w >= 3:
                                act.wait_ge(S["tap_add"], w - 2)
                            act.activation(prod[:, w % 2, :], src, ACT.Copy, scale=cwv[:, col:col + 1])\
                                .then_inc(S["tap_done"], 1)

                    def row_out(b):
                        act.wait_ge(S["dpv_mm"], (b + 1) * NPG)
                        q = 32 * (b % 3)
                        act.activation(orow[b // 3][q:q + 1, :], PS[q:q + 1, 7, :], ACT.Copy).then_inc(S["orow_cp"], 1)

                    def front(h):
                        if h >= NSP:
                            act.wait_ge(S["pv_mm"], h - NSP + 1)
                        act.wait_ge(S["z_mm"], h + 1)
                        s = sp_[:, h % NSP, :]
                        act.activation(s, z_ps, ACT.Abs, scale=SCALE, bias=biasb[:, h:h + 1])\
                            .then_inc(S["abs_done"], 1)
                        act.wait_ge(S["abs_done"], h + 1)
                        act.activation(s, s, ACT.Exp, scale=-1.0).then_inc(S["e_done"], 1)
                        act.wait_ge(S["e_done"], h + 1)
                        act.activation(s, s, ACT.Ln, bias=1.0).then_inc(S["lnp_done"], 1)
                        if h >= 1:
                            tap(5)
                            act.wait_ge(S["t_done"], h)
                        act.activation(zc[:, :], z_ps, ACT.Identity, scale=SCALE, bias=biasb[:, h:h + 1])\
                            .then_inc(S["z_cp"], 1)

                    for i in range(NH + 2):
                        if i == 3:
                            act.wait_ge(S["dt_done"], 1)
                            act.wait_ge(S["dsum_mm"], 1)
                            act.activation(fl(dz), fl(dz), ACT.Exp).then_inc(S["dw_exp"], 1)
                        if i == 0:
                            front(i)
                        if i <= 1:
                            for m in range(i * len(MISC) // 2, (i + 1) * len(MISC) // 2):
                                kind, t = MISC[m]
                                act.wait_ge(S["misc_tr"], m + 1)
                                dst, rows = {"k": (ktok[:, t, :], P), "tail": (tl, PADW + B), "krow": (krow, B)}[kind]
                                act.activation(dst, PS[0:rows, 6 + m % 2, :], ACT.Copy).then_inc(S["misc_cp"], 1)
                        if 1 <= i < NH:
                            front(i)
                        if i == 0:
                            act.wait_ge(S["dscore"], 1)
                            act.activation(fl(dsp), fl(dz), ACT.Abs).then_inc(S["dabs"], 1)
                            act.wait_ge(S["dabs"], 1)
                            act.activation(fl(dsp), fl(dsp), ACT.Exp, scale=-1.0).then_inc(S["de"], 1)
                            act.wait_ge(S["de"], 1)
                            act.activation(fl(dsp), fl(dsp), ACT.Ln, bias=1.0).then_inc(S["dlnp"], 1)
                        if i == 0:
                            tap(2)
                        if 1 <= i <= NH:
                            act.wait_ge(S["t_done"], i)
                            w = sp_[:, (i - 1) % NSP, :]
                            act.activation(w, w, ACT.Exp).then_inc(S["w_exp"], 1)
                        if i >= 3 and i % 2 == 1:
                            pair = (i - 3) // 2
                            act.wait_ge(S["pv_mm"], 2 * pair + 2)
                            act.activation(hh[:, CB + pair, 0:T], PS[:, 6, :], ACT.Copy)\
                                .then_inc(S["pv_hi"], 1)
                        if i == 4:
                            hi_static(act, N0 + KS + 1)
                        for b in range(B):
                            if vstart(i - 1) < (b + 1) * NPG <= vstart(i):
                                row_out(b)
                        if i == NH:
                            for k in range(CB):
                                if k == 2:
                                    act.wait_ge(S["pv_mm"], NH - 2)
                                act.wait_ge(S["ln_cc"], k + 1)
                                act.activation(lnsq(k), cbuf[:, k, :], ACT.Square).then_inc(S["ln_sq"], 1)
                    row_out(B - 1)
                    act.wait_ge(S["os_tr"], 1)
                    act.activation(hh[:, CB:CB + NB, T:NT], sample_out, ACT.Copy).then_inc(S["os_hi"], 1)
                    act.wait_ge(S["ln_var"], 1)
                    act.activation(halves(sdev[:, :]), PS[:, 0:2, 0:H2], ACT.Sqrt, bias=epst[:, 0:1])\
                        .then_inc(S["ln_sd"], 1)
                    for k in range(CB):
                        act.wait_ge(S["ln_cn"], k + 1)
                        act.activation(cbuf[:, k, :], cbuf[:, k, :], ACT.Silu, bias=vec[:, V_LB + k:V_LB + k + 1])\
                            .then_inc(S["ln_act"], 1)
                        act.wait_ge(S["ln_act"], k + 1)
                        act.activation(hh[:, k, :], cbuf[:, k, :], ACT.Copy).then_inc(S["ln_hi"], 1)
                    for i in range(1, 4):
                        hi_static(act, N0 + KS + i + 1)
                    act.wait_ge(w_used, N0 + NS_A + 2)
                    for k in range(KB):
                        act.wait_ge(S[f"u{k % 2}_free"], KS + k // 2 + 1)
                        norm_split_hi(act, V_NORM[FFN_W[1]], k)

                @block.vector
                def _(dve):
                    ch = Chain(dve, S["d_chain"])

                    def conv_step(c, w):
                        out, col = cbuf[:, c, 0:T], cwv[:, w * CB + c:w * CB + c + 1]
                        if w == 0:
                            ch(dve.tensor_scalar(out, uA[:, c, w:w + T], col, vec[:, V_CB + c:V_CB + c + 1],
                                                 ALU.mult, ALU.add))
                        else:
                            ch(dve.scalar_tensor_tensor(out=out, in0=uA[:, c, w:w + T], scalar=col, in1=out,
                                                        op0=ALU.mult, op1=ALU.add))

                    def conv_sample(c):
                        col = cwv[:, c:CW * CB:CB].rearrange("p (a w) -> p a w", a=1).to_broadcast([P, B, CW])
                        ch(dve.tensor_tensor(uS[:, c, :, :], uS[:, c, :, :], col, ALU.mult))
                        ch(dve.tensor_reduce(csum[:, c, :], uS[:, c, :, :], AX.X, ALU.add))
                        ch(dve.tensor_scalar(cbuf[:, c, T:NT], csum[:, c, :], vec[:, V_CB + c:V_CB + c + 1], None,
                                             ALU.add))

                    pos = [0]

                    def conv(n):
                        for _ in range(n):
                            if pos[0] == LC * CW:
                                return
                            c, w = divmod(pos[0], CW)
                            conv_step(c, w)
                            pos[0] += 1

                    def reduce(i):
                        dve.wait_ge(S["prod_done"], i + 1)
                        b, pg = divmod(i, NPG)
                        dve.tensor_reduce(dz[:, b, pg, :], prod[:, i % 2, :].rearrange("p (h e) -> p h e", h=NH),
                                          AX.X, ALU.add).then_inc(S["prod_free"], 1)

                    def evacuate(i, j):
                        if j == 0:
                            dve.wait_ge(S["u0_mm"], i + 1)
                        else:
                            dve.wait_ge(w_used, N0 + i + 3)
                        if QS <= i < QS + CB:
                            dst = vbuf[:, 0, :] if j == 0 else uA[:, i - QS, PADW:UW]
                            if i > QS and j == 0:
                                dve.wait_ge(S["u_done"], i - QS)
                        elif i < QS:
                            dst = qT[:, 2 * i + j, :]
                        elif i < 8:
                            dst = kT[:, 2 * (i - 6) + j, :]
                        else:
                            dst = vbuf[:, j, :]
                            if i == 9:
                                dve.wait_ge(S["v_tr"], j + 1)
                        dve.tensor_tensor(halves(dst), PS[:, 2 * j:2 * j + 2, 0:H2], halves(rstd[:, :]), ALU.mult)\
                            .then_inc(S[f"u{j}_free"], 1)

                    def diagonal(a):
                        ms = qmask[:, :].rearrange("p (a c) -> p a c", a=1).to_broadcast([P, 2, P])
                        for t in (a[:, 0:KO[2]].rearrange("p (a c) -> p a c", a=2)[:, :, 0:P],
                                  a[:, KO[3]:KO[3] + 2 * P].rearrange("p (a c) -> p a c", a=2)):
                            ins = dve.tensor_tensor(t, t, ms, ALU.mult)
                        return ins

                    norm_rstd(dve, 1)
                    for i in range(KS):
                        lo_static(dve, N0 + i + 1)
                        c = i - QS
                        if i == 0:
                            dve.wait_ge(S["tr_done"], 1)
                            hb = B // 2
                            for r in range(2):
                                for k in range(CB):
                                    ins = dve.tensor_copy(uS[:, k, r * hb:(r + 1) * hb, 0:PADW],
                                                          PS[:, 6 + r, k * P:k * P + cst_rows]
                                                          .rearrange("p (b w) -> p b w", b=hb))
                            ins.then_inc(S["cp_done"], 1)
                            dve.wait_ge(S["cp_done"], 1)
                            dve.wait_ge(S["masks"], 5)
                        for r in range(max(REDUCES)):
                            if i >= ES and r < REDUCES[i - ES]:
                                reduce(sum(REDUCES[:i - ES]) + r)
                            if r == 2:
                                evacuate(i, 0)
                            if r == 7:
                                evacuate(i, 1)
                                if 0 <= c < CB:
                                    dve.wait_ge(S["u1_free"], i + 1)
                                    dve.wait_ge(S["gate_sig"], c + 1)
                                    dve.tensor_tensor(uA[:, c, PADW:UW], uA[:, c, PADW:UW], vbuf[:, 0, :], ALU.mult)\
                                        .then_inc(S["u_done"], 1)
                                    dve.wait_ge(S["u_done"], c + 1)
                                    ch(dve.tensor_copy(uS[:, c, :, PADW], uA[:, c, PADW + T:UW]))
                                    conv_sample(c)

                    for i in range(NH + 2):
                        if i == 0:
                            bb = biasb[:, :].rearrange("p (a h) -> p a h", a=1).to_broadcast([P, B * NPG, NH])
                            dve.wait_ge(S["small_in"], 32)
                            dve.wait_ge(S["prod_free"], B * NPG)
                            dve.scalar_tensor_tensor(out=fl3(dz), in0=fl3(dz), scalar=SCALE, in1=bb, op0=ALU.mult,
                                                     op1=ALU.add).then_inc(S["dscore"], 1)
                            dve.wait_ge(S["dscore"], 1)
                        conv(12)
                        if 1 <= i <= NH:
                            dve.wait_ge(S["sum_mm"], i)
                            dve.tensor_tensor(sp_[:, (i - 1) % NSP, :], zc[:, :],
                                              PS[:, 3:6, :].rearrange("p b c -> p (b c)")[:, 0:W],
                                              ALU.subtract).then_inc(S["t_done"], 1)
                        if i < NH:
                            s = sp_[:, i % NSP, :]
                            dve.wait_ge(S["lnp_done"], i + 1)
                            dve.wait_ge(S["z_cp"], i + 1)
                            dve.scalar_tensor_tensor(out=s, in0=zc[:, :], scalar=0.0, in1=s, op0=ALU.max, op1=ALU.add)\
                                .then_inc(S["sp_max"], 1)
                            dve.wait_ge(S["sp_max"], i + 1)
                            diagonal(s).then_inc(S["sp_done"], 1)
                        if i == 1:
                            dve.wait_ge(S["dlnp"], 1)
                            ch(dve.scalar_tensor_tensor(out=fl(dsp), in0=fl(dz), scalar=0.0, in1=fl(dsp), op0=ALU.max,
                                                        op1=ALU.add))
                            ch(dve.memset(dsf[:, :, NPG - 1, :], 0.0))
                            for pg in range(NPG - 2, -1, -1):
                                ins = dve.tensor_tensor(dsf[:, :, pg, :], dsf[:, :, pg + 1, :], dsp[:, :, pg + 1, :],
                                                        ALU.add)
                                if pg:
                                    ch(ins)
                            ins.then_inc(S["dsf_done"], 1)
                        if 1 <= i <= NH:
                            dve.wait_ge(S["w_exp"], i)
                            diagonal(sp_[:, (i - 1) % NSP, :]).then_inc(S["w_mask"], 1)
                        if i == 2:
                            dve.wait_ge(S["dsum_mm"], 1)
                            dve.tensor_tensor(fl(dz), fl(dz), PS[:, 7, 0:B * NPH], ALU.subtract)\
                                .then_inc(S["dt_done"], 1)
                        if i >= 3 and i % 2 == 1:
                            pair = (i - 3) // 2
                            dve.wait_ge(S["pv_hi"], pair + 1)
                            dve.tensor_tensor(hl[:, CB + pair, 0:T], PS[:, 6, :],
                                              hh[:, CB + pair, 0:T].bitcast(F32), ALU.subtract)\
                                .then_inc(S["pv_lo"], 1)
                        if i == 4:
                            lo_static(dve, N0 + KS + 1)
                        if i == NH - 1:
                            conv(LC * CW)
                            dve.sem_inc(S["conv_done"], 1)
                        if i == NH:
                            dve.wait_ge(S["ln_ms"], 1)
                            for k in range(CB):
                                dve.tensor_tensor(halves(cbuf[:, k, :]), halves(cbuf[:, k, :]), PS[:, 0:2, 0:H2],
                                                  ALU.subtract).then_inc(S["ln_cc"], 1)
                    dve.wait_ge(S["os_hi"], 1)
                    dve.tensor_tensor(hl[:, CB:CB + NB, T:NT], sample_out,
                                      hh[:, CB:CB + NB, T:NT].bitcast(F32), ALU.subtract).then_inc(S["mix_lo"], 1)
                    dve.wait_ge(S["ln_sd"], 1)
                    ch(dve.reciprocal(rstd[:, :], sdev[:, :]))
                    for k in range(CB):
                        dve.wait_ge(S["ln_sq"], k + 1)
                        dve.scalar_tensor_tensor(out=cbuf[:, k, :], in0=cbuf[:, k, :],
                                                 scalar=vec[:, V_LG + k:V_LG + k + 1], in1=rstd[:, :],
                                                 op0=ALU.mult, op1=ALU.mult).then_inc(S["ln_cn"], 1)
                    for k in range(CB):
                        dve.wait_ge(S["ln_hi"], k + 1)
                        dve.tensor_tensor(hl[:, k, :], cbuf[:, k, :], hh[:, k, :].bitcast(F32), ALU.subtract)\
                            .then_inc(S["mix_lo"], 1)
                    for i in range(4):
                        n = N0 + KS + i
                        if i >= 1:
                            lo_static(dve, n + 1)
                        for j in range(2):
                            if j == 0:
                                dve.wait_ge(S["u0_mm"], KS + i + 1)
                            else:
                                dve.wait_ge(w_used, n + 3)
                            k = 2 * i + j
                            free = S[f"u{j}_free"]
                            dve.tensor_tensor(halves(xT[:, k, :]), halves(xT[:, k, :]), PS[:, 2 * j:2 * j + 2, 0:H2],
                                              ALU.add).then_inc(free, 1)
                    for k in range(KB):
                        dve.wait_ge(S[f"u{k % 2}_free"], KS + k // 2 + 1)
                        norm_split_lo(dve, 2, V_NORM[FFN_W[1]], k)
            nc.clear_and_free_semaphores(list(S.values()))

        def stage_m():
            N0 = N_M
            MT = MCW - 1
            NBX = MCD // P
            GC = GB * P
            TAIL = MT + B
            NR = 4
            NX = GB + 2
            with ExitStack() as st:
                zs = sb_in(st, "zs", [P, GB, NT])
                xraw = sb_in(st, "xraw", [P, 2, MT + NT])
                xwin = sb_in(st, "xwin", [P, 2, B, MCW])
                xcs = sb_in(st, "xcs", [P, 2, NX, NT])
                dtxe = sb_in(st, "dtxe", [P, 2, GC])
                btok = sb_in(st, "btok", [P, NTT, MN])
                cbT = sb_in(st, "cbT", [P, NTT, P])
                dec = sb_in(st, "dec", [P, 2, T])
                cdec = sb_in(st, "cdec", [P, 2, T - P])
                grs = sb_in(st, "grs", [P, NT])
                mst = sb_in(st, "mst", [P, NBX, B * MT])
                tails = sb_in(st, "tails", [P, NBX, TAIL])
                ms_b = sb_in(st, "ms_b", [P, NR, GB, MN])
                ms_t = sb_in(st, "ms_t", [P, 2, GB, MN])
                bcs = sb_in(st, "bcs", [P, 2, 2 * MN])
                bsr = sb_in(st, "bsr", [B, 2 * MN])
                xdt = sb_in(st, "xdt", [P, GB, B])
                ysm = sb_in(st, "ysm", [P, GB, B])
                exs = sb_in(st, "exs", [P, GB, 2 * B])
                dtT = dec[:, :, :].rearrange("p a c -> p (a c)")[0:MH, 0:NT]
                daT = cdec[:, :, :].rearrange("p a c -> p (a c)")[0:MH, 0:NT]
                acsT = sb_in(st, "acsT", [MH, T])
                smp = sb_in(st, "smp", [MH, 2 * B])
                hvec = sb_in(st, "hvec", [MH, 4])
                dcol = sb_in(st, "dcol", [P, MH // 2])
                ttok = sb_in(st, "ttok", [P, 2, NTT, MH])
                etot = sb_in(st, "etot", [P, NTT, MH])
                wend = sb_in(st, "wend", [P, NTT, MH])
                causal = sb_in(st, "causal", [P, P])
                hout = sb_in(st, "hout", [P, GB, MN])
                flat = xcs[:, 1, :, :].rearrange("p a c -> p (a c)")
                strows = flat[0:B * MT, 0:MCD]
                ttail = xcs[:, 0, :, :].rearrange("p a c -> p (a c)")[0:TAIL, 0:MCD]

                with ExitStack() as scan:
                    dtx = sb_in(scan, "dtx", [P, NTT, GC])
                    hT = sb_in(scan, "hT", [P, NTT, GC])
                yh = sb_in(st, "yh", [P, GB, NT], F32R)
                yl = sb_in(st, "yl", [P, GB, NT], F32R)

                names = ("st_in vec3_in masks st_tr st_cp u0_mm u0_free u1_free d_chain g_chain dt_b dt_nabs dt_lne "
                         "dt_lnp dt_done exa acs_done smp_exp tk_tr tk_cp tot_mm tot_e wend_e wend_done dcol_mm dcol_cp "
                         "tap0 conv_done silu_done z_done xt_tr dtx_done bt_tr bt_cp cb_mm cb_done s_mm s_done "
                         "head_bc dec_arg dec_exp dec_cb cdec_e cdec_c y_mm y_done exs_mm exs_cp bcs_mm bcs_cp "
                         "xdt_done ms0 ms1 ms2 ms3 ms_new ms_prod ms_y ms_st0 ms_st1 ms_st2 ms_st3 ysq_done yms_done "
                         "ysd_done yh_done yl_done gated ho_tr ho_cp ho_st t_tr t_cp uo_mm h_scaled x_final").split()
                S = {n: sem("m_" + n) for n in names}
                block = st.enter_context(nc.Block())

                def z_slot(g, q):
                    return 4 + 7 * g + q

                def x_slot(g, q):
                    return 1 + q if g == 0 else 4 + 7 * (g - 1) + 2 + q

                def o_slot(g, q):
                    return 4 + 7 * g + (5 if g + 1 < MG else 2) + q

                def table_units(g):
                    return [("z", g, q, j) for q in range(2 if g + 1 < MG else 1) for j in range(2)]

                def head_unit(g, hd):
                    if g + 1 < MG:
                        k = {0: 0, 1: 1, 3: 2, 4: 3, 6: 4, 7: 5}.get(hd)
                        return None if k is None else ("x", g + 1, k // 2, k % 2)
                    k = {4: 0, 7: 1}.get(hd)
                    return None if k is None else ("z", g, 1, k)

                def slot_of(unit):
                    kind, g, q, _ = unit
                    return (z_slot if kind == "z" else x_slot)(g, q)

                def frees(n, j, turn=0):
                    return (1 - j if n >= 1 else 0) + max(n - 1, 0) + turn \
                        + sum(1 for g in range(MG) for q in range(2) if o_slot(g, q) < n)

                def u0s(n):
                    return sum(1 for g in range(MG) for q in range(3) if x_slot(g, q) < n) \
                        + sum(1 for g in range(MG) for q in range(2) if z_slot(g, q) < n)

                def conv_block(g, k):
                    return g * GB + k if k < GB else MDI // P + g + (k - GB) * MG

                def ssm(ap, g):
                    return ap[g * HPG:(g + 1) * HPG].rearrange("h q n -> (h q) n").rearrange("(j p) n -> p j n", p=P)

                byh = lambda a: a.rearrange("p (h q) -> p h q", h=HPG)
                perh = lambda a: a.rearrange("p (h a) -> p h a", a=1).to_broadcast([P, HPG, MP])

                @block.sync
                def _(sp):
                    sp.dma_start(strows, d["state_mamba_conv"][0].rearrange("b w c -> (b w) c"))\
                        .then_inc(S["st_in"], 16)
                    for i, name in enumerate(("m_dt_bias", "m_A_log", "m_D")):
                        sp.dma_start(hvec[:, i:i + 1], d[name].rearrange("l h -> h l")).then_inc(S["vec3_in"], 16)
                    sp.dma_start(o[10][0, :, 0:MT - 1, :], d["state_mamba_conv"][0][:, 1:MT, :]).then_inc(stored, 16)
                    n_stores[0] += 1

                    def load_state(k):
                        if k >= NR:
                            sp.wait_ge(S[f"ms_st{k % NR}"], 16 * (k // NR))
                            sp.wait_ge(S["ms_prod"], k - NR + 1)
                        sp.dma_start(ms_b[:, k % NR, :, :], ssm(d["state_ssm"][0, k % B], k // B))\
                            .then_inc(S[f"ms{k % NR}"], 16)

                    def ahead(n):
                        load_static(sp, N0 + n + 2)

                    for k in range(NR - 1):
                        load_state(k)
                    for n in range(4):
                        ahead(n)
                    for g in range(MG):
                        for unit in table_units(g):
                            if unit[3] == 0:
                                ahead(slot_of(unit))
                        for hd in range(HPG):
                            k = g * B + hd
                            unit = head_unit(g, hd)
                            if unit and unit[3] == 0:
                                ahead(slot_of(unit))
                            sp.wait_ge(S["ms_new"], k + 1)
                            sp.dma_start(ssm(o[11][0, hd], g), ms_b[:, k % NR, :, :]).then_inc(S[f"ms_st{k % NR}"], 16)
                            if k + NR - 1 < MG * B:
                                load_state(k + NR - 1)
                        sp.wait_ge(S["ho_cp"], g + 1)
                        sp.dma_start(ssm(o[6][0, 0], g), hout[:, :, :]).then_inc(S["ho_st"], 16)
                        for q in range(2):
                            ahead(o_slot(g, q))
                    sp.wait_ge(S["t_cp"], NBX // 4)
                    sp.dma_start(o[5][0, 0], ttail[0:MT, :]).then_inc(stored, 16)
                    sp.dma_start(o[10][0, :, MT - 1, :], ttail[MT:TAIL, :]).then_inc(stored, 16)
                    n_stores[0] += 2
                    sp.wait_ge(stored, 16 * n_stores[0])
                    sp.wait_ge(S["ho_st"], 16 * MG)
                    for i in range(NR):
                        sp.wait_ge(S[f"ms_st{i}"], 16 * MG * B // NR)

                @block.gpsimd
                def _(pool):
                    pool.memset(causal[:, :], 1.0).then_inc(S["masks"], 1)
                    pool.memset(xraw[:, :, 0:MT], 0.0).then_inc(S["masks"], 1)
                    pool.wait_ge(S["masks"], 1)
                    pool.affine_select(out=causal[:, :], in_=causal[:, :], compare_op=ALU.is_ge, fill=0.0, base=0,
                                       pattern=[[1, P]], channel_multiplier=-1).then_inc(S["masks"], 1)
                    col = lambda a, c: a[:, :, c:c + 1].to_broadcast([P, GB, MN])
                    for k in range(MG * B):
                        g, b = divmod(k, B)
                        s, t = ms_b[:, k % NR, :, :], ms_t[:, k % 2, :, :]
                        bc, cc = (bcs[:, k % 2, j * MN:(j + 1) * MN].rearrange("p (a n) -> p a n", a=1)
                                  .to_broadcast([P, GB, MN]) for j in range(2))
                        pool.wait_ge(S["xdt_done"], g + 1)
                        pool.wait_ge(S["bcs_cp"], k + 1)
                        if k >= 2:
                            pool.wait_ge(S["ms_y"], k - 1)
                        pool.tensor_tensor(t, col(xdt, b), bc, ALU.mult).then_inc(S["g_chain"], 1)
                        pool.wait_ge(S[f"ms{k % NR}"], 16 * (k // NR + 1))
                        pool.tensor_tensor(s, s, col(exs, B + b), ALU.mult).then_inc(S["g_chain"], 1)
                        pool.wait_ge(S["g_chain"], 2 * k + 2)
                        pool.tensor_tensor(s, s, t, ALU.add).then_inc(S["ms_new"], 1)
                        pool.wait_ge(S["ms_new"], k + 1)
                        pool.tensor_tensor(t, s, cc, ALU.mult).then_inc(S["ms_prod"], 1)
                    norm_zero(pool, 5)
                    for j in range(KB):
                        pool.wait_ge(S["x_final"], j + 1)
                        norm_sum(pool, 5, j)

                @block.tensor
                def _(pe):
                    def expand(out, h, rows):
                        for r in range(2):
                            ins = pe.matmul(out[r * MP:(r + 1) * MP, :],
                                            ident[0:MH, h + r:h + r + 1].to_broadcast([MH, MP]),
                                            rows, start=True, stop=True)
                        return ins

                    def project(unit):
                        n, j = slot_of(unit), unit[3]
                        if j == 0:
                            pe.wait_ge(w_ready, N0 + n + 3)
                        if frees(n, j) >= 1:
                            pe.wait_ge(S[f"u{j}_free"], frees(n, j))
                        ins = mm3(pe, [PS[:, 2 * j + h, 0:H2] for h in range(2)], lambda k: (j * KB + k) * P,
                                  (N0 + n) % 2, KB, hh, hl)
                        ins.then_inc(S["u0_mm"] if j == 0 else w_used, 1)

                    pe.wait_ge(w_ready, N0 + 3)
                    mm3(pe, [PS[0:MH, h, 0:H2] for h in range(2)], lambda k: k * MH, N0 % 2, KB, hh, hl, m=MH,
                        before=wait_h(pe, 4)).then_inc(w_used, 1)
                    norm_mean(pe, 4, 4)
                    pe.wait_ge(S["st_in"], 16)
                    r = B * MT
                    for c in range(NBX):
                        ins = pe.transpose(PS[:, 6 + c // 12, (c % 12) * r:(c % 12 + 1) * r],
                                           strows[:, c * P:(c + 1) * P], ident[0:r, 0:r])
                    ins.then_inc(S["st_tr"], 1)
                    project(("x", 0, 0, 0))
                    project(("x", 0, 0, 1))
                    pe.wait_ge(S["acs_done"], NTT)
                    pe.wait_ge(S["st_cp"], 2)
                    for j, src in enumerate((dtT, acsT)):
                        for t in range(NTT):
                            ins = pe.transpose(PS[:, 4, (j * NTT + t) * MH:(j * NTT + t + 1) * MH],
                                               src[:, t * P:(t + 1) * P], ident[0:MH, 0:MH])
                    ins.then_inc(S["tk_tr"], 1)
                    pe.wait_ge(S["vec3_in"], 48)
                    for j in range(MH // 2):
                        ins = expand(PS[:, 6, j:j + 1], 2 * j, hvec[:, 2:3])
                    ins.then_inc(S["dcol_mm"], 1)
                    project(("x", 0, 1, 0))
                    pe.wait_ge(S["tk_cp"], 1)
                    pe.matmul(PS[:, 5, 0:NTT * MH], ident[:, P - 1:P].to_broadcast([P, P]),
                              ttok[:, 1, :, :].rearrange("p t h -> p (t h)"), start=True, stop=True)\
                        .then_inc(S["tot_mm"], 1)
                    project(("x", 0, 1, 1))
                    project(("x", 0, 2, 0))
                    project(("x", 0, 2, 1))

                    def head_bc(g, hd):
                        i = g * HPG + hd
                        if hd >= 2:
                            pe.wait_ge(S["dec_arg"], i - 1)
                            pe.wait_ge(S["cdec_e"], i - 1)
                        pe.matmul(PS[:, 4 + hd % 2, :], ident[0:MH, i:i + 1].to_broadcast([MH, P]), acsT[:, :],
                                  start=True, stop=True).then_inc(S["head_bc"], 1)

                    def sample_bc(g, b):
                        if b >= 1:
                            pe.wait_ge(S["bcs_cp"], g * B + b)
                        pe.matmul(PS[:, 6, 0:2 * MN], ident[0:B, b:b + 1].to_broadcast([B, P]), bsr[:, :],
                                  start=True, stop=True).then_inc(S["bcs_mm"], 1)

                    for g in range(MG):
                        xc = xcs[:, g % 2, :, :]
                        units = table_units(g)

                        def between(k):
                            if k < len(units):
                                project(units[k])

                        def x_tokens(t):
                            if t >= 2:
                                pe.wait_ge(S["dtx_done"], g * NTT + t - 1)
                            for c in range(GB):
                                ins = pe.transpose(PS[:, 4 + t % 2, c * P:(c + 1) * P], xc[:, c, t * P:(t + 1) * P],
                                                   ident[:, :])
                            ins.then_inc(S["xt_tr"], 1)

                        def chunk_state(t):
                            pe.wait_ge(S["dtx_done"], g * NTT + t + 1)
                            if t >= 2:
                                pe.wait_ge(S["s_done"], g * NTT + t - 1)
                            pe.matmul(PS[:, 6 + t % 2, 0:GC], btok[:, t, :], dtxe[:, t % 2, :], start=True,
                                      stop=True).then_inc(S["s_mm"], 1)

                        if g == 0:
                            between(0)
                        pe.wait_ge(S["silu_done"], NX * (g + 1))
                        if g >= 1:
                            pe.wait_ge(S["ysd_done"], g)
                            pe.wait_ge(S["ho_cp"], g)
                        else:
                            pe.wait_ge(S["wend_done"], 1)
                            pe.wait_ge(S["dcol_cp"], 1)
                        for t in range(NTT):
                            ins = pe.transpose(PS[:, 6, t * P:(t + 1) * P], xc[:, GB, t * P:(t + 1) * P], ident[:, :])
                        ins.then_inc(S["bt_tr"], 1)
                        for t in range(NTT):
                            ins = pe.matmul(PS[:, 7, t * P:(t + 1) * P], xc[:, GB, t * P:(t + 1) * P],
                                            xc[:, GB + 1, t * P:(t + 1) * P], start=True, stop=True)
                        ins.then_inc(S["cb_mm"], 1)
                        x_tokens(0)
                        x_tokens(1)
                        if g >= 1:
                            between(0)
                        pe.wait_ge(S["bt_cp"], g + 1)
                        chunk_state(0)
                        pe.wait_ge(S["cb_done"], g + 1)
                        chunk_state(1)
                        x_tokens(2)
                        x_tokens(3)
                        between(1)
                        chunk_state(2)
                        chunk_state(3)
                        between(2)
                        pe.wait_ge(S["s_done"], (g + 1) * NTT)
                        for j in range(2):
                            ins = pe.transpose(PS[0:B, 6, j * MN:(j + 1) * MN], xc[:, GB + j, T:NT], ident[:, :])
                        pe.wait_ge(S["smp_exp"], 1)
                        for j in range(GB):
                            ins = expand(PS[:, 6, 2 * MN + j * 2 * B:2 * MN + (j + 1) * 2 * B], g * HPG + 2 * j,
                                         smp[:, :])
                        ins.then_inc(S["exs_mm"], 1)
                        head_bc(g, 0)
                        head_bc(g, 1)
                        between(3)
                        pe.wait_ge(S["exs_cp"], g + 1)
                        sample_bc(g, 0)
                        for hd in range(HPG):
                            i = g * HPG + hd
                            if hd + 2 < HPG:
                                head_bc(g, hd + 2)
                            if hd % 2 == 0 and hd >= 2:
                                pe.wait_ge(S["y_done"], 4 * g + hd // 2)
                            pe.wait_ge(S["dec_cb"], i + 1)
                            pe.wait_ge(S["cdec_c"], i + 1)
                            r = MP * (hd % 2)
                            for t in range(NTT):
                                out = PS[r:r + MP, 7, t * P:(t + 1) * P]
                                ins = pe.matmul(out, dtx[:, t, hd * MP:(hd + 1) * MP], dec[:, i % 2, t * P:(t + 1) * P],
                                                start=True, stop=t == 0)
                                if t >= 1:
                                    ins = pe.matmul(out, hT[:, t - 1, hd * MP:(hd + 1) * MP],
                                                    cdec[:, i % 2, (t - 1) * P:t * P], start=False, stop=True)
                            ins.then_inc(S["y_mm"], 1)
                            if hd + 1 < B:
                                sample_bc(g, hd + 1)
                            if hd == HPG - 1:
                                pe.wait_ge(S["dec_arg"], (g + 1) * HPG)
                                pe.wait_ge(S["cdec_e"], (g + 1) * HPG)
                                for j in range(GB):
                                    ins = pe.transpose(PS[:, 5, j * P:(j + 1) * P], hT[:, NTT - 1, j * P:(j + 1) * P],
                                                       ident[:, :])
                                ins.then_inc(S["ho_tr"], 1)
                            unit = head_unit(g, hd)
                            if unit:
                                project(unit)
                        pe.wait_ge(S["bcs_cp"], (g + 1) * B)
                        pe.wait_ge(S["y_done"], 4 * (g + 1))
                        pe.wait_ge(S["ysq_done"], (g + 1) * (GB + 1))
                        for k in range(GB):
                            for half in range(2):
                                ins = pe.matmul(PS[:, 6 + half, 0:H2], mean_c[:, :],
                                                zs[:, k, half * H2:(half + 1) * H2], start=k == 0,
                                                stop=k == GB - 1)
                        ins.then_inc(S["yms_done"], 1)

                        def yl_in(k):
                            pe.wait_ge(S["yl_done"], g * GB + k + 1)

                        for q in range(2):
                            n = o_slot(g, q)
                            pe.wait_ge(w_ready, N0 + n + 3)
                            for j in range(4):
                                pe.wait_ge(S[f"u{j % 2}_free"], frees(n, j % 2, j // 2))
                                b = 2 * (j % 2)
                                ins = mm3(pe, [PS[:, b + h, 0:H2] for h in range(2)],
                                          lambda k: (k * 4 + j) * P, (N0 + n) % 2, GB, yh, yl,
                                          before=yl_in if q == 0 and j == 0 else None)
                                ins.then_inc(S["uo_mm"] if j < 3 else w_used, 1)
                    for q in range(NBX // 4):
                        if q >= 2:
                            pe.wait_ge(S["t_cp"], q - 1)
                        for c in range(4):
                            ins = pe.transpose(PS[0:TAIL, 4 + q % 2, c * P:(c + 1) * P], tails[:, 4 * q + c, :],
                                               ident[:, :])
                        ins.then_inc(S["t_tr"], 1)

                @block.scalar
                def _(act):
                    def first(unit):
                        kind, g, q, j = unit
                        if j == 0:
                            hi_static(act, N0 + slot_of(unit) + 1)
                        if kind == "x":
                            k = 2 * q + j
                            cb = conv_block(g, k)
                            act.wait_ge(S[f"u{j}_free"], frees(slot_of(unit), j) + 1)
                            act.activation(xcs[:, g % 2, k, 0:T], xraw[:, j, 0:T], ACT.Identity,
                                           scale=mwv[:, cb:cb + 1], bias=vec[:, V_MB + cb:V_MB + cb + 1])\
                                .then_inc(S["tap0"], 1)

                    def silu(unit):
                        kind, g, q, j = unit
                        if j == 0:
                            return
                        for k in (2 * q, 2 * q + 1):
                            if kind == "z":
                                act.wait_ge(S[f"u{k % 2}_free"], frees(slot_of(unit), k % 2) + 1)
                                act.activation(zs[:, k, :], zs[:, k, :], ACT.Silu).then_inc(S["z_done"], 1)
                            else:
                                act.wait_ge(S["conv_done"], g * NX + k + 1)
                                act.activation(xcs[:, g % 2, k, :], xcs[:, g % 2, k, :], ACT.Silu)\
                                    .then_inc(S["silu_done"], 1)

                    def both(unit):
                        first(unit)
                        silu(unit)

                    hi_static(act, N0 + 1)
                    norm_root(act, 4, 4)
                    act.wait_ge(S["vec3_in"], 48)
                    act.activation(hvec[:, 3:4], hvec[:, 1:2], ACT.Exp).then_inc(S["exa"], 1)
                    act.wait_ge(S["u0_free"], 1)
                    act.activation(daT[:, :], daT[:, :], ACT.Identity, bias=hvec[:, 0:1]).then_inc(S["dt_b"], 1)
                    act.wait_ge(S["dt_nabs"], 1)
                    act.activation(dtT[:, :], dtT[:, :], ACT.Exp).then_inc(S["dt_lne"], 1)
                    act.wait_ge(S["dt_lne"], 1)
                    act.activation(dtT[:, :], dtT[:, :], ACT.Ln, bias=1.0).then_inc(S["dt_lnp"], 1)
                    act.wait_ge(S["dt_done"], 2)
                    act.activation(smp[:, B:2 * B], daT[:, T:NT], ACT.Exp).then_inc(S["smp_exp"], 1)
                    both(("x", 0, 0, 0))
                    both(("x", 0, 0, 1))
                    both(("x", 0, 1, 0))
                    act.wait_ge(S["tot_mm"], 1)
                    act.activation(etot[:, :, :].rearrange("p t h -> p (t h)"), PS[:, 5, 0:NTT * MH], ACT.Exp)\
                        .then_inc(S["tot_e"], 1)
                    act.wait_ge(S["wend_e"], 1)
                    act.activation(wend[:, :, :], wend[:, :, :], ACT.Exp).then_inc(S["tot_e"], 1)
                    both(("x", 0, 1, 1))
                    both(("x", 0, 2, 0))
                    both(("x", 0, 2, 1))
                    for g in range(MG):
                        units = table_units(g)
                        if g == 0:
                            both(units[0])
                        act.wait_ge(S["bt_tr"], g + 1)
                        act.activation(btok[:, :, :], PS[:, 6, :].rearrange("p (t n) -> p t n", t=NTT), ACT.Copy)\
                            .then_inc(S["bt_cp"], 1)
                        for unit in units[int(g == 0):3]:
                            both(unit)
                        act.wait_ge(S["exs_mm"], g + 1)
                        act.activation(bsr[:, :], PS[0:B, 6, 0:2 * MN], ACT.Copy)
                        act.activation(exs[:, :, :], PS[:, 6, 2 * MN:2 * MN + GB * 2 * B]
                                       .rearrange("p (j c) -> p j c", j=GB), ACT.Copy).then_inc(S["exs_cp"], 1)

                        def decays(hd):
                            i = g * HPG + hd
                            act.wait_ge(S["dec_arg"], i + 1)
                            act.activation(dec[:, i % 2, :], dec[:, i % 2, :], ACT.Exp).then_inc(S["dec_exp"], 1)
                            if i >= 2:
                                act.wait_ge(S["y_mm"], i - 1)
                            act.activation(cdec[:, i % 2, :], PS[:, 4 + hd % 2, P:T], ACT.Exp).then_inc(S["cdec_e"], 1)

                        def gated_square(k):
                            act.wait_ge(S["gated"], g * (GB + 1) + k + 1)
                            act.activation(zs[:, k, 0:T], xcs[:, g % 2, k, 0:T], ACT.Square)\
                                .then_inc(S["ysq_done"], 1)

                        decays(0)
                        decays(1)
                        for unit in units[3:]:
                            both(unit)
                        for hd in range(HPG):
                            k = g * B + hd
                            act.wait_ge(S["bcs_mm"], k + 1)
                            if k >= 2:
                                act.wait_ge(S["ms_prod"], k - 1)
                            act.activation(bcs[:, k % 2, :], PS[:, 6, 0:2 * MN], ACT.Copy).then_inc(S["bcs_cp"], 1)
                            if hd + 2 < HPG:
                                decays(hd + 2)
                            unit = head_unit(g, hd)
                            if hd % 2 == 0 and hd >= 2 and g < MG - 1:
                                gated_square(hd // 2 - 1)
                            if hd >= 1 and head_unit(g, hd - 1):
                                silu(head_unit(g, hd - 1))
                            if unit and hd < HPG - 1:
                                first(unit)
                        act.wait_ge(S["ho_tr"], g + 1)
                        if g >= 1:
                            act.wait_ge(S["ho_st"], 16 * g)
                        act.activation(hout[:, :, :], PS[:, 5, :].rearrange("p (j n) -> p j n", j=GB), ACT.Copy)\
                            .then_inc(S["ho_cp"], 1)
                        last = head_unit(g, HPG - 1)
                        if last[0] == "z":
                            both(last)
                            for k in range(GB - 1):
                                gated_square(k)
                        gated_square(GB - 1)
                        act.wait_ge(S["gated"], (g + 1) * (GB + 1))
                        act.activation(zs[:, :, T:NT], xcs[:, g % 2, 0:GB, T:NT], ACT.Square)\
                            .then_inc(S["ysq_done"], 1)
                        for k in range(GB):
                            c = V_MN + g * GB + k
                            act.activation(yh[:, k, :], xcs[:, g % 2, k, :], ACT.Copy, scale=vec[:, c:c + 1])\
                                .then_inc(S["yh_done"], 1)
                        hi_static(act, N0 + o_slot(g, 0) + 1)
                        act.wait_ge(S["yms_done"], g + 1)
                        act.activation(halves(sdev[:, :]), PS[:, 6:8, 0:H2], ACT.Sqrt, bias=epst[:, 0:1])\
                            .then_inc(S["ysd_done"], 1)
                        if last[0] == "x":
                            both(last)
                        hi_static(act, N0 + o_slot(g, 1) + 1)
                        if g == MG - 1:
                            for k in range(KB):
                                act.wait_ge(S["x_final"], k + 1)
                                norm_split_hi(act, V_NORM[FFN_W[3]], k)

                @block.vector
                def _(dve):
                    ch = Chain(dve, S["d_chain"])

                    def evacuate(unit):
                        kind, g, q, j = unit
                        n = slot_of(unit)
                        if j == 0:
                            lo_static(dve, N0 + n + 1)
                            dve.wait_ge(S["u0_mm"], u0s(n) + 1)
                        else:
                            dve.wait_ge(w_used, N0 + n + 3)
                        ps = PS[:, 2 * j:2 * j + 2, 0:H2]
                        free = S[f"u{j}_free"]
                        k = 2 * q + j
                        if kind == "z":
                            if g >= 1:
                                dve.wait_ge(S["yms_done"], g)
                            dve.tensor_tensor(halves(zs[:, k, :]), ps, halves(rstd[:, :]), ALU.mult).then_inc(free, 1)
                            return
                        x = xraw[:, j, :]
                        dve.tensor_tensor(halves(x[:, MT:MT + NT]), ps, halves(rstd[:, :]), ALU.mult).then_inc(free, 1)

                    def conv(unit):
                        kind, g, q, j = unit
                        if kind == "z":
                            return
                        k = 2 * q + j
                        cb = conv_block(g, k)
                        x = xraw[:, j, :]
                        out = xcs[:, g % 2, k, :]
                        tap = lambda w: mwv[:, w * NBX + cb:w * NBX + cb + 1]
                        ch(dve.tensor_copy(xwin[:, j, :, 0:MT], mst[:, cb, :].rearrange("p (b w) -> p b w", b=B)))
                        dve.wait_ge(S[f"u{j}_free"], frees(slot_of(unit), j) + 1)
                        ch(dve.tensor_copy(xwin[:, j, :, MT], x[:, MT + T:MT + NT]))
                        dve.tensor_copy(tails[:, cb, :], x[:, T:T + TAIL])
                        ch(dve.tensor_scalar(out[:, T:NT], xwin[:, j, :, 0], tap(0), vec[:, V_MB + cb:V_MB + cb + 1],
                                             ALU.mult, ALU.add))
                        dve.wait_ge(S["tap0"], g * NX + k + 1)
                        for w in range(1, MCW):
                            for dst, src in ((out[:, 0:T], x[:, w:w + T]), (out[:, T:NT], xwin[:, j, :, w])):
                                ins = dve.scalar_tensor_tensor(out=dst, in0=src, scalar=tap(w), in1=dst,
                                                               op0=ALU.mult, op1=ALU.add)
                            if w < MCW - 1:
                                ch(ins)
                        ins.then_inc(S["conv_done"], 1)

                    lo_static(dve, N0 + 1)
                    norm_rstd(dve, 4)
                    dve.wait_ge(w_used, N0 + 3)
                    dve.tensor_tensor(halves(daT[:, :]), PS[0:MH, 0:2, 0:H2], halves(rstd[0:MH, :]), ALU.mult)\
                        .then_inc(S["u0_free"], 1)
                    r = B * MT
                    for i in range(2):
                        dve.wait_ge(S["st_tr"], 1)
                        dve.tensor_copy(mst[:, i * 12:(i + 1) * 12, :],
                                        PS[:, 6 + i, 0:12 * r].rearrange("p (c r) -> p c r", c=12))\
                            .then_inc(S["st_cp"], 1)
                    dve.wait_ge(S["st_cp"], 2)
                    dve.wait_ge(S["dt_b"], 1)
                    dve.scalar_tensor_tensor(out=dtT[:, :], in0=daT[:, :], scalar=-1.0, in1=daT[:, :], op0=ALU.mult,
                                             op1=ALU.min).then_inc(S["dt_nabs"], 1)
                    dve.wait_ge(S["dt_lnp"], 1)
                    dve.scalar_tensor_tensor(out=dtT[:, :], in0=daT[:, :], scalar=0.0, in1=dtT[:, :], op0=ALU.max,
                                             op1=ALU.add).then_inc(S["dt_done"], 1)
                    dve.wait_ge(S["exa"], 1)
                    dve.wait_ge(S["dt_done"], 1)
                    dve.tensor_scalar(daT[:, :], dtT[:, :], hvec[:, 3:4], -1.0, ALU.mult, ALU.mult)\
                        .then_inc(S["dt_done"], 1)
                    dve.wait_ge(S["dt_done"], 2)
                    for t in range(NTT):
                        c = slice(t * P, (t + 1) * P)
                        dve.tensor_tensor_scan(acsT[:, c], ones[0:MH, 0:P], daT[:, c], 0.0, ALU.mult, ALU.add)\
                            .then_inc(S["acs_done"], 1)
                    ch(dve.tensor_copy(smp[:, 0:B], dtT[:, T:NT]))
                    dve.wait_ge(S["masks"], 3)
                    evacuate(("x", 0, 0, 0))
                    conv(("x", 0, 0, 0))
                    evacuate(("x", 0, 0, 1))
                    conv(("x", 0, 0, 1))
                    dve.wait_ge(S["tk_tr"], 1)
                    dve.tensor_copy(ttok[:, :, :, :].rearrange("p a t h -> p (a t h)"), PS[:, 4, 0:2 * NTT * MH])\
                        .then_inc(S["tk_cp"], 1)
                    dve.wait_ge(S["dcol_mm"], 1)
                    dve.tensor_copy(dcol[:, :], PS[:, 6, 0:MH // 2]).then_inc(S["dcol_cp"], 1)
                    evacuate(("x", 0, 1, 0))
                    conv(("x", 0, 1, 0))
                    dve.wait_ge(S["tk_cp"], 1)
                    dve.wait_ge(S["tot_mm"], 1)
                    dve.wait_ge(S["tot_e"], 1)
                    dve.tensor_tensor(wend[:, :, :], PS[:, 5, 0:NTT * MH].rearrange("p (t h) -> p t h", t=NTT),
                                      ttok[:, 1, :, :], ALU.subtract).then_inc(S["wend_e"], 1)
                    evacuate(("x", 0, 1, 1))
                    conv(("x", 0, 1, 1))
                    dve.wait_ge(S["tot_e"], 2)
                    dve.tensor_tensor(wend[:, :, :], wend[:, :, :], ttok[:, 0, :, :], ALU.mult)\
                        .then_inc(S["wend_done"], 1)
                    evacuate(("x", 0, 2, 0))
                    conv(("x", 0, 2, 0))
                    evacuate(("x", 0, 2, 1))
                    conv(("x", 0, 2, 1))
                    dve.wait_ge(S["dcol_cp"], 1)
                    dve.wait_ge(S["wend_done"], 1)
                    for g in range(MG):
                        xc = xcs[:, g % 2, :, :]
                        units = table_units(g)
                        hs = slice(g * HPG, (g + 1) * HPG)

                        def between(k):
                            if k < len(units):
                                evacuate(units[k])

                        def dt_x(t):
                            i = g * NTT + t
                            dve.wait_ge(S["xt_tr"], i + 1)
                            ps = byh(PS[:, 4 + t % 2, :])
                            dve.tensor_tensor(byh(dtx[:, t, :]), ps, perh(ttok[:, 0, t, hs]), ALU.mult)
                            if t >= 2:
                                dve.wait_ge(S["s_mm"], i - 1)
                            dve.tensor_tensor(byh(dtxe[:, t % 2, :]), ps, perh(wend[:, t, hs]), ALU.mult)\
                                .then_inc(S["dtx_done"], 1)

                        def state(t):
                            i = g * NTT + t
                            dve.wait_ge(S["s_mm"], i + 1)
                            if t == 0:
                                dve.tensor_copy(hT[:, 0, :], PS[:, 6, 0:GC]).then_inc(S["s_done"], 1)
                                return
                            dve.wait_ge(S["s_done"], i)
                            dve.tensor_tensor(byh(hT[:, t, :]), byh(hT[:, t - 1, :]), perh(etot[:, t, hs]), ALU.mult)\
                                .then_inc(S["h_scaled"], 1)
                            dve.wait_ge(S["h_scaled"], g * (NTT - 1) + t)
                            dve.tensor_tensor(hT[:, t, :], hT[:, t, :], PS[:, 6 + t % 2, 0:GC], ALU.add)\
                                .then_inc(S["s_done"], 1)

                        if g == 0:
                            between(0)
                        dve.wait_ge(S["cb_mm"], g + 1)
                        dve.tensor_tensor(cbT[:, :, :], PS[:, 7, :].rearrange("p (t c) -> p t c", t=NTT),
                                          causal[:, :].rearrange("p (a c) -> p a c", a=1).to_broadcast([P, NTT, P]),
                                          ALU.mult).then_inc(S["cb_done"], 1)
                        dt_x(0)
                        dt_x(1)
                        if g >= 1:
                            between(0)
                        dt_x(2)
                        state(0)
                        dt_x(3)
                        state(1)
                        between(1)
                        state(2)
                        state(3)
                        between(2)
                        dve.wait_ge(S["exs_cp"], g + 1)
                        dve.tensor_tensor(xdt[:, :, :], xc[:, 0:GB, T:NT], exs[:, :, 0:B], ALU.mult)\
                            .then_inc(S["xdt_done"], 1)
                        dve.wait_ge(S["cb_done"], g + 1)

                        def decay_args(hd):
                            i = g * HPG + hd
                            dve.wait_ge(S["head_bc"], i + 1)
                            if i >= 2:
                                dve.wait_ge(S["y_mm"], i - 1)
                            for t in range(NTT):
                                ins = dve.tensor_scalar(dec[:, i % 2, t * P:(t + 1) * P],
                                                        PS[:, 4 + hd % 2, t * P:(t + 1) * P],
                                                        ttok[:, 1, t, i:i + 1], 0.0, ALU.subtract, ALU.min)
                            ins.then_inc(S["dec_arg"], 1)

                        def sample_y(b):
                            k = g * B + b
                            dve.wait_ge(S["ms_prod"], k + 1)
                            dve.tensor_reduce(ysm[:, :, b], ms_t[:, k % 2, :, :], AX.X, ALU.add)\
                                .then_inc(S["ms_y"], 1)

                        def pair_y(pair):
                            dve.wait_ge(S["y_mm"], g * HPG + 2 * pair + 2)
                            dve.scalar_tensor_tensor(out=xc[:, pair, 0:T], in0=xc[:, pair, 0:T],
                                                     scalar=dcol[:, g * GB + pair:g * GB + pair + 1],
                                                     in1=PS[:, 7, :], op0=ALU.mult, op1=ALU.add)\
                                .then_inc(S["y_done"], 1)

                        def gate(pair):
                            dve.wait_ge(S["z_done"], g * GB + pair + 1)
                            dve.wait_ge(S["y_done"], g * GB + pair + 1)
                            dve.tensor_tensor(xc[:, pair, 0:T], xc[:, pair, 0:T], zs[:, pair, 0:T], ALU.mult)\
                                .then_inc(S["gated"], 1)

                        def decays(hd):
                            i = g * HPG + hd
                            dve.wait_ge(S["dec_exp"], i + 1)
                            dve.tensor_tensor(dec[:, i % 2, :], dec[:, i % 2, :],
                                              cbT[:, :, :].rearrange("p t c -> p (t c)"), ALU.mult)\
                                .then_inc(S["dec_cb"], 1)
                            dve.wait_ge(S["cdec_e"], i + 1)
                            dve.tensor_tensor(cdec[:, i % 2, :], cdec[:, i % 2, :], xc[:, GB + 1, P:T],
                                              ALU.mult).then_inc(S["cdec_c"], 1)

                        decay_args(0)
                        decay_args(1)
                        decays(0)
                        between(3)
                        for hd in range(HPG):
                            if hd + 1 < HPG:
                                decays(hd + 1)
                            if hd % 2 == 1:
                                pair_y(hd // 2)
                            if hd + 2 < HPG:
                                decay_args(hd + 2)
                            if hd % 2 == 0 and hd >= 2 and g < MG - 1:
                                gate(hd // 2 - 1)
                            if hd >= 1 and head_unit(g, hd - 1):
                                conv(head_unit(g, hd - 1))
                            if hd >= 1:
                                sample_y(hd - 1)
                            unit = head_unit(g, hd)
                            if unit and hd < HPG - 1:
                                evacuate(unit)
                        if g < MG - 1:
                            gate(GB - 1)
                        last = head_unit(g, HPG - 1)
                        if last[0] == "z":
                            evacuate(last)
                            for k in range(GB):
                                gate(k)
                        sample_y(B - 1)
                        dcb = dcol[:, g * GB:(g + 1) * GB].rearrange("p (j a) -> p j a", a=1).to_broadcast([P, GB, B])
                        ch(dve.tensor_tensor(xc[:, 0:GB, T:NT], xc[:, 0:GB, T:NT], dcb, ALU.mult))
                        dve.wait_ge(S["ms_y"], (g + 1) * B)
                        ch(dve.tensor_tensor(xc[:, 0:GB, T:NT], xc[:, 0:GB, T:NT], ysm[:, :, :], ALU.add))
                        dve.tensor_tensor(xc[:, 0:GB, T:NT], xc[:, 0:GB, T:NT], zs[:, :, T:NT], ALU.mult)\
                            .then_inc(S["gated"], 1)
                        for k in range(GB):
                            dve.wait_ge(S["yh_done"], g * GB + k + 1)
                            c = V_MN + g * GB + k
                            dve.scalar_tensor_tensor(out=yl[:, k, :], in0=xc[:, k, :], scalar=vec[:, c:c + 1],
                                                     in1=yh[:, k, :].bitcast(F32), op0=ALU.mult, op1=ALU.subtract)\
                                .then_inc(S["yl_done"], 1)
                        if last[0] == "x":
                            evacuate(last)
                            conv(last)
                        lo_static(dve, N0 + o_slot(g, 0) + 1)
                        dve.wait_ge(S["ysd_done"], g + 1)
                        ch(dve.reciprocal(grs[:, :], sdev[:, :]))
                        for q in range(2):
                            n = o_slot(g, q)
                            if q == 1:
                                lo_static(dve, N0 + n + 1)
                            for j in range(4):
                                if j < 3:
                                    dve.wait_ge(S["uo_mm"], 6 * g + 3 * q + j + 1)
                                else:
                                    dve.wait_ge(w_used, N0 + n + 3)
                                k = 4 * q + j
                                b = 2 * (j % 2)
                                free, cnt = S[f"u{j % 2}_free"], frees(n, j % 2, j // 2) + 1
                                tmp = xraw[:, j % 2, MT:MT + NT]
                                dve.tensor_tensor(halves(tmp), PS[:, b:b + 2, 0:H2], halves(grs[:, :]), ALU.mult)\
                                    .then_inc(free, 1)
                                dve.wait_ge(free, cnt)
                                ins = dve.tensor_tensor(xT[:, k, :], xT[:, k, :], tmp, ALU.add)
                                if g < MG - 1:
                                    ch(ins)
                                    continue
                                ins.then_inc(S["x_final"], 1)
                                if k >= 1:
                                    norm_split_lo(dve, 5, V_NORM[FFN_W[3]], k - 1)
                    norm_split_lo(dve, 5, V_NORM[FFN_W[3]], KB - 1)
                    for q in range(NBX // 4):
                        dve.wait_ge(S["t_tr"], q + 1)
                        dve.tensor_copy(ttail[:, 4 * q * P:4 * (q + 1) * P], PS[0:TAIL, 4 + q % 2, :])\
                            .then_inc(S["t_cp"], 1)

        def stage_final():
            with ExitStack() as st:
                hf = sb_in(st, "hf", [P, KB, NT])
                yout = sb_in(st, "yout", [P, NTT + 1, DM])
                normed = sem("normed")
                out_tr = sem("out_tr")
                out_cp = sem("out_cp")
                block = st.enter_context(nc.Block())

                @block.scalar
                def _(act):
                    norm_root(act, 6, 4)

                @block.tensor
                def _(pe):
                    norm_mean(pe, 6, 4)
                    pe.wait_ge(normed, KB)
                    for t in range(NTT + 1):
                        if t >= 2:
                            pe.wait_ge(out_cp, t - 1)
                        b = 2 * (t % 2)
                        m = P if t < NTT else B
                        for k in range(KB):
                            ins = pe.transpose(PS[0:m, b + k // 4, (k % 4) * P:(k % 4 + 1) * P],
                                               hf[:, k, t * P:t * P + m], ident[:, :])
                        ins.then_inc(out_tr, 1)

                @block.vector
                def _(dve):
                    norm_rstd(dve, 6)
                    col = V_NORM[("final", 0)]
                    for k in range(KB):
                        dve.scalar_tensor_tensor(out=hf[:, k, :], in0=xT[:, k, :], scalar=vec[:, col + k:col + k + 1],
                                                 in1=rstd[:, :], op0=ALU.mult, op1=ALU.mult).then_inc(normed, 1)
                    for t in range(NTT + 1):
                        m = P if t < NTT else B
                        dve.wait_ge(out_tr, t + 1)
                        b = 2 * (t % 2)
                        dve.tensor_copy(yout[0:m, t, :].rearrange("p (b c) -> p b c", b=2), PS[0:m, b:b + 2, :])\
                            .then_inc(out_cp, 1)

                @block.sync
                def _(sp):
                    for t in range(NTT + 1):
                        sp.wait_ge(out_cp, t + 1)
                        if t < NTT:
                            sp.dma_start(o[0][0, t * P:(t + 1) * P, :], yout[:, t, :]).then_inc(stored, 16)
                        else:
                            sp.dma_start(o[1].rearrange("b t c -> (b t) c"), yout[0:B, t, :]).then_inc(stored, 16)
                        n_stores[0] += 1
                    sp.wait_ge(stored, 16 * n_stores[0])

        stage_setup()
        stage_ffn(0)
        stage_a()
        stage_ffn(1)
        stage_ffn(2)
        stage_m()
        stage_ffn(3)
        stage_final()


def kernel(**inputs):
    import numpy as _np
    import concourse.bacc as _bacc
    from concourse import mybir as _mybir
    from concourse.bass_utils import run_bass_kernel_spmd as _run

    nc = _bacc.Bacc("TRN2", target_bir_lowering=False, num_devices=1)
    arrays, d = {}, {}
    for name in inputs:
        a = _np.ascontiguousarray(inputs[name])
        arrays[f"in_{name}_dram"] = a
        d[name] = nc.dram_tensor(f"in_{name}_dram", a.shape, _mybir.dt.from_np(a.dtype), kind="ExternalInput").ap()
    s = {k: v.shape for k, v in d.items()}
    nb, t, dm = s["x_prompt"]
    b, ts, _ = s["x_sample"]
    ne, _, _, nh, dh = s["cache_sb_k"]
    no, _, mh, mp, mn = s["state_ssm"]
    cw1, cch = s["state_conv_a"][2:]
    mw1, mcd = s["state_mamba_conv"][2:]
    shapes = [(nb, t, dm), (b, ts, dm), (ne, nb, t, nh, dh), (ne, nb, t, nh, dh), (ne, nb, cw1, cch),
              (no, nb, mw1, mcd), (no, nb, mh, mp, mn), (ne, b, ts, nh, dh), (ne, b, ts, nh, dh), (ne, b, cw1, cch),
              (no, b, mw1, mcd), (no, b, mh, mp, mn)]
    outs = [nc.dram_tensor(f"out_{i}_dram", sh, _mybir.dt.float32, kind="ExternalOutput").ap()
            for i, sh in enumerate(shapes)]
    bass_trunk(nc, d, outs)
    r = _run(nc, [arrays], core_ids=[0])
    return tuple(r.results[0][f"out_{i}_dram"] for i in range(len(shapes)))
```
